# Optimizing a Trainium2 kernel written in Bass

```python
import math
import jax, jax.numpy as jnp
from jax import lax
import numpy as np

D_MODEL = 2048
BATCH = 1
SEQ = 512
DEPTH = 1

GRID_W = 64
CTX_LEN = 256
HEAD_DIM = 128
RMS_EPS = 1e-6
N_BRANCH = 4
BRANCH_W = 512
NA_HEADS = 4
NA_WIN_R = 8
NA_WIN_C = 16
NA_QBLOCK = 16
NA_KBLOCK = 32
NA_W = NA_HEADS * HEAD_DIM
SSD_HEADS = 8
SSD_HEAD_DIM = 64
SSD_GROUPS = 2
SSD_STATE = 128
SSD_CONV = 5
SSD_CHUNK = 128
SSD_W = SSD_HEADS * SSD_HEAD_DIM
SSD_XBC_W = SSD_W + 2 * SSD_GROUPS * SSD_STATE
SSD_DT_W = 2 * SSD_HEADS
GQA_HEADS = 4
GQA_KV_HEADS = 2
GQA_W = GQA_HEADS * HEAD_DIM
GQA_KV_W = GQA_KV_HEADS * HEAD_DIM
GQA_QBLOCK = 128
ROPE_THETA = 10000.0
FNET_GROUPS = 4
FNET_GROUP_DIM = 128
FNET_W = FNET_GROUPS * FNET_GROUP_DIM
PROJ_SPLITS = (NA_W, NA_W, NA_W, SSD_W, SSD_XBC_W, SSD_DT_W, GQA_W, GQA_KV_W, GQA_KV_W, FNET_W, N_BRANCH * D_MODEL)
PROJ_W = sum(PROJ_SPLITS)
N_EXPERTS = 16
EXPERT_FF = D_MODEL // 2
CAPACITY_FACTOR = 2

kernel_name = 'hybrid_gated_parallel_mixers_ec_moe_dit'

def rms_norm(x, w):
    xf = x.astype(jnp.float32)
    y = xf * lax.rsqrt(jnp.mean(xf * xf, axis=-1, keepdims=True) + RMS_EPS)
    return (y * w.astype(jnp.float32)).astype(x.dtype)

def ada_mod(cvec, w, b):
    m = jax.nn.silu(cvec) @ w + b
    return [t[..., None, :] for t in jnp.split(m, 6, axis=-1)]

def split_proj(p):
    return jnp.split(p, np.cumsum(PROJ_SPLITS)[:-1].tolist(), axis=-1)

def heads(t, nh):
    return t.reshape(t.shape[0], t.shape[1], nh, -1)

def axial_rope_tables(n_tok):
    t = jnp.arange(n_tok)
    pos = jnp.stack([t // GRID_W, t % GRID_W], axis=-1).astype(jnp.float32)
    n_freq = HEAD_DIM // 4
    inv = ROPE_THETA ** (-jnp.arange(n_freq, dtype=jnp.float32) / n_freq)
    ang = pos[:, :, None] * inv
    return jnp.cos(ang), jnp.sin(ang)

def apply_rope(x, cos, sin):
    b, n, h, d = x.shape
    xf = x.astype(jnp.float32).reshape(b, n, h, 2, 2, d // 4)
    re, im = xf[..., 0, :], xf[..., 1, :]
    c, s = cos[None, :, None], sin[None, :, None]
    out = jnp.stack([re * c - im * s, re * s + im * c], axis=-2)
    return out.reshape(b, n, h, d).astype(x.dtype)

def head_rms_rope(raw, nh, gain, rope):
    t = rms_norm(heads(raw, nh), gain)
    return t if rope is None else apply_rope(t, *rope)

def mha(q, k, v):
    b, nq, hq, d = q.shape
    hkv = k.shape[2]
    qg = q.reshape(b, nq, hkv, hq // hkv, d)
    s = jnp.einsum('bqgrd,bkgd->bgrqk', qg, k).astype(jnp.float32) * d ** -0.5
    p = jax.nn.softmax(s, axis=-1).astype(v.dtype)
    return jnp.einsum('bgrqk,bkgd->bqgrd', p, v).reshape(b, nq, hq * d)

def gqa_latent(q, k, v, kc, vc):
    b, n = q.shape[:2]
    k_all = jnp.concatenate([kc, k], axis=1)
    v_all = jnp.concatenate([vc, v], axis=1)
    nb = n // GQA_QBLOCK
    qb = q.reshape(b, nb, GQA_QBLOCK, GQA_HEADS, HEAD_DIM).transpose(1, 0, 2, 3, 4)
    ob = lax.map(lambda qq: mha(qq, k_all, v_all), qb)
    return ob.transpose(1, 0, 2, 3).reshape(b, n, GQA_W)

def _na_indices(rows):
    kr = min(NA_WIN_R, rows)
    ncb = GRID_W // NA_QBLOCK
    r = np.arange(rows)
    row_start = np.clip(r - kr // 2, 0, rows - kr)
    krow = row_start[:, None] + np.arange(kr)
    qcol = np.arange(ncb)[:, None] * NA_QBLOCK + np.arange(NA_QBLOCK)
    kcol_start = np.clip(np.arange(ncb) * NA_QBLOCK - (NA_KBLOCK - NA_QBLOCK) // 2, 0, GRID_W - NA_KBLOCK)
    kcol = kcol_start[:, None] + np.arange(NA_KBLOCK)
    key_idx = (krow[:, None, :, None] * GRID_W + kcol[None, :, None, :]).reshape(-1)
    col_start = np.clip(qcol - NA_WIN_C // 2, 0, GRID_W - NA_WIN_C)
    kc3 = kcol[:, None, :]
    col_ok = (kc3 >= col_start[..., None]) & (kc3 < col_start[..., None] + NA_WIN_C)
    bias_r = krow - r[:, None] + NA_WIN_R - 1
    bias_c = np.clip(kc3 - qcol[:, :, None] + NA_WIN_C - 1, 0, 2 * NA_WIN_C - 2)
    return kr, key_idx, bias_r, bias_c, col_ok

def na_latent(q, k, v, kc, vc, rpb):
    b, n, nh, hd = q.shape
    rows = n // GRID_W
    ncb = GRID_W // NA_QBLOCK
    kr, key_idx, bias_r, bias_c, col_ok = _na_indices(rows)
    nk = kr * NA_KBLOCK
    bias = rpb.astype(jnp.float32)[:, bias_r[:, None, None, :, None], bias_c[None, :, :, None, :]]
    bias = jnp.where(col_ok[None, None, :, :, None, :], bias, -jnp.inf).reshape(nh, rows, ncb, NA_QBLOCK, nk)
    kg = jnp.take(k, key_idx, axis=1).reshape(b, rows, ncb, nk, nh, hd)
    vg = jnp.take(v, key_idx, axis=1).reshape(b, rows, ncb, nk, nh, hd)
    qb = q.reshape(b, rows, ncb, NA_QBLOCK, nh, hd)
    scale = hd ** -0.5
    s_win = jnp.einsum('brjqhd,brjkhd->bhrjqk', qb, kg).astype(jnp.float32) * scale + bias[None]
    s_ctx = jnp.einsum('brjqhd,bchd->bhrjqc', qb, kc).astype(jnp.float32) * scale
    p = jax.nn.softmax(jnp.concatenate([s_win, s_ctx], axis=-1), axis=-1).astype(v.dtype)
    o = jnp.einsum('bhrjqk,brjkhd->brjqhd', p[..., :nk], vg) + jnp.einsum('bhrjqc,bchd->brjqhd', p[..., nk:], vc)
    return o.reshape(b, n, nh * hd)

def dwconv(u, w, bias):
    ch = u.shape[-1]
    out = lax.conv_general_dilated(u, w.astype(u.dtype)[:, None, :], window_strides=(1,),
                                   padding=((SSD_CONV // 2, SSD_CONV // 2),),
                                   dimension_numbers=('NWC', 'WIO', 'NWC'), feature_group_count=ch)
    return out + bias.astype(u.dtype)

def ssd_prepare(xbc, dt_raw, conv_w, conv_b, dt_bias):
    b, n, _ = xbc.shape
    u = jax.nn.silu(dwconv(xbc, conv_w, conv_b))
    xs, bm, cm = jnp.split(u, [SSD_W, SSD_W + SSD_GROUPS * SSD_STATE], axis=-1)
    xs = xs.reshape(b, n, SSD_HEADS, SSD_HEAD_DIM)
    bm = bm.reshape(b, n, SSD_GROUPS, SSD_STATE)
    cm = cm.reshape(b, n, SSD_GROUPS, SSD_STATE)
    dt = jax.nn.softplus(dt_raw.astype(jnp.float32) + dt_bias.reshape(-1).astype(jnp.float32)).reshape(b, n, 2, SSD_HEADS)
    return xs, bm, cm, dt[:, :, 0], dt[:, :, 1]

def ssd_chunked(x, dt, a_log, b_mat, c_mat, h0, with_output):
    bsz, n, nh, hp = x.shape
    g, ns = b_mat.shape[2], b_mat.shape[3]
    e = nh // g
    nc = n // SSD_CHUNK
    f32 = jnp.float32
    a_neg = -jnp.exp(a_log.astype(f32)).reshape(g, e)
    xr = x.astype(f32).reshape(bsz, nc, SSD_CHUNK, g, e, hp)
    dtr = dt.astype(f32).reshape(bsz, nc, SSD_CHUNK, g, e)
    bc = b_mat.astype(f32).reshape(bsz, nc, SSD_CHUNK, g, ns)
    cc = c_mat.astype(f32).reshape(bsz, nc, SSD_CHUNK, g, ns)
    a_cum = jnp.cumsum(dtr * a_neg, axis=2)
    a_tot = a_cum[:, :, -1]
    x_dt = xr * dtr[..., None]
    states = jnp.einsum('bclgn,bclge,bclgep->bcgepn', bc, jnp.exp(a_tot[:, :, None] - a_cum), x_dt)

    def carry_step(h, inp):
        st, at = inp
        return h * jnp.exp(at)[..., None, None] + st, h

    h_fin, h_start = lax.scan(carry_step, h0, (jnp.moveaxis(states, 1, 0), jnp.moveaxis(a_tot, 1, 0)))
    if not with_output:
        return None, h_fin
    h_start = jnp.moveaxis(h_start, 0, 1)
    causal = np.tril(np.ones((SSD_CHUNK, SSD_CHUNK), dtype=bool))
    seg = a_cum[:, :, :, None] - a_cum[:, :, None, :]
    decay = jnp.exp(jnp.where(causal[:, :, None, None], seg, -jnp.inf))
    cb = jnp.einsum('bclgn,bcsgn->bclsg', cc, bc)
    y = (jnp.einsum('bclsg,bclsge,bcsgep->bclgep', cb, decay, x_dt)
         + jnp.einsum('bclgn,bclge,bcgepn->bclgep', cc, jnp.exp(a_cum), h_start))
    return y.reshape(bsz, n, nh, hp), h_fin

def ssd_bidir(prep, a_log, h0_f, h0_b, with_output):
    xs, bm, cm, dt_f, dt_b = prep
    flip = lambda t: jnp.flip(t, axis=1)
    y_f, h_f = ssd_chunked(xs, dt_f, a_log[0], bm, cm, h0_f, with_output)
    y_b, h_b = ssd_chunked(flip(xs), flip(dt_b), a_log[1], flip(bm), flip(cm), h0_b, with_output)
    y = y_f + flip(y_b) if with_output else None
    return y, h_f, h_b

def ssd_output(y, xs, z, d_skip, norm_w):
    b, n = xs.shape[:2]
    y = y + d_skip.astype(jnp.float32)[:, None] * xs.astype(jnp.float32)
    gated = (y * jax.nn.silu(z.astype(jnp.float32)).reshape(b, n, SSD_HEADS, SSD_HEAD_DIM))
    gated = gated.reshape(b, n, SSD_GROUPS, SSD_W // SSD_GROUPS)
    normed = gated * lax.rsqrt(jnp.mean(gated * gated, axis=-1, keepdims=True) + RMS_EPS)
    return (normed.reshape(b, n, SSD_W) * norm_w.astype(jnp.float32)).astype(xs.dtype)

def fourier_mix(u):
    b, n, _ = u.shape
    uf = u.astype(jnp.float32).reshape(b, n, FNET_GROUPS, FNET_GROUP_DIM)
    out = jnp.fft.fft2(uf, axes=(1, 3), norm='ortho').real
    return out.reshape(b, n, FNET_W).astype(u.dtype)

def merge(branches, gates_raw, w_branch, w_out):
    g = jax.nn.sigmoid(gates_raw.astype(jnp.float32)).reshape(gates_raw.shape[0], gates_raw.shape[1], N_BRANCH, D_MODEL)
    y = g[..., 0, :] * (branches[0] @ w_branch[0]).astype(jnp.float32)
    for i in range(1, N_BRANCH):
        y = y + g[..., i, :] * (branches[i] @ w_branch[i]).astype(jnp.float32)
    return y.astype(gates_raw.dtype) @ w_out

def expert_choice(h, w_router, w_gate, w_up, w_down):
    b, n, d = h.shape
    cap = CAPACITY_FACTOR * n // N_EXPERTS
    aff = jax.nn.softmax((h @ w_router).astype(jnp.float32), axis=-1)
    gate, idx = lax.top_k(jnp.swapaxes(aff, 1, 2), cap)
    xs = jax.vmap(lambda hb, ib: hb[ib])(h, idx)
    hid = jax.nn.silu(jnp.einsum('becd,edf->becf', xs, w_gate)) * jnp.einsum('becd,edf->becf', xs, w_up)
    ye = jnp.einsum('becf,efd->becd', hid, w_down) * gate[..., None].astype(h.dtype)
    return jax.vmap(lambda yb, ib: jnp.zeros((n, d), h.dtype).at[ib.reshape(-1)].add(yb.reshape(-1, d).astype(h.dtype)))(ye, idx)

def layer_forward(x, xc, c, c_ctx, w_ada, b_ada, norm_mix, norm_ffn, w_in, na_rpb, conv_w, conv_b, a_log,
                  dt_bias, d_skip, ssd_gn, q_gain, k_gain, w_branch, w_out, w_router, w_gate, w_up, w_down,
                  rope, update_ctx):
    bsz = x.shape[0]
    sh1, sc1, g1, sh2, sc2, g2 = ada_mod(c, w_ada, b_ada)
    csh1, csc1, cg1, csh2, csc2, cg2 = ada_mod(c_ctx, w_ada, b_ada)
    h = rms_norm(x, norm_mix) * (1 + sc1) + sh1
    hc = rms_norm(xc, norm_mix) * (1 + csc1) + csh1
    na_q, na_k, na_v, s_z, s_xbc, s_dt, g_q, g_k, g_v, f_in, gates = split_proj(h @ w_in)
    na_qc, na_kc, na_vc, s_zc, s_xbcc, s_dtc, g_qc, g_kc, g_vc, f_inc, gates_c = split_proj(hc @ w_in)

    kc_na, vc_na = heads(na_kc, NA_HEADS), heads(na_vc, NA_HEADS)
    o_na = na_latent(heads(na_q, NA_HEADS), heads(na_k, NA_HEADS), heads(na_v, NA_HEADS), kc_na, vc_na, na_rpb)

    h0 = jnp.zeros((bsz, SSD_GROUPS, SSD_HEADS // SSD_GROUPS, SSD_HEAD_DIM, SSD_STATE), jnp.float32)
    prep_c = ssd_prepare(s_xbcc, s_dtc, conv_w, conv_b, dt_bias)
    y_c, hf_c, hb_c = ssd_bidir(prep_c, a_log, h0, h0, update_ctx)
    prep = ssd_prepare(s_xbc, s_dt, conv_w, conv_b, dt_bias)
    y, _, _ = ssd_bidir(prep, a_log, hf_c, hb_c, True)
    o_ssd = ssd_output(y, prep[0], s_z, d_skip, ssd_gn)

    kc_g, vc_g = head_rms_rope(g_kc, GQA_KV_HEADS, k_gain, None), heads(g_vc, GQA_KV_HEADS)
    o_gqa = gqa_latent(head_rms_rope(g_q, GQA_HEADS, q_gain, rope), head_rms_rope(g_k, GQA_KV_HEADS, k_gain, rope),
                       heads(g_v, GQA_KV_HEADS), kc_g, vc_g)

    o_fn = fourier_mix(f_in)

    x = x + g1 * merge((o_na, o_ssd, o_gqa, o_fn), gates, w_branch, w_out)
    h2 = rms_norm(x, norm_ffn) * (1 + sc2) + sh2
    x = x + g2 * expert_choice(h2, w_router, w_gate, w_up, w_down)

    if update_ctx:
        o_na_c = mha(heads(na_qc, NA_HEADS), kc_na, vc_na)
        o_ssd_c = ssd_output(y_c, prep_c[0], s_zc, d_skip, ssd_gn)
        o_gqa_c = mha(head_rms_rope(g_qc, GQA_HEADS, q_gain, None), kc_g, vc_g)
        o_fn_c = fourier_mix(f_inc)
        xc = xc + cg1 * merge((o_na_c, o_ssd_c, o_gqa_c, o_fn_c), gates_c, w_branch, w_out)
        hc2 = rms_norm(xc, norm_ffn) * (1 + csc2) + csh2
        xc = xc + cg2 * expert_choice(hc2, w_router, w_gate, w_up, w_down)
    return x, xc

def setup_inputs(seed: int = 0) -> dict:
    key = jax.random.key(seed)
    ks = jax.random.split(key, 26)
    f32 = jnp.float32
    L = DEPTH
    nrm = lambda k, shape, scale: jax.random.normal(k, shape, f32) * scale
    dt0 = jnp.exp(jax.random.uniform(ks[10], (L, 2, SSD_HEADS), f32, math.log(1e-3), math.log(1e-1)))
    return {
        'x': nrm(ks[0], (BATCH, SEQ, D_MODEL), 1.0),
        'c': nrm(ks[1], (BATCH, D_MODEL), 1.0),
        'ctx': nrm(ks[2], (BATCH, CTX_LEN, D_MODEL), 1.0),
        'c_ctx': nrm(ks[3], (D_MODEL,), 1.0),
        'w_ada': nrm(ks[4], (L, D_MODEL, 6 * D_MODEL), 0.5 * D_MODEL ** -0.5),
        'b_ada': nrm(ks[5], (L, 6 * D_MODEL), 0.01),
        'norm_mix': 1.0 + nrm(ks[6], (L, D_MODEL), 0.02),
        'norm_ffn': 1.0 + nrm(ks[7], (L, D_MODEL), 0.02),
        'w_in': nrm(ks[8], (L, D_MODEL, PROJ_W), D_MODEL ** -0.5),
        'na_rpb': nrm(ks[9], (L, NA_HEADS, 2 * NA_WIN_R - 1, 2 * NA_WIN_C - 1), 0.1),
        'ssd_conv_w': nrm(ks[11], (L, SSD_CONV, SSD_XBC_W), SSD_CONV ** -0.5),
        'ssd_conv_b': nrm(ks[12], (L, SSD_XBC_W), 0.01),
        'ssd_a_log': jnp.log(jax.random.uniform(ks[13], (L, 2, SSD_HEADS), f32, 1.0, 16.0)),
        'ssd_dt_bias': dt0 + jnp.log(-jnp.expm1(-dt0)),
        'ssd_d': 1.0 + nrm(ks[14], (L, SSD_HEADS), 0.1),
        'ssd_norm': 1.0 + nrm(ks[15], (L, SSD_W), 0.02),
        'gqa_q_norm': 1.0 + nrm(ks[16], (L, HEAD_DIM), 0.02),
        'gqa_k_norm': 1.0 + nrm(ks[17], (L, HEAD_DIM), 0.02),
        'w_branch': nrm(ks[18], (L, N_BRANCH, BRANCH_W, D_MODEL), BRANCH_W ** -0.5),
        'w_out': nrm(ks[19], (L, D_MODEL, D_MODEL), D_MODEL ** -0.5),
        'w_router': nrm(ks[20], (L, D_MODEL, N_EXPERTS), D_MODEL ** -0.5),
        'moe_w_gate': nrm(ks[21], (L, N_EXPERTS, D_MODEL, EXPERT_FF), D_MODEL ** -0.5),
        'moe_w_up': nrm(ks[22], (L, N_EXPERTS, D_MODEL, EXPERT_FF), D_MODEL ** -0.5),
        'moe_w_down': nrm(ks[23], (L, N_EXPERTS, EXPERT_FF, D_MODEL), EXPERT_FF ** -0.5),
        'final_norm': 1.0 + nrm(ks[24], (D_MODEL,), 0.02),
    }

def reference(x, c, ctx, c_ctx, w_ada, b_ada, norm_mix, norm_ffn, w_in, na_rpb, ssd_conv_w, ssd_conv_b,
              ssd_a_log, ssd_dt_bias, ssd_d, ssd_norm, gqa_q_norm, gqa_k_norm, w_branch, w_out, w_router,
              moe_w_gate, moe_w_up, moe_w_down, final_norm):
    rope = axial_rope_tables(x.shape[1])
    xc = ctx
    for l in range(DEPTH):
        x, xc = layer_forward(x, xc, c, c_ctx, w_ada[l], b_ada[l], norm_mix[l], norm_ffn[l], w_in[l], na_rpb[l],
                              ssd_conv_w[l], ssd_conv_b[l], ssd_a_log[l], ssd_dt_bias[l], ssd_d[l], ssd_norm[l],
                              gqa_q_norm[l], gqa_k_norm[l], w_branch[l], w_out[l], w_router[l], moe_w_gate[l],
                              moe_w_up[l], moe_w_down[l], rope, l < DEPTH - 1)
    return rms_norm(x, final_norm)


_drawn_inputs = setup_inputs


def setup_inputs(seed=0):
    import zlib

    import numpy as np

    out = dict(_drawn_inputs(seed))
    spreads = {}
    factors = {'ctx': 3.488,
     'b_ada': 5.719,
     'norm_mix': 8.0,
     'norm_ffn': 7.908,
     'na_rpb': 8.0,
     'ssd_conv_b': 24.86,
     'ssd_d': 40.176,
     'ssd_norm': 8.0,
     'gqa_q_norm': 8.0,
     'gqa_k_norm': 8.0,
     'final_norm': 8.225}
    for name, (base, spread) in spreads.items():
        noise = np.random.default_rng([zlib.crc32(name.encode()), seed]).standard_normal(out[name].shape)
        drawn = base * np.exp(spread * noise) if base else spread * noise
        out[name] = __import__('jax').numpy.asarray(drawn.astype(out[name].dtype))
    for name, factor in factors.items():
        out[name] = (out[name] * factor).astype(out[name].dtype)
    return out
```

```python
from contextlib import ExitStack

import numpy as np

import concourse.bass as bass
from concourse import mybir

F32 = mybir.dt.float32
F32R = mybir.dt.float32r
ACT = mybir.ActivationFunctionType
ALU = mybir.AluOpType
AX = mybir.AxisListType

P = 128
D = 2048
N = 512
NCTX = 256
NT = N // P
NTA = (N + NCTX) // P
NA_ALL = N + NCTX
KT = D // P
GRID_W = 64
NA_R, NA_C = 8, 16
HEADS = 4
HD = 128
SH = 8
SHD = 64
BW = 512
NB = 4
E = 16
CAP = 2 * N // E
FF = D // 2
EPS = 1e-6
NEG = -1e30
SCALE = HD ** -0.5
SW = 256
SLOTS = 4

C_NAQ, C_NAK, C_NAV, C_Z, C_XBC, C_DT, C_GQ, C_GKV, C_F, C_G = (
    0, 512, 1024, 1536, 2048, 3072, 3088, 3600, 4112, 4624)

K_ID, K_ONE, K_TU, K_TL, K_MF, K_MB, K_NAM, K_IOTA, K_SEL, K_EPS, K_W = (
    0, 128, 256, 384, 512, 640, 768, 832, 896, 928, 936)
Q_NORM, Q_CW, Q_CB, Q_C, Q_BADA, Q_W = 0, 16, 56, 64, 96, 128
R_ALOG, R_DTB, R_DSK, R_SSDN, R_QG, R_KG, R_W = 0, 16, 32, 40, 552, 680, 808


class Steps:

    def __init__(self, engine, sem):
        self.engine, self.sem, self.n = engine, sem, 0

    def done(self, instruction):
        instruction.then_inc(self.sem, 1)
        self.n += 1

    def wait(self):
        self.engine.wait_ge(self.sem, self.n)


def build_layer(nc, a, out):
    with ExitStack() as ctx:
        base = (nc.sbuf_base + 63) // 64 * 64

        def at(name, offset, shape, dtype=F32):
            return nc.alloc_sbuf_tensor_at(name, shape, dtype, offset=base + offset)

        def sem(name):
            return ctx.enter_context(nc.semaphore(name))

        M_RING, M_HT, M_OT, M_YT, M_X, M_K = 0, 65536, 114688, 147456, 180224, 205120
        RING = at("ring", M_RING, [P, SLOTS, KT, SW])
        HT = at("hT", M_HT, [P, KT, N])
        HTC = at("hT_ctx", M_HT + 32768, [P, KT, NCTX])
        OT = at("oT", M_OT, [P, NB, NB, N])
        YT = at("yT", M_YT, [P, KT, N])
        CST = at("cst", M_K, [P, K_W])
        COL = at("colp", M_K + 3744, [P, Q_W])
        ROW = at("rowp", M_K + 4256, [P, R_W])
        CSIL = at("csil", M_K + 7488, [P, KT, 2])
        assert base + M_K + 7488 + 128 <= 229360
        PS = ctx.enter_context(nc.psum_tensor("ps", [P, 8, 512], F32))

        ident = CST[:, K_ID:K_ID + P]
        ones = CST[:, K_ONE:K_ONE + P]
        triu = CST[:, K_TU:K_TU + P]
        tril = CST[:, K_TL:K_TL + P]
        sel = CST[:, K_SEL:K_SEL + 32]
        eps = CST[:, K_EPS:K_EPS + 1]

        XT = at("x_tiles", M_YT, [P, 2, D])
        JUNK0 = at("junk0", M_YT + 16384, [P, D])
        CSILP = at("csil_pad", M_YT + 24576, [P, KT, 32])
        ADAROW = at("ada_row", M_OT, [P, 2 * D])
        WDT = at("w_dt", M_X + 16384, [P, KT, 32])
        SM0 = at("small0", M_X + 20480, [P, 256])
        ss0, rs0 = SM0[:, 0:NTA], SM0[:, 8:8 + NTA]
        MOD = SM0[:, 16:80].rearrange("p (v k l) -> p v k l", v=2, l=2)
        MODA = SM0[:, 80:112].rearrange("p (k l) -> p k l", l=2)

        S0 = M_OT + 16384
        XB = at("xb", S0, [P, 2, 776])
        UL = at("u_lat", S0 + 6208, [P, 8, N])
        UC = at("u_ctx", S0 + 22592, [P, 6, NCTX])
        XTOK = at("x_tok", S0 + 28736, [P, NTA, 512])
        BTOK = at("b_tok", S0 + 41024, [P, NTA, 256])
        HF = at("h_f", S0 + 47168, [P, NT, 512])
        HB = at("h_b", S0 + 55360, [P, NT, 512])
        SM = at("small_ssd", S0, [P, 12, NTA * 16])
        LSEG = at("l_seg", S0 + 63552, [P, 16, P])
        SPILL = at("spill_stage", S0 + 71744, [P, 512])
        assert S0 + 71744 + 2048 <= M_X + 24928
        DTT = at("dt_t", S0 + 63552, [P, NA_ALL])
        DATRI = at("da_tri", S0 + 6208, [P, 16, P])
        TMP = at("tmp_ssd", S0 + 22592, [P, 3, 512])
        Z = at("z", M_OT, [P, NT, 512])
        SMY = at("small_y", S0 + 6208 - 256, [P, 16])
        dtv, dts, da, ncum, tcum, ecum, etot, wx = (
            SM[:, i, :].rearrange("p (t j) -> p t j", j=16) for i in range(8))
        ex, m0, lnu, ded = (SM[:, i, :].rearrange("p (t j) -> p t j", j=16) for i in range(8, 12))
        aneg = SMY

        FT = at("f_t", M_OT + 24576, [P, 4, N])
        XCS = at("xcs", M_YT + 12288, [P, NT, 4, 256])
        DFTN = at("dft_n", M_YT + 28672, [P, NT, 2, N])
        DFTC = at("dft_c", M_YT + 45056, [P, 256])

        GQR = at("gq_raw", M_OT, [P, NT, 512])
        GKV = at("gkv_raw", M_YT, [P, NTA, 512])
        GQT = at("gq_t", M_YT + 12288, [P, HEADS, N])
        GKT = at("gk_t", M_YT + 20480, [P, 2, NA_ALL])
        SQ = at("gsq", M_OT + 16384, [P, NT, 512])
        SQK = at("gsqk", M_YT + 46080, [P, NTA, 256])
        RTQ = at("rot_q", M_YT + 46080, [P, 4, 256])
        RTK = at("rot_k", M_YT + 50176, [P, 4, 128])
        ROPE = at("rope", M_YT + 52224, [P, NT, 2, 64])
        SMG = at("small_g", M_YT + 54272, [P, 64])
        ATTG = (at("pg", M_YT + 26624, [P, 3, NA_ALL]), at("ptg", M_YT + 35840, [P, NTA, N]), at("sg", M_YT + 49408, [P, 4, 16]))
        NQT = at("nq_t", M_YT, [P, HEADS, N])
        NKT = at("nk_t", M_YT + 8192, [P, HEADS, NA_ALL])
        NV = at("n_v", M_YT + 20480, [P, NTA, 512])
        ATTN = (at("pn", M_YT + 32768, [P, 3, NA_ALL]), at("ptn", M_HT + 32768, [P, NTA, N]), at("sn", M_YT + 49664, [P, 4, 16]))
        NBIAS = at("n_bias", M_YT + 41984, [P, 2, 15, GRID_W])

        RAW = at("w_raw", M_RING, [P, 2, KT, P])
        WLO = at("w_lo", M_RING + 16384, [P, 2, KT, P], F32R)
        WHI = at("w_hi", M_RING + 32768, [P, 2, KT, P], F32R)
        WADA = at("w_ada_sb", M_RING + 49152, [P, KT, P])
        HLO = at("h_lo", M_HT, [P, KT, N], F32R)
        hi_parts = [at("h_hi0", M_HT + 32768, [P, 8, N], F32R), at("h_hi1", M_RING + 57344, [P, 4, N], F32R),
                    at("h_hi2", M_X + 16384, [P, 4, N], F32R)]
        HHI = [hi_parts[0][:, k, :] for k in range(8)] + [hi_parts[1 + k // 4][:, k % 4, :] for k in range(8)]
        WB = at("w_branch_sb", M_X, [P, 2, NB, P])
        SG = at("gate", M_X + 4096, [P, 2, N])
        GP = at("gated", M_X + 8192, [P, 2, N])
        ADACC = at("ada_acc", M_X + 12288, [P, 2, P])
        STAGE = at("ada_stage", M_X + 13312, [P, 2, P])
        BROW = at("b_ada_row", M_X + 14336, [P, 2, P])
        XN = at("x_new", M_HT, [P, NT, D])
        SC2 = at("scale2", M_HT + 32768, [P, D])
        SH2 = at("shift2", M_HT + 40960, [P, D])
        H2 = at("h2", M_OT, [P, NT, D])
        G1R = at("gate1_row", M_X, [P, D])
        WR = at("w_router_sb", M_X + 8192, [P, KT, 32])
        SM3 = at("small3", M_X + 10240, [P, 512])
        T3 = at("t3", M_X + 12288, [P, 2, 512])
        ORAW = at("wo_raw", M_RING, [P, 2, 8, 512])
        OLO = at("wo_lo", M_RING, [P, 2, 8, 512], F32R)
        OHI = at("wo_hi", M_RING + 32768, [P, 2, 8, 512], F32R)
        YHI = at("y_hi", M_OT, [P, KT, N], F32R)
        YLO = at("y_lo", M_YT, [P, KT, N], F32R)
        NF = at("norm_ffn_row", M_X + 16384, [P, D])
        JUNK3 = at("junk3", M_X + 16384, [P, D])
        H2T = at("h2_t", M_YT, [P, KT, N])
        AT = at("aff_t", M_HT + 32768, [E, 5, N])
        M8 = at("top8", M_HT + 32768 + 10240, [E, 8, 8])
        AFF = at("aff", M_X + 22528, [P, NT, E])
        POS = at("pos", M_X + 22784, [P, NT, E])
        RING4 = at("ring4", M_YT, [P, 2, KT, SW])
        XS = at("xs", M_HT + 32768, [P, D])
        XST = at("xs_t", M_HT + 40960, [P, KT, P])
        G2R = at("gate2_row", M_X, [P, D])
        HID = at("hid", M_X + 8192, [P, FF])
        HIDT = at("hid_t", M_X + 12288, [P, FF // P, P])
        PSEL = at("p_sel", M_X + 16384, [P, NT, P])
        PG = at("p_gate", M_X + 18432, [P, NT, P])
        PGT = at("p_gate_t", M_X + 20480, [P, N])
        FN = at("final_norm_row", M_HT + 40960, [P, D])
        SM5 = at("small5", M_X + 23040, [P, 16])

        w_ada = a["w_ada"].rearrange("(p k) n -> p k n", k=KT)
        w_in = a["w_in"].rearrange("(p k) n -> p k n", k=KT)
        stream = [w_ada[:, :, n * SW:(n + 1) * SW] for n in range(2 * D // SW)]
        ADA1 = len(stream)
        chunks = [
            ("xbc", C_XBC, "T"), ("xbc2", C_XBC + 512, "T"), ("z", C_Z, "R"), ("f", C_F, "T"), ("gq", C_GQ, "R"),
            ("gkv", C_GKV, "R"), ("naq", C_NAQ, "T"), ("nak", C_NAK, "T"), ("nav", C_NAV, "R")]
        groups = []
        for name, c0, mode in chunks:
            load = len(stream)
            stream += [w_in[:, :, c0:c0 + SW], w_in[:, :, c0 + SW:c0 + 2 * SW]]
            if mode == "T":
                for b in range(4):
                    has_ctx = {"xbc": True, "xbc2": b < 2, "nak": True}.get(name, False)
                    for part in (0, 1) if has_ctx else (0,):
                        groups.append(dict(name=name, mode="T", load=load + b // 2, col=(b % 2) * P, b=b, ctx=part))
            else:
                for t in range(NTA if name in ("gkv", "nav") else NT):
                    groups.append(dict(name=name, mode="R", load=load, t=t))
        for g, gr in enumerate(groups):
            gr["n"] = g
        ada_read, proj_done = sem("ada_read"), sem("proj_done")
        freed = [(ada_read, n + 1) for n in range(ADA1)]
        for load in range(ADA1, len(stream)):
            users = [g["n"] + 1 for g in groups if g["load"] == load or (g["mode"] == "R" and g["load"] == load - 1)]
            freed.append((proj_done, max(users)))
        filled = [sem(f"ring_filled{s}") for s in range(SLOTS)]

        def slot_filled(eng, load):
            eng.wait_ge(filled[load % SLOTS], 16 * (load // SLOTS + 1))

        cst_in, x_in, dtw_zero = sem("cst_in"), [sem("x_in0"), sem("x_in1")], sem("dtw_zero")
        rms_ss, rms_sd, rms_rs, turned, turned_act, turned_dve = (
            sem(n) for n in ("rms_ss", "rms_sd", "rms_rs", "turned", "turned_act", "turned_dve"))
        NORM3, NORM5 = NTA, NTA + NT
        small_in = sem("small_in")
        SMALL_DTW, SMALL_TABLES, SMALL_WR, SMALL_G2 = 16, 48, 64, 80
        pads_zero, csil_set, csilp_set = sem("pads_zero"), sem("csil_set"), sem("csilp_set")
        xn_set = sem("xn_set")
        ada_evac, ada_col, mod_set, mod_lat, mod_ctx = (
            sem("ada_evac"), sem("ada_col"), sem("mod_set"), sem("mod_lat"), sem("mod_ctx"))
        arrive = sem("arrive")
        evac = [sem("evac0"), sem("evac1")]
        conv_tap, conv_done, u_set = sem("conv_tap"), sem("conv_done"), sem("u_set")
        tok_T, tok_x, tok_b = sem("tok_T"), sem("tok_x"), sem("tok_b")
        dt_ps, dt_t, dt_tok, dt_v, dt_act, dt_dve = (
            sem("dt_ps"), sem("dt_t"), sem("dt_tok"), sem("dt_v"), sem("dt_act"), sem("dt_dve"))
        cum_ps, cum_dve, cum_exp, wx_set = sem("cum_ps"), sem("cum_dve"), sem("cum_exp"), sem("wx_set")
        xw_set, st_ps, st_dve = sem("xw_set"), sem("st_ps"), sem("st_dve")
        datri_set, seg_ps, seg_dve, seg_exp, lf_set, m_dve, y_ps, y_dve, y_act, yT_ps, yT_set = (
            sem(n) for n in ("datri_set", "seg_ps", "seg_dve", "seg_exp", "lf_set", "m_dve", "y_ps", "y_dve",
                             "y_act", "yT_ps", "yT_set"))
        fc_ps, fc_set, fn_ps, fn_set = (sem(n) for n in ("fc_ps", "fc_set", "fn_ps", "fn_set"))
        spill_out, f_in, gq_in, gkv_in = (sem(n) for n in ("spill_out", "f_in", "gq_in", "gkv_in"))
        dftn_in = sem("dftn_in")
        g_dve, g_pool, g_sqk, g_ms, g_sd, g_rs, g_T, g_Tset = (
            sem(n) for n in ("g_dve", "g_pool", "g_sqk", "g_ms", "g_sd", "g_rs", "g_T", "g_Tset"))

        wb_in, brow_in, stage_out = [sem("wb_in0"), sem("wb_in1")], [sem("brow0"), sem("brow1")], [sem("st0"), sem("st1")]
        raw_in, ada_in = [sem("raw_in0"), sem("raw_in1")], sem("ada_in")
        gate_ps, gate_set, br_ps, gated, yt_add, ada_tap, ada_ps, stage_set, yt_zero, w_hi, w_lo, hh_hi, hh_lo = (
            sem(n) for n in ("gate_ps", "gate_set", "br_ps", "gated", "yt_add", "ada_tap", "ada_ps",
                             "stage_set", "yt_zero", "w_hi", "w_lo", "hh_hi", "hh_lo"))
        wo_hi, wo_lo, wo_read, y_hi, y_lo = (
            sem("wo_hi"), sem("wo_lo"), sem("wo_read"), sem("y_hi"), sem("y_lo"))
        rows_in, out_ps, out_t, xn_add, sc2_set = (
            sem(n) for n in ("rows_in", "out_ps", "out_t", "xn_add", "sc2_set"))
        h_mul, h_set = sem("h_mul"), sem("h_set")
        wr_zero, r_part, r_copy, r_log, r_dve, r_exp, aT_ps, topk, posT_ps, pos_set = (
            sem(n) for n in ("wr_zero", "r_part", "r_copy", "r_log", "r_dve", "r_exp", "aT_ps", "topk", "posT_ps",
                             "pos_set"))
        moe_read, psel_set, pg_set, xs_ps, xs_act, xs_dve, xst_ps, xst_act, xst_dve = (
            sem(n) for n in ("moe_read", "psel_set", "pg_set", "xs_ps", "xs_act", "xs_dve", "xst_ps", "xst_act", "xst_dve"))
        silu_set, hid_set, hidT_ps, hidT_act, hidT_dve, pgt_ps, pgt_set, ye_set, sc_ps, acc_set = (
            sem(n) for n in ("silu_set", "hid_set", "hidT_ps", "hidT_act", "hidT_dve", "pgt_ps", "pgt_set", "ye_set",
                             "sc_ps", "acc_set"))
        o_set, o_out = sem("o_set"), sem("o_out")
        spilled = [g for g in groups if g["name"] in ("f", "gq", "gkv")]
        spill_dram = nc.dram_tensor("spill", [len(spilled), P, 512], F32).ap()
        ada_dram = nc.dram_tensor("ada_rest", [4 * D], F32).ap()

        before4 = [len([n for n in range(len(stream)) if n % SLOTS == s]) for s in range(SLOTS)] + [0, 0]
        filled += [sem("ring_filled4"), sem("ring_filled5")]
        ring6 = [RING[:, s, :, :] for s in range(SLOTS)] + [RING4[:, s, :, :] for s in range(2)]
        RD = 6
        NL = 24
        w_out_v = a["w_out"].rearrange("(k p) n -> p k n", p=P)

        att_scores, att_raw, att_mx, att_exp, att_stat, att_pn, att_pT, att_pT_dve, att_pT_act, att_pv, att_out = (
            sem(n) for n in ("att_scores", "att_raw", "att_mx", "att_exp", "att_stat", "att_pn", "att_pT", "att_pT_dve",
                             "att_pT_act", "att_pv", "att_out"))
        bias_in, bias_set = sem("bias_in"), sem("bias_set")

        class Attention:

            def __init__(s, q, k, v, kv_of, work, bias, o, before):
                s.q, s.k, s.v, s.kv_of, s.bias, s.o = q, k, v, kv_of, bias, o
                s.p, s.pt, s.st = work
                s.u, s.h = before * HEADS * NT, before * HEADS

        gqa = Attention(GQT, GKT, GKV, lambda h: h // 2, ATTG, None, 2, 0)
        na = Attention(NQT, NKT, NV, lambda h: h, ATTN, NBIAS, 0, 1)

        def v_block(at_, kt, h):
            kv = at_.kv_of(h)
            return GKV[:, kt, 256 + kv * HD:256 + (kv + 1) * HD] if at_ is gqa else NV[:, kt, kv * HD:(kv + 1) * HD]

        rounds = {"n": {}}

        def meet(eng, who):
            k = rounds["n"][who] = rounds["n"].get(who, 0) + 1
            eng.drain().then_inc(arrive, 1)
            eng.wait_ge(arrive, 4 * k)

        def token_cols(k, t):
            src, o = (HT, t * P) if t < NT else (HTC, (t - NT) * P)
            return src[:, k:min(k + 4, KT), o:o + P]

        proj_of = lambda *names: [g for g in groups if g["name"] in names]

        block = ctx.enter_context(nc.Block())

        @block.sync
        def _(sp):
            sp.dma_start(CST[:, :], a["cst"]).then_inc(cst_in, 16)
            sp.dma_start(COL[:, :], a["colp"]).then_inc(cst_in, 16)
            sp.dma_start(ROW[:, :], a["rowp"].partition_broadcast(P)).then_inc(cst_in, 16)
            for load, src in enumerate(stream):
                if load == proj_of("nav")[0]["load"]:
                    sp.wait_ge(spill_out, 16 * len(spilled))
                    sp.wait_ge(arrive, 4)
                    back = lambda n0, n1: spill_dram[n0:n1].rearrange("g p n -> p g n")
                    sp.dma_start(FT[:, :, :], back(0, 4)).then_inc(f_in, 16)
                    sp.dma_start(GQR[:, :, :], back(4, 8)).then_inc(gq_in, 16)
                    sp.dma_start(GKV[:, :, :], back(8, 14)).then_inc(gkv_in, 16)
                if load >= SLOTS:
                    sp.wait_ge(*freed[load - SLOTS])
                sp.dma_start(RING[:, load % SLOTS, :, :], src).then_inc(filled[load % SLOTS], 16)
            sp.wait_ge(proj_done, len(groups))
            sp.sem_inc(w_lo, 2)
            wbr = a["w_branch"].rearrange("i (k p) n -> p i k n", p=P)
            badr = a["b_ada"].rearrange("(a n) -> a n", a=1)
            with sp.Fori(0, NB) as i:
                with sp.Fori(0, 8) as q:
                    for k in range(2):
                        n = 16 * i + 2 * q + k
                        sp.wait_ge(w_lo, n + 1)
                        sp.dma_start(RAW[:, k, :, :], w_in[:, :, bass.ds(n * P + C_G, P)]).then_inc(raw_in[k], 16)
                        sp.wait_ge(br_ps, n + 1)
                        sp.dma_start(WB[:, k, :, :], wbr[:, bass.ds(i, 1), :, bass.ds((2 * q + k) * P, P)].rearrange(
                            "p i k n -> p (i k) n")).then_inc(wb_in[k], 16)
                        sp.wait_ge(ada_tap, 16 * n + 16)
                        sp.dma_start(WADA[:, :, :], w_ada[:, :, bass.ds(n * P + 2 * D, P)]).then_inc(ada_in, 16)
                        sp.wait_ge(ada_ps, n + 1)
                        sp.dma_start(BROW[0:1, k, :], badr[:, bass.ds(n * P + 2 * D, P)]).then_inc(brow_in[k], 16)
            sp.wait_ge(ada_tap, 16 + 16 * 64)
            sp.wait_ge(arrive, 4 * 6)
            for n in range(8):
                c, half = divmod(n, 2)
                if n >= 2:
                    sp.wait_ge(wo_read, n - 1)
                sp.dma_start(ORAW[:, n % 2, :, :], w_out_v[:, 8 * half:8 * half + 8, c * 512:(c + 1) * 512]).then_inc(raw_in[n % 2], 16)
                if n == 1:
                    sp.dma_start(XN[:, :, :], a["x"].rearrange("(t p) d -> p t d", p=P)).then_inc(rows_in, 16)
                    for k in range(2):
                        sp.wait_ge(stage_out[k], 16 * 33)
                    row = lambda r: ada_dram[r * D:(r + 1) * D].partition_broadcast(P)
                    sp.dma_start(G1R[:, :], row(0)).then_inc(rows_in, 16)
                    sp.dma_start(SH2[:, :], row(1)).then_inc(rows_in, 16)
                    sp.dma_start(SC2[:, :], row(2)).then_inc(rows_in, 16)
                    sp.dma_start(NF[:, :], a["norm_ffn"].partition_broadcast(P)).then_inc(rows_in, 16)
            sp.wait_ge(out_ps, 16)
            sp.sem_inc(moe_read, SLOTS)
            wg, wu = (a[n].rearrange("e (p k) n -> p e k n", k=KT) for n in ("w_gate", "w_up"))
            wd = a["w_down"].rearrange("e (p f) n -> p e f n", f=FF // P)
            with sp.Fori(0, E // 2) as m:
                for l in range(NL):
                    pos = l % RD
                    dst = ring6[pos].rearrange("p a b -> p (a b)")
                    if l < 16:
                        g = l % 8
                        src = (wg, wu)[l // 8][:, bass.ds(2 * m, 2), 2 * g:2 * g + 2, :]
                        dst = dst.rearrange("p (e k n) -> p e k n", e=2, k=2)
                    else:
                        src = wd[:, bass.ds(2 * m, 2), l - 16, :]
                        dst = dst.rearrange("p (e n) -> p e n", e=2)
                    sp.wait_ge(moe_read, NL * m + l + 1)
                    sp.dma_start(dst, src).then_inc(filled[pos], 16)
            sp.wait_ge(moe_read, RD + NL * (E // 2 - 1) + 16)
            sp.dma_start(FN[:, :], a["final_norm"].partition_broadcast(P)).then_inc(cst_in, 16)
            for t in range(NT):
                sp.wait_ge(o_set, t + 1)
                sp.dma_start(out[t * P:(t + 1) * P, :], XN[:, t, :]).then_inc(o_out, 16)
            sp.wait_ge(o_out, 16 * NT)

        @block.tensor
        def _(pe):
            pe.wait_ge(cst_in, 48)
            for t in range(NTA):
                pe.wait_ge(xn_set, t + 1)
                if t:
                    pe.wait_ge(turned_act, 2 * t)
                    pe.wait_ge(turned_dve, 2 * t)
                for k in range(KT):
                    mm = pe.transpose(PS[:, k // 4, (k % 4) * P:(k % 4 + 1) * P], XT[:, t % 2, k::KT], ident)
                mm.then_inc(turned, 1)
            pe.wait_ge(csilp_set, 1)
            for n in range(ADA1):
                slot_filled(pe, n)
                if n >= 2:
                    pe.wait_ge(ada_evac, n - 1)
                for k in range(KT):
                    j = k % 4
                    mm = pe.matmul(PS[32 * j:32 * j + 32, 4 + n % 2, 0:SW], CSILP[:, k, :], RING[:, n % SLOTS, k, :],
                                   start=k < 4, stop=k >= KT - 4)
                mm.then_inc(ada_read, 1)
            for v in range(2):
                pe.wait_ge(ada_evac, ADA1 // 2 * (v + 1))
                for k in range(KT):
                    c = 2 * k
                    mm = pe.matmul(PS[:, 6 + v, c:c + 2], ADAROW[:, v * D + k:(v + 1) * D:KT], sel[:, 0:2],
                                   start=True, stop=True)
                mm.then_inc(ada_col, 1)

            def project(gs):
                for gr in gs:
                    g = gr["n"]
                    slot_filled(pe, gr["load"])
                    if gr["mode"] == "R":
                        slot_filled(pe, gr["load"] + 1)
                    if g >= 2:
                        pe.wait_ge(evac[g % 2], g // 2)
                    s = gr["load"] % SLOTS
                    for k in range(KT):
                        if g == 0:
                            pe.wait_ge(mod_lat, k + 1)
                        if g == 1:
                            pe.wait_ge(mod_ctx, k + 1)
                        if gr["mode"] == "T":
                            w = RING[:, s, k, gr["col"]:gr["col"] + P]
                            x = HTC[:, k, :] if gr["ctx"] else HT[:, k, :]
                            o = PS[:, g % 2, 0:NCTX] if gr["ctx"] else PS[:, g % 2, :]
                            mm = pe.matmul(o, w, x, start=k == 0, stop=k == KT - 1)
                        else:
                            o = PS[:, g % 2, :].rearrange("p (a b) -> p a b", a=2)
                            mm = pe.matmul(o, token_cols(k, gr["t"])[:, 0, :], RING[:, s:s + 2, k, :],
                                           start=k == 0, stop=k == KT - 1)
                    mm.then_inc(proj_done, 1)

            project(proj_of("xbc", "xbc2"))
            pe.wait_ge(small_in, SMALL_DTW)
            for part, (x, n) in enumerate(((HT, N), (HTC, NCTX))):
                for k in range(KT):
                    j = k % 4
                    mm = pe.matmul(PS[32 * j:32 * j + 32, 2 + part, 0:n], WDT[:, k, :], x[:, k, :],
                                   start=k < 4, stop=k >= KT - 4)
            mm.then_inc(dt_ps, 1)
            project(proj_of("z"))
            pe.wait_ge(dt_t, 2)
            for t in range(NTA):
                mm = pe.matmul(PS[:, 4, 16 * t:16 * t + 16], DTT[:, t * P:(t + 1) * P], sel[:, 0:16], start=True, stop=True)
            mm.then_inc(dt_tok, 1)
            pe.wait_ge(u_set, 14)
            for t in range(NTA):
                if t >= 2:
                    pe.wait_ge(tok_x, t - 1)
                    pe.wait_ge(tok_b, t - 1)
                src, o = (UL, t * P) if t < NT else (UC, (t - NT) * P)
                for b in range(4):
                    pe.transpose(PS[:, 2 + t % 2, b * P:(b + 1) * P], src[:, b, o:o + P], ident)
                for b in range(2):
                    mm = pe.transpose(PS[:, 6 + t % 2, b * P:(b + 1) * P], src[:, 4 + b, o:o + P], ident)
                mm.then_inc(tok_T, 1)
            project(spilled[0:1])
            pe.wait_ge(dt_dve, 7)
            pe.matmul(PS[:, 5, 0:48], triu, da[:, :, 0:8], start=True, stop=True)
            pe.matmul(PS[:, 5, 48:96], tril, da[:, :, 8:16], start=True, stop=True)
            pe.matmul(PS[:, 5, 96:192], ones, da[:, :, :], start=True, stop=True).then_inc(cum_ps, 1)
            project(spilled[1:2])
            steps = [(i, d, t) for i, ft in enumerate(zip((4, 5, 0, 1, 2), (5, 4, 3, 2, 1))) for d, t in enumerate(ft)]
            pe.wait_ge(tok_x, NTA)
            pe.wait_ge(tok_b, NTA)
            for n, (i, d, t) in enumerate(steps):
                pe.wait_ge(xw_set, n + 1)
                if i:
                    pe.wait_ge(st_dve, 2 * n - 4 if i > 1 else n - 1)
                for g in range(2):
                    mm = pe.matmul(PS[:, 2 + d, g * 256:(g + 1) * 256], BTOK[:, t, g * P:(g + 1) * P],
                                   TMP[:, d, g * 256:(g + 1) * 256], start=True, stop=True)
                mm.then_inc(st_ps, 1)
                if n % 2 and n < 8:
                    project(spilled[2 + n // 2:3 + n // 2])
            for t in range(NT):
                pe.wait_ge(datri_set, 2 * t + 2)
                if t:
                    pe.wait_ge(y_dve, 11 * t)
                    pe.wait_ge(yT_set, t)
                else:
                    pe.wait_ge(st_dve, 18)
                for j in range(4):
                    pe.matmul(PS[:, 2 + j, :], ones, DATRI[:, 4 * j:4 * j + 4, :], start=True, stop=True)
                for g in range(2):
                    mm = pe.matmul(PS[:, 7, g * P:(g + 1) * P], UL[:, 4 + g, t * P:(t + 1) * P],
                                   UL[:, 6 + g, t * P:(t + 1) * P], start=True, stop=True)
                mm.then_inc(seg_ps, 1)
                project(spilled[6 + 2 * t:7 + 2 * t])
                pe.wait_ge(seg_dve, 16 * t + 8)
                for d, h in enumerate((HF, HB)):
                    for g in range(2):
                        pe.matmul(PS[:, 2 + d, g * 256:(g + 1) * 256], UL[:, 6 + g, t * P:(t + 1) * P],
                                  h[:, t, g * 256:(g + 1) * 256], start=True, stop=True)
                pe.wait_ge(m_dve, 3 * t + 3)
                for h in range(SH):
                    mm = pe.matmul(PS[:, 6, h * SHD:(h + 1) * SHD], LSEG[:, h, :], XTOK[:, t, h * SHD:(h + 1) * SHD],
                                   start=True, stop=True)
                mm.then_inc(y_ps, 1)
                project(spilled[7 + 2 * t:8 + 2 * t])
                pe.wait_ge(y_dve, 11 * t + 11)
                for b in range(4):
                    mm = pe.transpose(PS[:, 7, b * P:(b + 1) * P], TMP[:, 0, b * P:(b + 1) * P], ident)
                mm.then_inc(yT_ps, 1)
            meet(pe, "pe")

            pe.wait_ge(f_in, 16)
            pe.wait_ge(small_in, SMALL_TABLES)
            for g in range(4):
                for t in range(NT):
                    n = g * NT + t
                    if n >= 2:
                        pe.wait_ge(fc_set, n - 1)
                    pe.matmul(PS[:, 2 + n % 2, 0:256], FT[:, g, t * P:(t + 1) * P], DFTC[:, :],
                              start=True, stop=True).then_inc(fc_ps, 1)
            pe.wait_ge(dftn_in, 16)
            for g in range(4):
                pe.wait_ge(fc_set, NT * (g + 1))
                if g >= 2:
                    pe.wait_ge(fn_set, g - 1)
                for t in range(NT):
                    for c in range(2):
                        mm = pe.matmul(PS[:, 4 + g % 2, :], XCS[:, t, g, c * P:(c + 1) * P], DFTN[:, t, c, :],
                                       start=t + c == 0, stop=t + c == NT)
                mm.then_inc(fn_ps, 1)

            def attend(s):
                units = [(h, t) for h in range(HEADS) for t in range(NT)]

                def values(h):
                    pe.wait_ge(att_pT_dve, s.u + NT * (h + 1))
                    pe.wait_ge(att_pT_act, s.u + NT * (h + 1))
                    if h:
                        pe.wait_ge(att_out, s.h + h)
                    for k in range(NTA):
                        mm = pe.matmul(PS[:, 6, :], v_block(s, k, h), s.pt[:, k, :], start=k == 0, stop=k == NTA - 1)
                    mm.then_inc(att_pv, 1)

                for n in range(len(units) + 2):
                    if n < len(units):
                        h, t = units[n]
                        b = 2 * (n % 2)
                        if n >= 2:
                            pe.wait_ge(att_exp, s.u + n - 1)
                        q = s.q[:, h, t * P:(t + 1) * P]
                        pe.matmul(PS[:, b, :], q, s.k[:, s.kv_of(h), 0:N], start=True, stop=True)
                        pe.matmul(PS[:, b + 1, 0:NCTX], q, s.k[:, s.kv_of(h), N:], start=True,
                                  stop=True).then_inc(att_scores, 1)
                    if n >= 2:
                        m = n - 2
                        h, t = units[m]
                        if t == 0 and h:
                            values(h - 1)
                        pe.wait_ge(att_pn, s.u + m + 1)
                        if m:
                            pe.wait_ge(att_pT_dve, s.u + m)
                            pe.wait_ge(att_pT_act, s.u + m)
                        for k in range(NTA):
                            mm = pe.transpose(PS[:, 4 + k // 4, (k % 4) * P:(k % 4 + 1) * P],
                                              s.p[:, m % 3, k * P:(k + 1) * P], ident)
                        mm.then_inc(att_pT, 1)
                values(HEADS - 1)

            pe.wait_ge(g_dve, 3 + 6 * NT)
            for h in range(HEADS):
                if h:
                    pe.wait_ge(g_Tset, h)
                for t in range(NT):
                    mm = pe.transpose(PS[:, 2, t * P:(t + 1) * P], GQR[:, t, h * HD:(h + 1) * HD], ident)
                mm.then_inc(g_T, 1)
            pe.wait_ge(g_pool, 3 + 6 * NT)
            pe.wait_ge(fn_set, 4)
            for g in range(2):
                pe.wait_ge(g_Tset, HEADS + g)
                for t in range(NTA):
                    mm = pe.transpose(PS[:, 4 + t // 4, (t % 4) * P:(t % 4 + 1) * P], GKV[:, t, g * HD:(g + 1) * HD], ident)
                mm.then_inc(g_T, 1)
            pe.wait_ge(g_Tset, HEADS + 2)
            meet(pe, "pe")
            attend(gqa)
            meet(pe, "pe")
            project(proj_of("naq", "nak", "nav"))
            meet(pe, "pe")
            attend(na)
            meet(pe, "pe")
            pe.sem_inc(ada_ps, 2)
            pe.sem_inc(br_ps, 2)
            pe.wait_ge(hh_lo, KT)
            with pe.Fori(0, NB) as i:
                with pe.Fori(0, 8) as q:
                    for k in range(2):
                        n = 16 * i + 2 * q + k
                        pe.wait_ge(w_lo, n + 1 + 2)
                        pe.wait_ge(gate_set, n + 1)
                        for c in range(KT):
                            pe.matmul(PS[:, k, :], WHI[:, k, c, :], HHI[c], start=c == 0, stop=False)
                            pe.matmul(PS[:, k, :], WHI[:, k, c, :], HLO[:, c, :], start=False, stop=False)
                            mm = pe.matmul(PS[:, k, :], WLO[:, k, c, :], HHI[c], start=False, stop=c == KT - 1)
                        mm.then_inc(gate_ps, 1)
                        pe.wait_ge(wb_in[k], (8 * i + q) * 16 + 16)
                        pe.wait_ge(gated, n + 1)
                        for c in range(NB):
                            mm = pe.matmul(PS[:, 2 + k, :], WB[:, k, c, :],
                                           OT[:, bass.ds(i, 1), c, :].rearrange("p i n -> p (i n)"),
                                           start=c == 0, stop=c == NB - 1)
                        mm.then_inc(br_ps, 1)
                        pe.wait_ge(ada_tap, 16 * n + 16 + 16)
                        pe.wait_ge(brow_in[k], (8 * i + q) * 16 + 16)
                        pe.wait_ge(stage_set, n + 1)
                        pe.matmul(PS[:, 4 + k, 0:P], ones, ADACC[:, k, :], start=True, stop=False)
                        pe.matmul(PS[:, 4 + k, 0:P], CST[0:1, K_ONE:K_ONE + P], BROW[0:1, k, :], start=False,
                                  stop=True).then_inc(ada_ps, 1)
            meet(pe, "pe")
            pe.wait_ge(y_lo, 4)
            for n in range(8):
                c, half = divmod(n, 2)
                pe.wait_ge(wo_lo, 2 * n + 2)
                for t in range(NT):
                    if half == 0 and c >= 2:
                        pe.wait_ge(out_t, 4 * (c - 2) + t + 1)
                    o = PS[:, 4 * (c % 2) + t, :]
                    for k in range(8):
                        kk = 8 * half + k
                        hi, lo = YHI[:, kk, t * P:(t + 1) * P], YLO[:, kk, t * P:(t + 1) * P]
                        first, last = half == 0 and k == 0, half == 1 and k == 7
                        pe.matmul(o, hi, OHI[:, n % 2, k, :], start=first, stop=False)
                        pe.matmul(o, hi, OLO[:, n % 2, k, :], start=False, stop=False)
                        mm = pe.matmul(o, lo, OHI[:, n % 2, k, :], start=False, stop=last)
                    if half == 1:
                        mm.then_inc(out_ps, 1)
                pe.drain().then_inc(wo_read, 1)
            for t in range(NT):
                pe.wait_ge(h_set, t + 1)
                if t:
                    pe.wait_ge(turned_act, 2 * NTA + 2 * t)
                    pe.wait_ge(turned_dve, 2 * NTA + 2 * t)
                else:
                    pe.wait_ge(out_t, 16)
                for k in range(KT):
                    mm = pe.transpose(PS[:, k // 4, (k % 4) * P:(k % 4 + 1) * P], H2[:, t, k::KT], ident)
                mm.then_inc(turned, 1)
            pe.wait_ge(turned_act, 2 * NTA + 2 * NT)
            pe.wait_ge(turned_dve, 2 * NTA + 2 * NT)
            pe.wait_ge(small_in, SMALL_WR)
            for k in range(KT):
                j = k % 4
                mm = pe.matmul(PS[32 * j:32 * j + 32, 4, :], WR[:, k, :], H2T[:, k, :], start=k < 4, stop=k >= KT - 4)
            mm.then_inc(r_part, 1)
            pe.wait_ge(r_copy, 1)
            for t in range(NT):
                mm = pe.matmul(PS[:, 5, E * t:E * (t + 1)], T3[:, 0, t * P:(t + 1) * P], sel[:, 0:E], start=True, stop=True)
            mm.then_inc(r_log, 1)
            pe.drain().then_inc(moe_read, RD - SLOTS)
            pe.wait_ge(r_dve, 4)
            for t in range(NT):
                mm = pe.transpose(PS[0:E, 6, t * P:(t + 1) * P], AFF[:, t, :], ident)
            mm.then_inc(aT_ps, 1)
            pe.wait_ge(topk, 21)
            for t in range(NT):
                mm = pe.transpose(PS[:, 7, E * t:E * (t + 1)], AT[:, 4, t * P:(t + 1) * P], ident[0:E, 0:E])
            mm.then_inc(posT_ps, 1)
            meet(pe, "pe")

            def gather(m):
                pe.wait_ge(psel_set, m + 1)
                for c in range(4):
                    for t in range(NT):
                        mm = pe.matmul(PS[:, 4 + c, :], PSEL[:, t, :], H2[:, t, c * 512:(c + 1) * 512], start=t == 0, stop=t == NT - 1)
                    mm.then_inc(xs_ps, 1)

            def turn_rows(m):
                pe.wait_ge(xs_act, 2 * m + 2)
                pe.wait_ge(xs_dve, 2 * m + 2)
                for k in range(KT):
                    mm = pe.transpose(PS[:, k // 4, (k % 4) * P:(k % 4 + 1) * P], XS[:, k::KT], ident)
                    if k % 4 == 3:
                        mm.then_inc(xst_ps, 1)

            def expert_pair(m, last):
                pe.wait_ge(xst_act, 2 * m + 2)
                pe.wait_ge(xst_dve, 2 * m + 2)
                pe.wait_ge(ye_set, 4 * m + 4)
                for l in range(16):
                    pos = l % RD
                    pe.wait_ge(filled[pos], 16 * (NL // RD) * m + 16 * (before4[pos] + l // RD + 1))
                    w = ring6[pos].rearrange("p a b -> p (a b)").rearrange("p (e k n) -> p e k n", e=2, k=2)
                    for kk in range(2):
                        k = 2 * (l % 8) + kk
                        for half in range(2):
                            for e in range(2):
                                mm = pe.matmul(PS[64 * e:64 * e + 64, 2 * (l // 8) + half, :], XST[:, k, 64 * e:64 * e + 64],
                                               w[:, e, kk, half * 512:(half + 1) * 512], start=k == 0, stop=k == KT - 1)
                    mm.then_inc(moe_read, 1)
                if not last:
                    pe.wait_ge(acc_set, 16 * m + 16)
                    gather(m + 1)
                pe.wait_ge(hid_set, m + 1)
                if not last:
                    turn_rows(m + 1)
                else:
                    pe.wait_ge(acc_set, 16 * m + 16)
                for f in range(FF // P):
                    mm = pe.transpose(PS[:, 4 + f // 4, (f % 4) * P:(f % 4 + 1) * P], HID[:, f::FF // P], ident)
                    if f % 4 == 3:
                        mm.then_inc(hidT_ps, 1)
                pe.wait_ge(pg_set, m + 1)
                for t in range(NT):
                    mm = pe.transpose(PS[:, 6, t * P:(t + 1) * P], PG[:, t, :], ident)
                mm.then_inc(pgt_ps, 1)
                pe.wait_ge(hidT_act, m + 1)
                pe.wait_ge(hidT_dve, m + 1)
                if not last:
                    pe.wait_ge(xst_act, 2 * m + 4)
                    pe.wait_ge(xst_dve, 2 * m + 4)
                for l in range(16, NL):
                    pos, f = l % RD, l - 16
                    pe.wait_ge(filled[pos], 16 * (NL // RD) * m + 16 * (before4[pos] + l // RD + 1))
                    w = ring6[pos].rearrange("p a b -> p (a b)").rearrange("p (e n) -> p e n", e=2)
                    for c in range(4):
                        for e in range(2):
                            mm = pe.matmul(PS[64 * e:64 * e + 64, c, :], HIDT[:, f, 64 * e:64 * e + 64],
                                           w[:, e, c * 512:(c + 1) * 512], start=f == 0, stop=f == FF // P - 1)
                    mm.then_inc(moe_read, 1)
                pe.wait_ge(pgt_set, m + 1)
                pe.wait_ge(ye_set, 4 * m + 8)
                for g in range(16):
                    t, c = divmod(g, 4)
                    if g >= 4:
                        pe.wait_ge(acc_set, 16 * m + g + 13)
                    pe.matmul(PS[:, 4 + g % 4, :], PGT[:, t * P:(t + 1) * P], XS[:, c * 512:(c + 1) * 512], start=True,
                              stop=True).then_inc(sc_ps, 1)

            gather(0)
            turn_rows(0)
            with pe.Fori(0, E // 2 - 1) as m:
                expert_pair(m, False)
            expert_pair(E // 2 - 1, True)

        @block.scalar
        def _(act):
            act.wait_ge(cst_in, 48)
            act.activation(CSIL[:, :, :], COL[:, Q_C:Q_C + 32].rearrange("p (k v) -> p k v", v=2), ACT.Silu).then_inc(csil_set, 1)
            act.wait_ge(csil_set, 1)
            act.wait_ge(pads_zero, 1)
            act.copy(CSILP[:, :, 0:2], CSIL[:, :, :]).then_inc(csilp_set, 1)
            for t in range(NTA):
                act.wait_ge(x_in[t % 2], 16 * (t // 2 + 1))
                act.activation(JUNK0[:, :], XT[:, t % 2, :], ACT.Square, accum_out=ss0[:, t:t + 1]).then_inc(rms_ss, 1)
                act.wait_ge(rms_ss, t + 1)
                act.activation(rs0[:, t:t + 1], ss0[:, t:t + 1], ACT.Sqrt, bias=eps, scale=1.0 / D).then_inc(rms_sd, 1)
                act.wait_ge(turned, t + 1)
                for q in range(2):
                    act.copy(token_cols(4 * q, t),
                             PS[:, q, :].rearrange("p (a b) -> p a b", a=4)).then_inc(turned_act, 1)
            for n in range(ADA1):
                act.wait_ge(ada_read, n + 1)
                act.copy(ADAROW[:, n * SW:(n + 1) * SW], PS[:, 4 + n % 2, 0:SW]).then_inc(ada_evac, 1)
            act.wait_ge(mod_set, 4)
            for k in range(KT):
                act.activation(HTC[:, k, :], HTC[:, k, :], ACT.Identity, bias=MOD[:, 0, k, 1:2],
                               scale=MODA[:, k, 1:2]).then_inc(mod_ctx, 1)

            act.wait_ge(pads_zero, 2)
            pieces = proj_of("xbc", "xbc2")

            def conv_silu(n):
                gr = pieces[n]
                b = gr["b"] + (4 if gr["name"] == "xbc2" else 0)
                u = UC[:, b, :] if gr["ctx"] else UL[:, b, :]
                act.wait_ge(conv_done, n + 1)
                act.activation(u, u, ACT.Silu).then_inc(u_set, 1)

            for n, gr in enumerate(pieces):
                act.wait_ge(proj_done, gr["n"] + 1)
                if n >= 2:
                    act.wait_ge(conv_done, n - 1)
                w, o = (NCTX, 518) if gr["ctx"] else (N, 2)
                src = PS[:, gr["n"] % 2, 0:w]
                act.copy(XB[:, n % 2, o:o + w], src).then_inc(evac[gr["n"] % 2], 1)
                if n:
                    conv_silu(n - 1)
            conv_silu(len(pieces) - 1)
            act.wait_ge(dt_ps, 1)
            act.copy(DTT[:, 0:N], PS[:, 2, :]).then_inc(dt_t, 1)
            act.copy(DTT[:, N:], PS[:, 3, 0:NCTX]).then_inc(dt_t, 1)
            for gr in proj_of("z"):
                act.wait_ge(proj_done, gr["n"] + 1)
                act.activation(Z[:, gr["t"], :], PS[:, gr["n"] % 2, :], ACT.Silu).then_inc(evac[gr["n"] % 2], 1)
            for t in range(NTA):
                act.wait_ge(tok_T, t + 1)
                act.copy(BTOK[:, t, :], PS[:, 6 + t % 2, 0:256]).then_inc(tok_b, 1)
            def spill(n):
                gr = spilled[n]
                act.wait_ge(proj_done, gr["n"] + 1)
                if n:
                    act.wait_ge(spill_out, 16 * n)
                act.copy(SPILL[:, :], PS[:, gr["n"] % 2, :]).then_inc(evac[gr["n"] % 2], 1)
                act.wait_ge(evac[gr["n"] % 2], gr["n"] // 2 + 1)
                act.dma_start(spill_dram[n], SPILL[:, :]).then_inc(spill_out, 16)

            act.activation(aneg[:, :], ROW[:, R_ALOG:R_ALOG + 16], ACT.Exp).then_inc(dt_act, 1)
            act.wait_ge(dt_v, 1)
            act.activation(m0, dtv, ACT.Abs).then_inc(dt_act, 1)
            act.wait_ge(dt_act, 2)
            act.activation(ex, m0, ACT.Exp, scale=-1.0).then_inc(dt_act, 1)
            act.wait_ge(dt_act, 3)
            act.activation(lnu, ex, ACT.Ln, bias=CST[:, K_ONE:K_ONE + 1]).then_inc(dt_act, 1)
            spill(0)
            act.wait_ge(cum_dve, 1)
            act.activation(ecum, ncum, ACT.Exp, scale=-1.0).then_inc(cum_exp, 1)
            act.wait_ge(cum_dve, 2)
            act.activation(etot, PS[:, 5, 96:192].rearrange("p (t j) -> p t j", j=16), ACT.Exp).then_inc(cum_exp, 1)
            act.activation(tcum, tcum, ACT.Exp).then_inc(cum_exp, 1)
            for n in range(1, 6):
                spill(n)
            for t in range(NT):
                act.wait_ge(seg_dve, 16 * t + 8)
                act.activation(LSEG[:, 0:8, :], LSEG[:, 0:8, :], ACT.Exp).then_inc(seg_exp, 1)
                act.wait_ge(seg_dve, 16 * t + 16)
                act.activation(LSEG[:, 8:16, :], LSEG[:, 8:16, :], ACT.Exp).then_inc(seg_exp, 1)
                spill(6 + 2 * t)
                act.wait_ge(y_dve, 11 * t + 7)
                for g in range(2):
                    act.activation(TMP[:, 2, g * 256:(g + 1) * 256], TMP[:, 0, g * 256:(g + 1) * 256], ACT.Square,
                                   accum_out=ex[:, t, g:g + 1]).then_inc(y_act, 1)
                act.wait_ge(y_act, 3 * t + 2)
                act.activation(m0[:, t, 0:2], ex[:, t, 0:2], ACT.Sqrt, bias=eps, scale=1.0 / 256).then_inc(y_act, 1)
                spill(7 + 2 * t)
            meet(act, "act")

            def evacuate(eng, copy, gs, parity, dest):
                for gr in gs:
                    if gr["n"] % 2 == parity:
                        eng.wait_ge(proj_done, gr["n"] + 1)
                        w = NCTX if gr.get("ctx") else 512
                        copy(dest(gr), PS[:, parity, 0:w]).then_inc(evac[parity], 1)

            for n in range(1, 16, 2):
                act.wait_ge(fc_ps, n + 1)
                act.wait_ge(fc_set, n)
                act.copy(XCS[:, n % NT, n // NT, :], PS[:, 2 + n % 2, 0:256]).then_inc(fc_set, 1)
            act.wait_ge(g_ms, 2)
            act.activation(SMG[:, 32:60], SMG[:, 0:28], ACT.Sqrt, bias=eps, scale=1.0 / HD).then_inc(g_sd, 1)
            for g in range(4):
                act.wait_ge(fn_ps, g + 1)
                act.copy(OT[:, 3, g, :], PS[:, 4 + g % 2, :]).then_inc(fn_set, 1)
            for g in range(2):
                act.wait_ge(g_T, HEADS + g + 1)
                act.copy(GKT[:, g, :], PS[:, 4:6, :].rearrange("p a b -> p (a b)")[:, 0:NA_ALL]).then_inc(g_Tset, 1)
            meet(act, "act")

            def attend(s):
                def head_out(h):
                    act.wait_ge(att_pv, s.h + h + 1)
                    act.copy(OT[:, s.o, h, :], PS[:, 6, :]).then_inc(att_out, 1)

                for n in range(HEADS * NT + 2):
                    if n < HEADS * NT:
                        act.wait_ge(att_mx, s.u + n + 1)
                        pr = s.p[:, n % 3, :]
                        if s.bias is None:
                            if n >= 3:
                                act.wait_ge(att_pT, s.u + n - 2)
                            src = PS[:, 2 * (n % 2):2 * (n % 2) + 2, :].rearrange("p a b -> p (a b)")[:, 0:NA_ALL]
                            sc = SCALE
                        else:
                            src, sc = pr, 1.0
                        act.activation(pr, src, ACT.Exp, bias=s.st[:, 1, n:n + 1], scale=sc,
                                       accum_out=s.st[:, 2, n:n + 1]).then_inc(att_exp, 1)
                    if n >= 2:
                        m = n - 2
                        h, t = divmod(m, NT)
                        if t == 0 and h:
                            head_out(h - 1)
                        act.wait_ge(att_pT, s.u + m + 1)
                        act.copy(s.pt[:, 4:6, t * P:(t + 1) * P],
                                 PS[:, 5, 0:256].rearrange("p (a b) -> p a b", a=2)).then_inc(att_pT_act, 1)
                head_out(HEADS - 1)

            attend(gqa)
            meet(act, "act")
            ndest = lambda gr: (NV[:, gr["t"], :] if gr["mode"] == "R" else NQT[:, gr["b"], :] if gr["name"] == "naq"
                                else NKT[:, gr["b"], N:] if gr["ctx"] else NKT[:, gr["b"], 0:N])
            evacuate(act, act.copy, proj_of("naq", "nak", "nav"), 0, ndest)
            meet(act, "act")
            attend(na)
            meet(act, "act")
            act.sem_inc(gate_set, 2)
            act.sem_inc(stage_set, 2)
            for k in range(2):
                act.sem_inc(stage_out[k], 16)
            for k in range(KT):
                act.copy(HHI[k], HT[:, k, :]).then_inc(hh_hi, 1)
            with act.Fori(0, NB) as i:
                with act.Fori(0, 8) as q:
                    for k in range(2):
                        n = 16 * i + 2 * q + k
                        act.wait_ge(gate_ps, n + 1)
                        act.wait_ge(gated, n + 1)
                        act.activation(SG[:, k, :], PS[:, k, :], ACT.Sigmoid).then_inc(gate_set, 1)
                        act.wait_ge(ada_ps, n + 1 + 2)
                        act.wait_ge(stage_out[k], (8 * i + q) * 16 + 16)
                        act.copy(STAGE[0:1, k, :], PS[0:1, 4 + k, 0:P]).then_inc(stage_set, 1)
                        act.wait_ge(stage_set, n + 1 + 2)
                        act.dma_start(ada_dram.rearrange("(a n) -> a n", a=1)[:, bass.ds(n * P, P)],
                                      STAGE[0:1, k, :]).then_inc(stage_out[k], 16)
            meet(act, "act")
            for k in range(4):
                act.copy(YHI[:, 4 * k:4 * k + 4, :], YT[:, 4 * k:4 * k + 4, :]).then_inc(y_hi, 1)
            for n in range(8):
                act.wait_ge(raw_in[n % 2], 16 * (32 + n // 2 + 1))
                if n >= 2:
                    act.wait_ge(wo_read, n - 1)
                for h in range(2):
                    act.copy(OHI[:, n % 2, 4 * h:4 * h + 4, :], ORAW[:, n % 2, 4 * h:4 * h + 4, :]).then_inc(wo_hi, 1)
            for t in range(NT):
                act.wait_ge(xn_add, 16 + 0 if t == NT - 1 else 13 + t)
                act.activation(JUNK3[:, :], XN[:, t, :], ACT.Square, accum_out=SM3[:, t:t + 1]).then_inc(rms_ss, 1)
                act.wait_ge(rms_ss, NORM3 + t + 1)
                act.activation(SM3[:, 4 + t:5 + t], SM3[:, t:t + 1], ACT.Sqrt, bias=eps, scale=1.0 / D).then_inc(rms_sd, 1)
            for t in range(NT):
                act.wait_ge(turned, NTA + t + 1)
                for q in range(2):
                    act.copy(H2T[:, 4 * q:4 * q + 4, t * P:(t + 1) * P],
                             PS[:, q, :].rearrange("p (a b) -> p a b", a=4)).then_inc(turned_act, 1)
            act.wait_ge(r_part, 1)
            act.copy(T3[:, 0, :], PS[:, 4, :]).then_inc(r_copy, 1)
            act.wait_ge(r_dve, 2)
            act.activation(SM3[:, 64:128], SM3[:, 64:128], ACT.Exp).then_inc(r_exp, 1)
            meet(act, "act")

            def rows(m):
                for c in range(2):
                    act.wait_ge(xs_ps, 4 * m + c + 1)
                    act.copy(XS[:, c * 512:(c + 1) * 512], PS[:, 4 + c, :]).then_inc(xs_act, 1)
                for q in range(2):
                    act.wait_ge(xst_ps, 4 * m + q + 1)
                    act.copy(XST[:, 4 * q:4 * q + 4, :], PS[:, q, :].rearrange("p (a b) -> p a b", a=4)).then_inc(xst_act, 1)

            def expert_pair(m, last):
                act.wait_ge(moe_read, NL * m + RD + 8)
                act.activation(HID[:, :].rearrange("p (a b) -> p a b", a=2), PS[:, 0:2, :], ACT.Silu).then_inc(silu_set, 1)
                if not last:
                    rows(m + 1)
                act.wait_ge(hidT_ps, 2 * m + 1)
                act.copy(HIDT[:, 0:4, :], PS[:, 4, :].rearrange("p (a b) -> p a b", a=4)).then_inc(hidT_act, 1)

            rows(0)
            with act.Fori(0, E // 2 - 1) as m:
                expert_pair(m, False)
            expert_pair(E // 2 - 1, True)
            for t in range(NT):
                act.wait_ge(acc_set, 16 * (E // 2) + 4 * t + 4)
                act.activation(H2[:, t, :], XN[:, t, :], ACT.Square, accum_out=SM5[:, t:t + 1]).then_inc(rms_ss, 1)
                act.wait_ge(rms_ss, NORM5 + t + 1)
                act.activation(SM5[:, 4 + t:5 + t], SM5[:, t:t + 1], ACT.Sqrt, bias=eps, scale=1.0 / D).then_inc(rms_sd, 1)

        @block.vector
        def _(dve):
            tt, ts, stt = dve.tensor_tensor, dve.tensor_scalar, dve.scalar_tensor_tensor
            dve.wait_ge(cst_in, 48)
            for t in range(NTA):
                dve.wait_ge(rms_sd, t + 1)
                dve.reciprocal(rs0[:, t:t + 1], rs0[:, t:t + 1]).then_inc(rms_rs, 1)
                dve.wait_ge(rms_rs, t + 1)
                ts(XT[:, t % 2, :], XT[:, t % 2, :], rs0[:, t:t + 1], None, ALU.mult).then_inc(xn_set, 1)
                dve.wait_ge(turned, t + 1)
                for q in range(2, 4):
                    dve.tensor_copy(token_cols(4 * q, t),
                                    PS[:, q, :].rearrange("p (a b) -> p a b", a=4)).then_inc(turned_dve, 1)
            m = Steps(dve, mod_set)
            for v in range(2):
                dve.wait_ge(ada_col, v + 1)
                b = COL[:, Q_BADA + v * KT:Q_BADA + (v + 1) * KT].unsqueeze(2).to_broadcast([P, KT, 2])
                m.done(tt(MOD[:, v, :, :], PS[:, 6 + v, 0:32].rearrange("p (k l) -> p k l", l=2), b, ALU.add))
            m.wait()
            m.done(ts(MODA, MOD[:, 1, :, :], 1.0, None, ALU.add))
            m.wait()
            m.done(tt(MODA, MODA, COL[:, Q_NORM:Q_NORM + KT].unsqueeze(2).to_broadcast([P, KT, 2]), ALU.mult))
            m.wait()
            dve.wait_ge(turned_act, 2 * NTA)
            for k in range(KT):
                ts(HT[:, k, 0:N], HT[:, k, 0:N], MODA[:, k, 0:1], MOD[:, 0, k, 0:1], ALU.mult, ALU.add).then_inc(mod_lat, 1)

            pieces = proj_of("xbc", "xbc2")
            taps = Steps(dve, conv_tap)
            for n, gr in enumerate(pieces):
                b = gr["b"] + (4 if gr["name"] == "xbc2" else 0)
                dve.wait_ge(evac[gr["n"] % 2], gr["n"] // 2 + 1)
                w, o = (NCTX, 516) if gr["ctx"] else (N, 0)
                u = UC[:, b, :] if gr["ctx"] else UL[:, b, :]
                for tap in range(5):
                    wcol = COL[:, Q_CW + 5 * b + tap:Q_CW + 5 * b + tap + 1]
                    src = XB[:, n % 2, o + tap:o + tap + w]
                    if tap == 0:
                        taps.done(ts(u, src, wcol, COL[:, Q_CB + b:Q_CB + b + 1], ALU.mult, ALU.add))
                    else:
                        taps.wait()
                        ins = stt(u, src, wcol, u, ALU.mult, ALU.add)
                        if tap < 4:
                            taps.done(ins)
                        else:
                            ins.then_inc(conv_done, 1)
            for t in range(NTA):
                dve.wait_ge(tok_T, t + 1)
                dve.tensor_copy(XTOK[:, t, :], PS[:, 2 + t % 2, :]).then_inc(tok_x, 1)
            dve.wait_ge(dt_tok, 1)
            bc = lambda row: row.unsqueeze(1).to_broadcast([P, NTA, 16])
            tt(dtv, PS[:, 4, 0:96].rearrange("p (t j) -> p t j", j=16), bc(ROW[:, R_DTB:R_DTB + 16]), ALU.add).then_inc(dt_v, 1)
            q = Steps(dve, dt_dve)
            dve.wait_ge(dt_v, 1)
            q.done(ts(dts, dtv, 0.0, None, ALU.max))
            dve.wait_ge(dt_act, 3)
            q.done(ts(ded, ex, 1.0, -1.0, ALU.add, ALU.add))
            q.wait()
            q.done(tt(ded, ex, ded, ALU.subtract))
            dve.wait_ge(dt_act, 4)
            q.done(tt(dts, dts, lnu, ALU.add))
            q.wait()
            q.done(tt(dts, dts, ded, ALU.add))
            q.wait()
            q.done(tt(da, dts, bc(aneg[:, :]), ALU.mult))
            q.wait()
            q.done(ts(da, da, -1.0, None, ALU.mult))
            dve.wait_ge(cum_ps, 1)
            ts(ncum[:, :, 0:8], PS[:, 5, 0:48].rearrange("p (t j) -> p t j", j=8), -1.0, None, ALU.mult)
            ts(ncum[:, :, 8:16], PS[:, 5, 48:96].rearrange("p (t j) -> p t j", j=8), -1.0, None, ALU.mult).then_inc(cum_dve, 1)
            dve.wait_ge(cum_dve, 1)
            tt(tcum, PS[:, 5, 96:192].rearrange("p (t j) -> p t j", j=16), ncum, ALU.add).then_inc(cum_dve, 1)
            dve.wait_ge(cum_exp, 3)
            tt(wx, tcum, dts, ALU.mult).then_inc(wx_set, 1)
            store = {0: (3, 0, 1, 2, 3), 1: (0, 3, 2, 1, 0)}
            steps = [(i, d, t) for i, ft in enumerate(zip((4, 5, 0, 1, 2), (5, 4, 3, 2, 1))) for d, t in enumerate(ft)]
            st = Steps(dve, st_dve)
            v3 = lambda ap: ap.rearrange("p (h c) -> p h c", c=SHD)
            for n, (i, d, t) in enumerate(steps):
                hbuf = (HF, HB)[d]
                new = hbuf[:, store[d][i], :]
                dve.wait_ge(st_ps, n + 1)
                if i == 0:
                    st.done(dve.tensor_copy(new, PS[:, 2 + d, :]))
                else:
                    old = hbuf[:, store[d][i - 1], :]
                    st.wait()
                    st.done(tt(v3(new), v3(old), etot[:, t, 8 * d:8 * d + 8].unsqueeze(2).to_broadcast([P, SH, SHD]), ALU.mult))
                    st.wait()
                    st.done(tt(new, new, PS[:, 2 + d, :], ALU.add))
            assert st.n == 18
            sg, mm_, yy = Steps(dve, seg_dve), Steps(dve, m_dve), Steps(dve, y_dve)
            for t in range(NT):
                dve.wait_ge(seg_ps, t + 1)
                if t:
                    dve.wait_ge(y_ps, t)
                for j in range(16):
                    mask = CST[:, K_MF:K_MF + P] if j < 8 else CST[:, K_MB:K_MB + P]
                    sg.done(stt(LSEG[:, j, :], PS[:, 2 + j // 4, (j % 4) * P:(j % 4 + 1) * P], ncum[:, t, j:j + 1], mask,
                                ALU.add, ALU.add))
                dve.wait_ge(seg_exp, 2 * t + 2)
                bj = lambda x, d: x[:, t, 8 * d:8 * d + 8].unsqueeze(2)
                mm_.done(tt(LSEG[:, 8:16, :], LSEG[:, 8:16, :], bj(dts, 1).to_broadcast([P, SH, P]), ALU.mult))
                mm_.wait()
                dve.wait_ge(lf_set, t + 1)
                mm_.done(tt(LSEG[:, 0:8, :], LSEG[:, 0:8, :], LSEG[:, 8:16, :], ALU.add))
                mm_.wait()
                mm_.done(tt(LSEG[:, 0:8, :].rearrange("p (g e) l -> p g e l", g=2),
                            LSEG[:, 0:8, :].rearrange("p (g e) l -> p g e l", g=2),
                            PS[:, 7, 0:256].rearrange("p (g l) -> p g l", g=2).unsqueeze(2).to_broadcast([P, 2, 4, P]), ALU.mult))
                dve.wait_ge(y_ps, t + 1)
                if t:
                    dve.wait_ge(yT_ps, t)
                T0, T1 = TMP[:, 0, :], TMP[:, 1, :]
                yy.done(tt(v3(T0), v3(PS[:, 2, :]), bj(ecum, 0).to_broadcast([P, SH, SHD]), ALU.mult))
                yy.done(tt(v3(T1), v3(PS[:, 3, :]), bj(ecum, 1).to_broadcast([P, SH, SHD]), ALU.mult))
                yy.wait()
                yy.done(tt(T0, T0, T1, ALU.add))
                yy.wait()
                yy.done(tt(T0, T0, PS[:, 6, :], ALU.add))
                yy.done(tt(v3(T1), v3(XTOK[:, t, :]), ROW[:, R_DSK:R_DSK + SH].unsqueeze(2).to_broadcast([P, SH, SHD]), ALU.mult))
                yy.wait()
                yy.done(tt(T0, T0, T1, ALU.add))
                yy.wait()
                yy.done(tt(T0, T0, Z[:, t, :], ALU.mult))
                dve.wait_ge(y_act, 3 * t + 3)
                yy.done(dve.reciprocal(m0[:, t, 2:4], m0[:, t, 0:2]))
                yy.wait()
                for g in range(2):
                    yy.done(ts(TMP[:, 0, g * 256:(g + 1) * 256], TMP[:, 0, g * 256:(g + 1) * 256], m0[:, t, 2 + g:3 + g], None, ALU.mult))
                yy.wait()
                yy.done(tt(T0, T0, ROW[:, R_SSDN:R_SSDN + 512], ALU.mult))
                assert yy.n == 11 * (t + 1)
                dve.wait_ge(yT_ps, t + 1)
                dve.tensor_copy(OT[:, 1, :, t * P:(t + 1) * P], PS[:, 7, :].rearrange("p (a b) -> p a b", a=4)).then_inc(yT_set, 1)
            meet(dve, "dve")

            def evacuate(gs, parity, dest):
                for gr in gs:
                    if gr["n"] % 2 == parity:
                        dve.wait_ge(proj_done, gr["n"] + 1)
                        w = NCTX if gr.get("ctx") else 512
                        dve.tensor_copy(dest(gr), PS[:, parity, 0:w]).then_inc(evac[parity], 1)

            for n in range(0, 16, 2):
                dve.wait_ge(fc_ps, n + 1)
                if n:
                    dve.wait_ge(fc_set, n)
                dve.tensor_copy(XCS[:, n % NT, n // NT, :], PS[:, 2, 0:256]).then_inc(fc_set, 1)

            dve.wait_ge(gq_in, 16)
            v = Steps(dve, g_dve)
            q16 = lambda ap: ap.rearrange("p t (h c) -> p (t h) c", c=HD)
            v.done(tt(SQ[:, :, :], GQR[:, :, :], GQR[:, :, :], ALU.mult))
            v.wait()
            dve.tensor_reduce(SMG[:, 0:16], q16(SQ[:, :, :]), AX.X, ALU.add).then_inc(g_ms, 1)
            dve.wait_ge(g_sqk, 1)
            dve.tensor_reduce(SMG[:, 16:28], q16(SQK[:, :, :]), AX.X, ALU.add).then_inc(g_ms, 1)
            dve.wait_ge(g_sd, 1)
            dve.reciprocal(SMG[:, 32:60], SMG[:, 32:60]).then_inc(g_rs, 1)
            dve.wait_ge(g_rs, 1)
            v.done(tt(q16(GQR[:, :, :]), q16(GQR[:, :, :]), SMG[:, 32:48].unsqueeze(2).to_broadcast([P, 16, HD]), ALU.mult))
            v.wait()
            v.done(tt(q16(GQR[:, :, :]), q16(GQR[:, :, :]), ROW[:, R_QG:R_QG + HD].unsqueeze(1).to_broadcast([P, 16, HD]), ALU.mult))
            v.wait()
            dve.wait_ge(small_in, SMALL_TABLES)
            rotate(v, tt, GQR, RTQ, ROPE, HEADS)
            for h in range(HEADS):
                dve.wait_ge(g_T, h + 1)
                dve.tensor_copy(GQT[:, h, :], PS[:, 2, :]).then_inc(g_Tset, 1)
            meet(dve, "dve")

            def attend(s):
                units = HEADS * NT
                stat = Steps(dve, att_stat)
                stat.n = 2 * s.u
                for n in range(units + 2):
                    if n < units:
                        h, t = divmod(n, NT)
                        dve.wait_ge(att_scores, s.u + n + 1)
                        src = PS[:, 2 * (n % 2):2 * (n % 2) + 2, :].rearrange("p a b -> p (a b)")
                        if s.bias is not None:
                            if n >= 3:
                                dve.wait_ge(att_pT, s.u + n - 2)
                            if t == 0:
                                dve.wait_ge(bias_set, h + 1)
                            pr = s.p[:, n % 3, :]
                            u0 = 7 - 2 * t
                            stt(pr[:, 0:N], src[:, 0:N], SCALE, NBIAS[:, h % 2, u0:u0 + 8, :].rearrange("p a b -> p (a b)"),
                                ALU.mult, ALU.add)
                            ts(pr[:, N:], src[:, N:NA_ALL], SCALE, None, ALU.mult).then_inc(att_raw, 1)
                            dve.wait_ge(att_raw, n + 1)
                            src, sc = pr, 1.0
                        else:
                            src, sc = src[:, 0:NA_ALL], SCALE
                        st0, st1 = s.st[:, 0, n:n + 1], s.st[:, 1, n:n + 1]
                        stat.done(dve.tensor_reduce(st0, src, AX.X, ALU.max))
                        stat.wait()
                        ts(st1, st0, -sc, None, ALU.mult).then_inc(att_mx, 1)
                    if 1 <= n <= units:
                        m = n - 1
                        dve.wait_ge(att_exp, s.u + m + 1)
                        st3 = s.st[:, 3, m:m + 1]
                        stat.done(dve.reciprocal(st3, s.st[:, 2, m:m + 1]))
                        stat.wait()
                        ts(s.p[:, m % 3, :], s.p[:, m % 3, :], st3, None, ALU.mult).then_inc(att_pn, 1)
                    if n >= 2:
                        m = n - 2
                        h, t = divmod(m, NT)
                        dve.wait_ge(att_pT, s.u + m + 1)
                        if t == 0 and h:
                            dve.wait_ge(att_pv, s.h + h)
                        dve.tensor_copy(s.pt[:, 0:4, t * P:(t + 1) * P],
                                        PS[:, 4, :].rearrange("p (a b) -> p a b", a=4)).then_inc(att_pT_dve, 1)

            attend(gqa)
            meet(dve, "dve")
            ndest = lambda gr: (NV[:, gr["t"], :] if gr["mode"] == "R" else NQT[:, gr["b"], :] if gr["name"] == "naq"
                                else NKT[:, gr["b"], N:] if gr["ctx"] else NKT[:, gr["b"], 0:N])
            evacuate(proj_of("naq", "nak", "nav"), 1, ndest)
            meet(dve, "dve")
            attend(na)
            meet(dve, "dve")
            dve.sem_inc(ada_tap, 16)
            dve.sem_inc(gated, 2)
            for k in range(KT):
                dve.wait_ge(hh_hi, k + 1)
                tt(HLO[:, k, :], HT[:, k, :], HHI[k].bitcast(F32), ALU.subtract).then_inc(hh_lo, 1)
            dve.wait_ge(yt_zero, 1)
            with dve.Fori(0, NB) as i:
                with dve.Fori(0, 8) as q:
                    for k in range(2):
                        n = 16 * i + 2 * q + k
                        dve.wait_ge(ada_in, 16 * n + 16)
                        dve.wait_ge(ada_ps, n + 1)
                        for c in range(KT):
                            w, col = WADA[:, c, :], CSIL[:, c, 0:1]
                            if c == 0:
                                ts(ADACC[:, k, :], w, col, None, ALU.mult).then_inc(ada_tap, 1)
                            else:
                                dve.wait_ge(ada_tap, 16 * n + 16 + c)
                                stt(ADACC[:, k, :], w, col, ADACC[:, k, :], ALU.mult, ALU.add).then_inc(ada_tap, 1)
                        dve.wait_ge(gate_set, n + 1 + 2)
                        dve.wait_ge(br_ps, n + 1 + 2)
                        tt(GP[:, k, :], SG[:, k, :], PS[:, 2 + k, :], ALU.mult).then_inc(gated, 1)
                        dve.wait_ge(gated, n + 1 + 2)
                        y = YT[:, bass.ds(2 * q + k, 1), :].rearrange("p a n -> p (a n)")
                        tt(y, y, GP[:, k, :], ALU.add).then_inc(yt_add, 1)
            meet(dve, "dve")
            for k in range(4):
                dve.wait_ge(y_hi, k + 1)
                tt(YLO[:, 4 * k:4 * k + 4, :], YT[:, 4 * k:4 * k + 4, :], YHI[:, 4 * k:4 * k + 4, :].bitcast(F32),
                   ALU.subtract).then_inc(y_lo, 1)

            def add_projection(c):
                for t in range(NT):
                    g = 4 * c + t
                    dve.wait_ge(out_ps, g + 1)
                    tt(T3[:, g % 2, :], PS[:, 4 * (c % 2) + t, :], G1R[:, c * 512:(c + 1) * 512], ALU.mult).then_inc(out_t, 1)
                    dve.wait_ge(out_t, g + 1)
                    x = XN[:, t, c * 512:(c + 1) * 512]
                    tt(x, x, T3[:, g % 2, :], ALU.add).then_inc(xn_add, 1)

            for n in range(8):
                for h in range(2):
                    dve.wait_ge(wo_hi, 2 * n + h + 1)
                    tt(OLO[:, n % 2, 4 * h:4 * h + 4, :], ORAW[:, n % 2, 4 * h:4 * h + 4, :],
                       OHI[:, n % 2, 4 * h:4 * h + 4, :].bitcast(F32), ALU.subtract).then_inc(wo_lo, 1)
                if n == 1:
                    dve.wait_ge(rows_in, 80)
                    stt(SC2[:, :], SC2[:, :], 1.0, NF[:, :], ALU.add, ALU.mult).then_inc(sc2_set, 1)
                if n >= 3 and n % 2:
                    add_projection((n - 3) // 2)
            add_projection(3)
            dve.wait_ge(sc2_set, 1)
            for t in range(NT):
                dve.wait_ge(rms_sd, NORM3 + t + 1)
                dve.reciprocal(SM3[:, 8 + t:9 + t], SM3[:, 4 + t:5 + t]).then_inc(rms_rs, 1)
                dve.wait_ge(rms_rs, NORM3 + t + 1)
                stt(H2[:, t, :], XN[:, t, :], SM3[:, 8 + t:9 + t], SC2[:, :], ALU.mult, ALU.mult).then_inc(h_mul, 1)
            for t in range(NT):
                dve.wait_ge(turned, NTA + t + 1)
                for q in range(2, 4):
                    dve.tensor_copy(H2T[:, 4 * q:4 * q + 4, t * P:(t + 1) * P],
                                    PS[:, q, :].rearrange("p (a b) -> p a b", a=4)).then_inc(turned_dve, 1)
            LG = SM3[:, 64:128].rearrange("p (t e) -> p t e", e=E)
            bE = lambda o: SM3[:, o:o + 4].unsqueeze(2).to_broadcast([P, NT, E])
            r = Steps(dve, r_dve)
            dve.wait_ge(r_log, 1)
            r.done(dve.tensor_reduce(SM3[:, 16:20], PS[:, 5, 0:64].rearrange("p (t e) -> p t e", e=E), AX.X, ALU.max))
            r.wait()
            r.done(tt(LG, PS[:, 5, 0:64].rearrange("p (t e) -> p t e", e=E), bE(16), ALU.subtract))
            dve.wait_ge(r_exp, 1)
            dve.tensor_reduce(SM3[:, 20:24], LG, AX.X, ALU.add).then_inc(pos_set, 1)
            dve.wait_ge(pos_set, 1)
            r.done(dve.reciprocal(SM3[:, 24:28], SM3[:, 20:24]))
            r.wait()
            r.done(tt(AFF[:, :, :], LG, bE(24), ALU.mult))
            k = Steps(dve, topk)
            dve.wait_ge(aT_ps, 1)
            k.done(dve.tensor_copy(AT[:, 0, :], PS[0:E, 6, :]))
            k.done(dve.memset(AT[:, 2, :], 1.0))
            for i in range(CAP // 8):
                k.wait()
                k.done(dve.max(M8[:, i, :], AT[:, i % 2, :]))
                k.wait()
                k.done(dve.match_replace(AT[:, (i + 1) % 2, :], M8[:, i, :], AT[:, i % 2, :], -1.0))
            k.wait()
            k.done(ts(AT[:, 1, :], AT[:, (CAP // 8) % 2, :], 0.0, None, ALU.is_lt))
            k.wait()
            k.done(dve.tensor_tensor_scan(AT[:, 3, :], AT[:, 2, :], AT[:, 1, :], 0.0, ALU.mult, ALU.add))
            k.wait()
            dve.tensor_tensor(AT[:, 3, :], AT[:, 3, :], AT[:, 1, :], ALU.mult).then_inc(pos_set, 1)
            dve.wait_ge(pos_set, 2)
            k.done(ts(AT[:, 4, :], AT[:, 3, :], -1.0, None, ALU.add))
            assert k.n == 21
            dve.wait_ge(posT_ps, 1)
            dve.tensor_copy(POS[:, :, :], PS[:, 7, 0:64].rearrange("p (t e) -> p t e", e=E)).then_inc(pos_set, 1)
            meet(dve, "dve")

            p4 = lambda x: x[:, :, :].rearrange("p t (e s) -> p t e s", e=2)

            def choice(m):
                iota = CST[:, K_IOTA:K_IOTA + 64].unsqueeze(1).unsqueeze(1).to_broadcast([P, NT, 2, 64])
                tt(p4(PSEL), POS[:, :, bass.ds(2 * m, 2)].unsqueeze(3).to_broadcast([P, NT, 2, 64]), iota,
                   ALU.is_equal).then_inc(psel_set, 1)

            def weighted_choice(m):
                dve.wait_ge(psel_set, m + 1)
                tt(p4(PG), p4(PSEL), AFF[:, :, bass.ds(2 * m, 2)].unsqueeze(3).to_broadcast([P, NT, 2, 64]),
                   ALU.mult).then_inc(pg_set, 1)

            def rows(m):
                for c in range(2, 4):
                    dve.wait_ge(xs_ps, 4 * m + c + 1)
                    dve.tensor_copy(XS[:, c * 512:(c + 1) * 512], PS[:, 4 + c, :]).then_inc(xs_dve, 1)
                for q in range(2, 4):
                    dve.wait_ge(xst_ps, 4 * m + q + 1)
                    dve.tensor_copy(XST[:, 4 * q:4 * q + 4, :], PS[:, q, :].rearrange("p (a b) -> p a b", a=4)).then_inc(xst_dve, 1)

            def expert_pair(m, last):
                if not last:
                    choice(m + 1)
                dve.wait_ge(moe_read, NL * m + RD + 16)
                dve.wait_ge(silu_set, m + 1)
                h = HID[:, :].rearrange("p (a b) -> p a b", a=2)
                tt(h, h, PS[:, 2:4, :], ALU.mult).then_inc(hid_set, 1)
                if not last:
                    rows(m + 1)
                dve.wait_ge(hidT_ps, 2 * m + 2)
                dve.tensor_copy(HIDT[:, 4:8, :], PS[:, 5, :].rearrange("p (a b) -> p a b", a=4)).then_inc(hidT_dve, 1)
                dve.wait_ge(pgt_ps, m + 1)
                dve.tensor_copy(PGT[:, :], PS[:, 6, :]).then_inc(pgt_set, 1)
                if not last:
                    weighted_choice(m + 1)
                dve.wait_ge(moe_read, NL * m + RD + NL)
                for c in range(4):
                    tt(XS[:, c * 512:(c + 1) * 512], PS[:, c, :], G2R[:, c * 512:(c + 1) * 512], ALU.mult).then_inc(ye_set, 1)
                for g in range(16):
                    t, c = divmod(g, 4)
                    dve.wait_ge(sc_ps, 16 * m + g + 1)
                    x = XN[:, t, c * 512:(c + 1) * 512]
                    tt(x, x, PS[:, 4 + g % 4, :], ALU.add).then_inc(acc_set, 1)

            dve.sem_inc(ye_set, 4)
            dve.sem_inc(acc_set, 16)
            choice(0)
            weighted_choice(0)
            dve.wait_ge(small_in, SMALL_G2)
            rows(0)
            with dve.Fori(0, E // 2 - 1) as m:
                expert_pair(m, False)
            expert_pair(E // 2 - 1, True)
            dve.wait_ge(cst_in, 64)
            for t in range(NT):
                dve.wait_ge(rms_sd, NORM5 + t + 1)
                dve.reciprocal(SM5[:, 8 + t:9 + t], SM5[:, 4 + t:5 + t]).then_inc(rms_rs, 1)
                dve.wait_ge(rms_rs, NORM5 + t + 1)
                stt(XN[:, t, :], XN[:, t, :], SM5[:, 8 + t:9 + t], FN[:, :], ALU.mult, ALU.mult).then_inc(o_set, 1)

        @block.gpsimd
        def _(pool):
            tt = pool.tensor_tensor
            pool.memset(CSILP[:, :, :], 0.0).then_inc(pads_zero, 1)
            for t in range(NTA):
                if t >= 2:
                    pool.wait_ge(turned, t - 1)
                src = a["x"][t * P:(t + 1) * P, :] if t < NT else a["ctx"][(t - NT) * P:(t - NT + 1) * P, :]
                pool.dma_start(XT[:, t % 2, :], src).then_inc(x_in[t % 2], 16)
            pool.memset(WDT[:, :, :], 0.0).then_inc(dtw_zero, 1)
            pool.memset(XB[:, :, :], 0.0).then_inc(pads_zero, 1)
            pool.wait_ge(dtw_zero, 1)
            pool.dma_start(WDT[:, :, 0:16], w_in[:, :, C_DT:C_DT + 16]).then_inc(small_in, 16)
            pool.wait_ge(wx_set, 1)
            pool.wait_ge(tok_x, NTA)
            v3 = lambda ap: ap.rearrange("p (h c) -> p h c", c=SHD)
            n = 0
            for i, ft in enumerate(zip((4, 5, 0, 1, 2), (5, 4, 3, 2, 1))):
                for d, t in enumerate(ft):
                    if i:
                        pool.wait_ge(st_ps, n - 1)
                    tt(v3(TMP[:, d, :]), v3(XTOK[:, t, :]), wx[:, t, 8 * d:8 * d + 8].unsqueeze(2).to_broadcast([P, SH, SHD]),
                       ALU.mult).then_inc(xw_set, 1)
                    n += 1
            for t in range(NT):
                if t:
                    pool.wait_ge(seg_ps, t)
                for d, tri in enumerate((triu, tril)):
                    tt(DATRI[:, 8 * d:8 * d + 8, :], tri.unsqueeze(1).to_broadcast([P, SH, P]),
                       da[:, t, 8 * d:8 * d + 8].unsqueeze(2).to_broadcast([P, SH, P]), ALU.mult).then_inc(datri_set, 1)
                pool.wait_ge(seg_exp, 2 * t + 1)
                tt(LSEG[:, 0:8, :], LSEG[:, 0:8, :], dts[:, t, 0:8].unsqueeze(2).to_broadcast([P, SH, P]),
                   ALU.mult).then_inc(lf_set, 1)
            meet(pool, "pool")
            pool.dma_start(DFTC[:, :], a["dft_c"]).then_inc(small_in, 16)
            pool.dma_start(ROPE[:, :, :, :], a["rope"].rearrange("p (t c n) -> p t c n", t=NT, c=2)).then_inc(small_in, 16)
            pool.wait_ge(f_in, 16)
            pool.dma_start(DFTN[:, :, :, :], a["dft_n"].rearrange("p (t c n) -> p t c n", t=NT, c=2)).then_inc(dftn_in, 16)
            pool.wait_ge(gkv_in, 16)
            v = Steps(pool, g_pool)
            kraw = GKV[:, :, 0:256]
            tt(SQK[:, :, :], kraw, kraw, ALU.mult).then_inc(g_sqk, 1)
            pool.wait_ge(g_rs, 1)
            k3 = kraw.rearrange("p t (h c) -> p t h c", c=HD)
            rk = SMG[:, 48:60].rearrange("p (t h) -> p t h", h=2).unsqueeze(3).to_broadcast([P, NTA, 2, HD])
            v.done(tt(k3, k3, rk, ALU.mult))
            v.wait()
            for h in range(2):
                kh = GKV[:, :, h * HD:(h + 1) * HD]
                v.done(tt(kh, kh, ROW[:, R_KG:R_KG + HD].unsqueeze(1).to_broadcast([P, NTA, HD]), ALU.mult))
            v.wait()
            pool.wait_ge(small_in, SMALL_TABLES)
            rotate(v, tt, GKV, RTK, ROPE, 2)
            meet(pool, "pool")
            meet(pool, "pool")
            def load_bias(h):
                for rr in range(2):
                    pool.dma_start(NBIAS[rr * GRID_W:(rr + 1) * GRID_W, h % 2, :, :],
                                   a["rpb_win"][:, h, 1 - rr:16 - rr, :]).then_inc(bias_in, 16)

            load_bias(0)
            load_bias(1)
            pool.wait_ge(bias_in, 64)
            for h in range(HEADS):
                if h >= 2:
                    pool.wait_ge(att_raw, NT * (h - 1))
                    load_bias(h)
                    pool.wait_ge(bias_in, 32 * (h + 1))
                tt(NBIAS[:, h % 2, :, :], NBIAS[:, h % 2, :, :],
                   CST[:, K_NAM:K_NAM + GRID_W].unsqueeze(1).to_broadcast([P, 15, GRID_W]), ALU.add).then_inc(bias_set, 1)
                if h == 1:
                    meet(pool, "pool")
            meet(pool, "pool")
            pool.memset(YT[:, :, :], 0.0).then_inc(yt_zero, 1)
            with pool.Fori(0, 32) as q:
                for k in range(2):
                    n = 2 * q + k
                    pool.wait_ge(raw_in[k], 16 * q + 16)
                    pool.wait_ge(br_ps, n + 1)
                    tt(WHI[:, k, :, :], RAW[:, k, :, :], ones.unsqueeze(1).to_broadcast([P, KT, P]),
                       ALU.mult).then_inc(w_hi, 1)
                    pool.wait_ge(w_hi, n + 1)
                    tt(WLO[:, k, :, :], RAW[:, k, :, :], WHI[:, k, :, :].bitcast(F32), ALU.subtract).then_inc(w_lo, 1)
            meet(pool, "pool")
            pool.memset(WR[:, :, :], 0.0).then_inc(wr_zero, 1)
            pool.wait_ge(wr_zero, 1)
            pool.dma_start(WR[:, :, 0:E], a["w_router"].rearrange("(p k) e -> p k e", k=KT)).then_inc(small_in, 16)
            for t in range(NT):
                pool.wait_ge(h_mul, t + 1)
                tt(H2[:, t, :], H2[:, t, :], SH2[:, :], ALU.add).then_inc(h_set, 1)
            pool.wait_ge(r_log, 1)
            pool.dma_start(G2R[:, :], ada_dram[3 * D:4 * D].partition_broadcast(P)).then_inc(small_in, 16)
            meet(pool, "pool")


def rotate(steps, tt, x, tmp, rope, heads):
    w = heads * 64
    for t in range(NT):
        v = x[:, t, 0:heads * HD].rearrange("p (m r d) -> p m r d", r=2, d=32)
        re, im = v[:, :, 0, :], v[:, :, 1, :]
        re = re.rearrange("p (h a) d -> p h a d", a=2)
        im = im.rearrange("p (h a) d -> p h a d", a=2)
        tab = lambda i: rope[:, t, i, :].rearrange("p (a d) -> p a d", a=2).unsqueeze(1).to_broadcast([P, heads, 2, 32])
        b = lambda i: tmp[:, i, 0:w].rearrange("p (h a d) -> p h a d", h=heads, a=2)
        if t:
            steps.wait()
        steps.done(tt(b(0), re, tab(0), ALU.mult))
        steps.done(tt(b(1), im, tab(1), ALU.mult))
        steps.done(tt(b(2), re, tab(1), ALU.mult))
        steps.done(tt(b(3), im, tab(0), ALU.mult))
        steps.wait()
        steps.done(tt(re, b(0), b(1), ALU.subtract))
        steps.done(tt(im, b(2), b(3), ALU.add))


def constants():
    i = np.arange(P)
    cst = np.zeros((P, K_W), np.float32)
    cst[:, K_ID:K_ID + P] = np.eye(P)
    cst[:, K_ONE:K_ONE + P] = 1
    up = i[:, None] <= i[None, :]
    cst[:, K_TU:K_TU + P] = up
    cst[:, K_TL:K_TL + P] = up.T
    cst[:, K_MF:K_MF + P] = np.where(up, 0, NEG)
    cst[:, K_MB:K_MB + P] = np.where(up.T, 0, NEG)
    c, kc = (i % GRID_W)[:, None], np.arange(GRID_W)[None, :]
    start = np.clip(c - NA_C // 2, 0, GRID_W - NA_C)
    cst[:, K_NAM:K_NAM + GRID_W] = np.where((kc >= start) & (kc < start + NA_C), 0, NEG)
    cst[:, K_IOTA:K_IOTA + 64] = np.arange(64)
    cst[:, K_SEL:K_SEL + 32] = (i % 32)[:, None] == np.arange(32)[None, :]
    cst[:, K_EPS] = EPS
    k = np.outer(np.arange(P), np.arange(P)) * (2 * np.pi / P)
    dft_c = np.concatenate([np.cos(k), np.sin(k)], 1).astype(np.float32)
    k = (np.outer(np.arange(N), np.arange(N)) % N) * (2 * np.pi / N)
    cs = np.stack([np.cos(k), -np.sin(k)], 1) / np.sqrt(N * P)
    dft_n = cs.reshape(NT, P, 2 * N).transpose(1, 0, 2).reshape(P, -1).astype(np.float32)
    t = np.arange(N)
    pos = np.stack([t // GRID_W, t % GRID_W], -1).astype(np.float32)
    inv = (np.float32(10000.0) ** (-np.arange(32, dtype=np.float32) / 32)).astype(np.float32)
    ang = (pos[:, :, None] * inv).reshape(N, 64)
    rope = np.stack([np.cos(ang), np.sin(ang)], 1).astype(np.float32)
    rope = rope.reshape(NT, P, 128).transpose(1, 0, 2).reshape(P, -1)
    return dict(cst=cst, dft_c=dft_c, dft_n=np.ascontiguousarray(dft_n), rope=np.ascontiguousarray(rope))


def layout(i):
    g = {k: np.asarray(v) for k, v in i.items()}
    r = lambda v: v.reshape(P, KT)
    c2 = np.stack([r(g["c"][0]), r(g["c_ctx"])], -1).reshape(P, 32)
    cw = g["ssd_conv_w"][0].T.reshape(8, P, 5).transpose(1, 0, 2).reshape(P, 40)
    cb = g["ssd_conv_b"][0].reshape(8, P).T
    bada = g["b_ada"][0]
    colp = np.concatenate([r(g["norm_mix"][0]), cw, cb, c2, r(bada[:D]), r(bada[D:2 * D])], 1)
    rowp = np.concatenate([g["ssd_a_log"][0].ravel(), g["ssd_dt_bias"][0].ravel(), g["ssd_d"][0], g["ssd_norm"][0],
                           g["gqa_q_norm"][0], g["gqa_k_norm"][0]])
    rpb = np.zeros((HEADS, 17, 127), np.float32)
    rpb[:, 1:16, 48:79] = g["na_rpb"][0]
    rpb_win = np.stack([rpb[:, :, 63 - c:127 - c] for c in range(GRID_W)])
    return dict(
        x=g["x"][0], ctx=g["ctx"][0], w_ada=g["w_ada"][0], w_in=g["w_in"][0], colp=colp, rowp=rowp, rpb_win=rpb_win,
        b_ada=bada, w_branch=g["w_branch"][0], w_out=g["w_out"][0], w_router=g["w_router"][0],
        w_gate=g["moe_w_gate"][0], w_up=g["moe_w_up"][0], w_down=g["moe_w_down"][0],
        norm_ffn=g["norm_ffn"][0], final_norm=g["final_norm"])


def kernel(**inputs):
    import concourse.bacc as bacc
    from concourse.bass_utils import run_bass_kernel_spmd

    nc = bacc.Bacc("TRN2", target_bir_lowering=False, num_devices=1)
    arrays = {f"in_{k}": np.ascontiguousarray(v) for k, v in {**layout(inputs), **constants()}.items()}
    aps = {k[3:]: nc.dram_tensor(k, v.shape, F32, kind="ExternalInput").ap() for k, v in arrays.items()}
    out = nc.dram_tensor("out", [N, D], F32, kind="ExternalOutput").ap()
    build_layer(nc, aps, out)
    r = run_bass_kernel_spmd(nc, [arrays], core_ids=[0])
    return r.results[0]["out"].reshape(1, N, D)
```

```python
from contextlib import ExitStack

import numpy as np

import concourse.bass as bass
from concourse import mybir

F32 = mybir.dt.float32
F32R = mybir.dt.float32r
ACT = mybir.ActivationFunctionType
ALU = mybir.AluOpType
AX = mybir.AxisListType

P = 128
D = 2048
N = 512
NCTX = 256
NT = N // P
NTA = (N + NCTX) // P
NA_ALL = N + NCTX
KT = D // P
GRID_W = 64
NA_R, NA_C = 8, 16
HEADS = 4
HD = 128
SH = 8
SHD = 64
BW = 512
NB = 4
E = 16
CAP = 2 * N // E
FF = D // 2
EPS = 1e-6
NEG = -1e30
SCALE = HD ** -0.5
SW = 256
SLOTS = 4

C_NAQ, C_NAK, C_NAV, C_Z, C_XBC, C_DT, C_GQ, C_GKV, C_F, C_G = (
    0, 512, 1024, 1536, 2048, 3072, 3088, 3600, 4112, 4624)

K_ID, K_ONE, K_TU, K_TL, K_MF, K_MB, K_NAM, K_IOTA, K_SEL, K_EPS, K_W = (
    0, 128, 256, 384, 512, 640, 768, 832, 896, 928, 936)
Q_NORM, Q_CW, Q_CB, Q_C, Q_BADA, Q_W = 0, 16, 56, 64, 96, 128
R_ALOG, R_DTB, R_DSK, R_SSDN, R_QG, R_KG, R_W = 0, 16, 32, 40, 552, 680, 808


class Steps:

    def __init__(self, engine, sem):
        self.engine, self.sem, self.n = engine, sem, 0

    def done(self, instruction):
        instruction.then_inc(self.sem, 1)
        self.n += 1

    def wait(self):
        self.engine.wait_ge(self.sem, self.n)


def build_layer(nc, a, out):
    with ExitStack() as ctx:
        base = (nc.sbuf_base + 63) // 64 * 64

        def at(name, offset, shape, dtype=F32):
            return nc.alloc_sbuf_tensor_at(name, shape, dtype, offset=base + offset)

        def sem(name):
            return ctx.enter_context(nc.semaphore(name))

        M_RING, M_HT, M_OT, M_YT, M_X, M_K = 0, 65536, 114688, 147456, 180224, 205120
        RING = at("ring", M_RING, [P, SLOTS, KT, SW])
        HT = at("hT", M_HT, [P, KT, N])
        HTC = at("hT_ctx", M_HT + 32768, [P, KT, NCTX])
        OT = at("oT", M_OT, [P, NB, NB, N])
        YT = at("yT", M_YT, [P, KT, N])
        CST = at("cst", M_K, [P, K_W])
        COL = at("colp", M_K + 3744, [P, Q_W])
        ROW = at("rowp", M_K + 4256, [P, R_W])
        CSIL = at("csil", M_K + 7488, [P, KT, 2])
        assert base + M_K + 7488 + 128 <= 229360
        PS = ctx.enter_context(nc.psum_tensor("ps", [P, 8, 512], F32))

        ident = CST[:, K_ID:K_ID + P]
        ones = CST[:, K_ONE:K_ONE + P]
        triu = CST[:, K_TU:K_TU + P]
        tril = CST[:, K_TL:K_TL + P]
        sel = CST[:, K_SEL:K_SEL + 32]
        eps = CST[:, K_EPS:K_EPS + 1]

        XT = at("x_tiles", M_YT, [P, 2, D])
        JUNK0 = at("junk0", M_YT + 16384, [P, D])
        CSILP = at("csil_pad", M_YT + 24576, [P, KT, 32])
        ADAROW = at("ada_row", M_OT, [P, 2 * D])
        WDT = at("w_dt", M_X + 16384, [P, KT, 32])
        SM0 = at("small0", M_X + 20480, [P, 256])
        ss0, rs0 = SM0[:, 0:NTA], SM0[:, 8:8 + NTA]
        MOD = SM0[:, 16:80].rearrange("p (v k l) -> p v k l", v=2, l=2)
        MODA = SM0[:, 80:112].rearrange("p (k l) -> p k l", l=2)

        S0 = M_OT + 16384
        XB = at("xb", S0, [P, 2, 776])
        UL = at("u_lat", S0 + 6208, [P, 8, N])
        UC = at("u_ctx", S0 + 22592, [P, 6, NCTX])
        XTOK = at("x_tok", S0 + 28736, [P, NTA, 512])
        BTOK = at("b_tok", S0 + 41024, [P, NTA, 256])
        HF = at("h_f", S0 + 47168, [P, NT, 512])
        HB = at("h_b", S0 + 55360, [P, NT, 512])
        SM = at("small_ssd", S0, [P, 12, NTA * 16])
        LSEG = at("l_seg", S0 + 63552, [P, 16, P])
        SPILL = at("spill_stage", S0 + 71744, [P, 512])
        assert S0 + 71744 + 2048 <= M_X + 24928
        DTT = at("dt_t", S0 + 63552, [P, NA_ALL])
        DATRI = at("da_tri", S0 + 6208, [P, 16, P])
        TMP = at("tmp_ssd", S0 + 22592, [P, 3, 512])
        Z = at("z", M_OT, [P, NT, 512])
        SMY = at("small_y", S0 + 6208 - 256, [P, 16])
        dtv, dts, da, ncum, tcum, ecum, etot, wx = (
            SM[:, i, :].rearrange("p (t j) -> p t j", j=16) for i in range(8))
        ex, m0, lnu, ded = (SM[:, i, :].rearrange("p (t j) -> p t j", j=16) for i in range(8, 12))
        aneg = SMY

        FT = at("f_t", M_OT + 24576, [P, 4, N])
        XCS = at("xcs", M_YT + 12288, [P, NT, 4, 256])
        DFTN = at("dft_n", M_YT + 28672, [P, NT, 2, N])
        DFTC = at("dft_c", M_YT + 45056, [P, 256])

        GQR = at("gq_raw", M_OT, [P, NT, 512])
        GKV = at("gkv_raw", M_YT, [P, NTA, 512])
        GQT = at("gq_t", M_YT + 12288, [P, HEADS, N])
        GKT = at("gk_t", M_YT + 20480, [P, 2, NA_ALL])
        SQ = at("gsq", M_OT + 16384, [P, NT, 512])
        SQK = at("gsqk", M_YT + 46080, [P, NTA, 256])
        RTQ = at("rot_q", M_YT + 46080, [P, 4, 256])
        RTK = at("rot_k", M_YT + 50176, [P, 4, 128])
        ROPE = at("rope", M_YT + 52224, [P, NT, 2, 64])
        SMG = at("small_g", M_YT + 54272, [P, 64])
        ATTG = (at("pg", M_YT + 26624, [P, 3, NA_ALL]), at("ptg", M_YT + 35840, [P, NTA, N]), at("sg", M_YT + 48128, [P, 4, 16]))
        NQT = at("nq_t", M_YT, [P, HEADS, N])
        NKT = at("nk_t", M_YT + 8192, [P, HEADS, NA_ALL])
        NV = at("n_v", M_YT + 20480, [P, NTA, 512])
        ATTN = (at("pn", M_YT + 40448, [P, 3, NA_ALL]), at("ptn", M_RING + 32768, [P, NTA, N]), at("sn", M_RING + 45056, [P, 4, 16]))
        NBIAS = at("n_bias", M_YT + 32768, [P, 2, 15, GRID_W])

        NRAW = [at("na_raw0", M_OT, [P, KT, P]), at("na_raw1", M_YT + 49472, [P, KT, P])]
        RAW = at("w_raw", M_HT + 32768, [P, 2, KT, P])
        WLO = at("w_lo", M_RING + 32768, [P, 2, KT, P], F32R)
        WHI = at("w_hi", M_RING + 49152, [P, 2, KT, P], F32R)
        WADA = at("w_ada_sb", M_X + 16384, [P, KT, P])
        HLO = at("h_lo", M_HT, [P, KT, N], F32R)
        HHI = at("h_hi", M_RING, [P, KT, N], F32R)
        OTHI = at("o_hi", M_YT, [P, NB, NB, N], F32R)
        OTLO = at("o_lo", M_OT, [P, NB, NB, N], F32R)
        WB = at("w_branch_sb", M_X, [P, 2, NB, P])
        WBLO = at("w_branch_lo", M_X, [P, 2, NB, P], F32R)
        WBHI = at("w_branch_hi", M_X + 4096, [P, 2, NB, P], F32R)
        SG = at("gate", M_X + 8192, [P, 2, N])
        YS = at("y_sum", M_X + 12288, [P, 2, N])
        ROWS2 = M_K + 4256
        ADACC = at("ada_acc", ROWS2, [P, 2, P])
        STAGE = at("ada_stage", ROWS2 + 1024, [P, 2, P])
        BROW = at("b_ada_row", ROWS2 + 2048, [P, 2, P])
        XN = at("x_new", M_HT, [P, NT, D])
        SC2 = at("scale2", M_HT + 32768, [P, D])
        SH2 = at("shift2", M_HT + 40960, [P, D])
        H2 = at("h2", M_OT, [P, NT, D])
        G1R = at("gate1_row", M_X, [P, D])
        WR = at("w_router_sb", M_X + 8192, [P, KT, 32])
        SM3 = at("small3", M_X + 10240, [P, 512])
        T3 = at("t3", M_X + 12288, [P, 2, 512])
        ORAW = at("wo_raw", M_RING, [P, 2, 8, 512])
        OLO = at("wo_lo", M_RING, [P, 2, 8, 512], F32R)
        ORAW0 = at("wo_raw0", M_HT + 32768, [P, 8, 512])
        OLO0 = at("wo_lo0", M_HT + 32768, [P, 8, 512], F32R)
        wo_raw = lambda n: ORAW[:, (n - 1) % 2, :, :] if n else ORAW0[:, :, :]
        wo_low = lambda n: OLO[:, (n - 1) % 2, :, :] if n else OLO0[:, :, :]
        OHI = at("wo_hi", M_RING + 32768, [P, 2, 8, 512], F32R)
        YHI = at("y_hi", M_OT, [P, KT, N], F32R)
        YLO = at("y_lo", M_YT, [P, KT, N], F32R)
        NF = at("norm_ffn_row", M_X + 16384, [P, D])
        JUNK3 = at("junk3", M_K + 4256, [P, 512])
        H2T = at("h2_t", M_YT, [P, KT, N])
        AT = at("aff_t", M_HT + 32768, [E, 5, N])
        M8 = at("top8", M_HT + 32768 + 10240, [E, 8, 8])
        AFF = at("aff", M_X + 22528, [P, NT, E])
        POS = at("pos", M_X + 22784, [P, NT, E])
        RING4 = at("ring4", M_YT, [P, 2, KT, SW])
        XS = at("xs", M_HT + 32768, [P, D])
        XST = at("xs_t", M_HT + 40960, [P, KT, P])
        G2R = at("gate2_row", M_X, [P, D])
        HID = at("hid", M_X + 8192, [P, FF])
        HIDT = at("hid_t", M_X + 12288, [P, FF // P, P])
        PSEL = at("p_sel", M_X + 16384, [P, NT, P])
        PG = at("p_gate", M_X + 18432, [P, NT, P])
        PGT = at("p_gate_t", M_X + 20480, [P, N])
        FN = at("final_norm_row", M_HT + 40960, [P, D])
        SM5 = at("small5", M_X + 23040, [P, 16])

        w_ada = a["w_ada"].rearrange("(p k) n -> p k n", k=KT)
        w_in = a["w_in"].rearrange("(p k) n -> p k n", k=KT)
        stream = [w_ada[:, :, n * SW:(n + 1) * SW] for n in range(2 * D // SW)]
        ADA1 = len(stream)
        chunks = [
            ("xbc", C_XBC, "T"), ("xbc2", C_XBC + 512, "T"), ("z", C_Z, "R"), ("f", C_F, "T"), ("gq", C_GQ, "R"),
            ("gkv", C_GKV, "R")]
        groups = []
        for name, c0, mode in chunks:
            load = len(stream)
            stream += [w_in[:, :, c0:c0 + SW], w_in[:, :, c0 + SW:c0 + 2 * SW]]
            if mode == "T":
                for b in range(4):
                    has_ctx = {"xbc": True, "xbc2": b < 2}.get(name, False)
                    for part in (0, 1) if has_ctx else (0,):
                        groups.append(dict(name=name, mode="T", load=load + b // 2, col=(b % 2) * P, b=b, ctx=part))
            else:
                for t in range(NTA if name == "gkv" else NT):
                    groups.append(dict(name=name, mode="R", load=load, t=t))
        for g, gr in enumerate(groups):
            gr["n"] = g
        G0 = len(groups)
        ada_read, proj_done = sem("ada_read"), sem("proj_done")

        NBLK = 12
        lat_done = lambda n: G0 + (n + 1 if n < 4 else 2 * n - 3)
        ctx_done = lambda n: G0 + 2 * n - 2
        blk_done = lambda n: lat_done(n) if n < 4 else ctx_done(n) if n < 8 else G0 + 5 + n
        nav_done = lambda t: G0 + 16 + t
        EV = [(G0 + 1) // 2, G0 // 2]
        freed = [(ada_read, n + 1) for n in range(ADA1)]
        for load in range(ADA1, len(stream)):
            users = [g["n"] + 1 for g in groups if g["load"] == load or (g["mode"] == "R" and g["load"] == load - 1)]
            freed.append((proj_done, max(users)))
        filled = [sem(f"ring_filled{s}") for s in range(SLOTS)]

        def slot_filled(eng, load):
            eng.wait_ge(filled[load % SLOTS], 16 * (load // SLOTS + 1))

        cst_in, x_in, dtw_zero = sem("cst_in"), [sem("x_in0"), sem("x_in1")], sem("dtw_zero")
        rms_ss, rms_sd, rms_rs, turned, turned_act, turned_dve = (
            sem(n) for n in ("rms_ss", "rms_sd", "rms_rs", "turned", "turned_act", "turned_dve"))
        NORM3, SS5, SD5, RS5 = NTA, NTA + 4 * NT, NTA + 1, NTA + 2
        small_in = sem("small_in")
        SMALL_DTW, SMALL_WR, SMALL_G2 = 16, 32, 48
        pads_zero, csil_set, csilp_set = sem("pads_zero"), sem("csil_set"), sem("csilp_set")
        xn_set = sem("xn_set")
        ada_evac, ada_col, mod_set, mod_lat, mod_ctx = (
            sem("ada_evac"), sem("ada_col"), sem("mod_set"), sem("mod_lat"), sem("mod_ctx"))
        arrive = sem("arrive")
        evac = [sem("evac0"), sem("evac1")]
        conv_tap, conv_done, u_set = sem("conv_tap"), sem("conv_done"), sem("u_set")
        tok_T, tok_x, tok_b = sem("tok_T"), sem("tok_x"), sem("tok_b")
        dt_ps, dt_t, dt_tok, dt_v, dt_act, dt_dve = (
            sem("dt_ps"), sem("dt_t"), sem("dt_tok"), sem("dt_v"), sem("dt_act"), sem("dt_dve"))
        cum_ps, cum_dve, cum_exp, wx_set = sem("cum_ps"), sem("cum_dve"), sem("cum_exp"), sem("wx_set")
        xw_set, st_ps, st_dve = sem("xw_set"), sem("st_ps"), sem("st_dve")
        datri_set, seg_ps, seg_dve, seg_exp, lf_set, m_dve, y_ps, y_dve, y_act, yT_ps, yT_set = (
            sem(n) for n in ("datri_set", "seg_ps", "seg_dve", "seg_exp", "lf_set", "m_dve", "y_ps", "y_dve",
                             "y_act", "yT_ps", "yT_set"))
        fc_ps, fc_set, fn_ps, fn_set = (sem(n) for n in ("fc_ps", "fc_set", "fn_ps", "fn_set"))
        spill_out, f_in, gq_in, gkv_in = (sem(n) for n in ("spill_out", "f_in", "gq_in", "gkv_in"))
        dftn_in = sem("dftn_in")
        g_dve, g_pool, g_sqk, g_ms, g_sd, g_rs, g_T, g_Tset = (
            sem(n) for n in ("g_dve", "g_pool", "g_sqk", "g_ms", "g_sd", "g_rs", "g_T", "g_Tset"))

        wb_in, brow_in, stage_out = [sem("wb_in0"), sem("wb_in1")], [sem("brow0"), sem("brow1")], [sem("st0"), sem("st1")]
        raw_in, ada_in = [sem("raw_in0"), sem("raw_in1")], sem("ada_in")
        gate_ps, gate_set, br_ps, gated, yt_add, ada_tap, ada_ps, stage_set, w_hi, w_lo, gw_lo, hh_hi, hh_lo = (
            sem(n) for n in ("gate_ps", "gate_set", "br_ps", "gated", "yt_add", "ada_tap", "ada_ps",
                             "stage_set", "w_hi", "w_lo", "gw_lo", "hh_hi", "hh_lo"))
        wb_hi, wb_lo, y_out, y_back = sem("wb_hi"), sem("wb_lo"), [sem("y_out0"), sem("y_out1")], [sem(f"y_back{k}") for k in range(4)]
        y_dram = nc.dram_tensor("y", [KT, P, N], F32).ap()
        wo_read = sem("wo_read")
        ACT_HI, ACT_LO, W_HI, W_LO = KT + NB, 4 + NB, NBLK + KT * NB, NBLK
        rows_in, out_ps, out_t, xn_add, sc2_set = (
            sem(n) for n in ("rows_in", "out_ps", "out_t", "xn_add", "sc2_set"))
        h_mul, h_set, h_set_dve = sem("h_mul"), sem("h_set"), sem("h_set_dve")
        wr_zero, r_ps, r_act, r_dve, topk, pos_set = (
            sem(n) for n in ("wr_zero", "r_ps", "r_act", "r_dve", "topk",
                             "pos_set"))
        moe_read, psel_set, pg_set, xs_ps, xs_act, xs_dve, xst_ps, xst_act, xst_dve = (
            sem(n) for n in ("moe_read", "psel_set", "pg_set", "xs_ps", "xs_act", "xs_dve", "xst_ps", "xst_act", "xst_dve"))
        silu_set, hid_set, hidT_ps, hidT_act, hidT_dve, pgt_ps, pgt_set, ye_set, sc_ps, acc_set = (
            sem(n) for n in ("silu_set", "hid_set", "hidT_ps", "hidT_act", "hidT_dve", "pgt_ps", "pgt_set", "ye_set",
                             "sc_ps", "acc_set"))
        o_set, o_out = sem("o_set"), sem("o_out")
        spilled = [g for g in groups if g["name"] in ("f", "gq", "gkv")]
        spill_dram = nc.dram_tensor("spill", [len(spilled), P, 512], F32).ap()
        ada_dram = nc.dram_tensor("ada_rest", [4 * D], F32).ap()

        before4 = [len([n for n in range(len(stream)) if n % SLOTS == s]) for s in range(SLOTS)] + [0, 0]
        filled += [sem("ring_filled4"), sem("ring_filled5")]
        ring6 = [RING[:, s, :, :] for s in range(SLOTS)] + [RING4[:, s, :, :] for s in range(2)]
        RD = 6
        NL = 24
        w_out_v = a["w_out"].rearrange("(k p) n -> p k n", p=P)

        att_scores, att_raw, att_mx, att_exp, att_stat, att_pn, att_pT, att_pT_dve, att_pT_act, att_pv, att_out = (
            sem(n) for n in ("att_scores", "att_raw", "att_mx", "att_exp", "att_stat", "att_pn", "att_pT", "att_pT_dve",
                             "att_pT_act", "att_pv", "att_out"))
        bias_in, bias_set = sem("bias_in"), sem("bias_set")

        class Attention:

            def __init__(s, q, k, v, kv_of, work, bias, o, before):
                s.q, s.k, s.v, s.kv_of, s.bias, s.o = q, k, v, kv_of, bias, o
                s.p, s.pt, s.st = work
                s.u, s.h = before * HEADS * NT, before * HEADS

        gqa = Attention(GQT, GKT, GKV, lambda h: h // 2, ATTG, None, 2, 0)
        na = Attention(NQT, NKT, NV, lambda h: h, ATTN, NBIAS, 0, 1)

        def v_block(at_, kt, h):
            kv = at_.kv_of(h)
            return GKV[:, kt, 256 + kv * HD:256 + (kv + 1) * HD] if at_ is gqa else NV[:, kt, kv * HD:(kv + 1) * HD]

        rounds = {"n": {}}

        def meet(eng, who):
            k = rounds["n"][who] = rounds["n"].get(who, 0) + 1
            eng.drain().then_inc(arrive, 1)
            eng.wait_ge(arrive, 4 * k)

        def token_cols(k, t):
            src, o = (HT, t * P) if t < NT else (HTC, (t - NT) * P)
            return src[:, k:min(k + 4, KT), o:o + P]

        proj_of = lambda *names: [g for g in groups if g["name"] in names]

        block = ctx.enter_context(nc.Block())

        @block.sync
        def _(sp):
            sp.dma_start(CST[:, :], a["cst"]).then_inc(cst_in, 16)
            sp.dma_start(COL[:, :], a["colp"]).then_inc(cst_in, 16)
            sp.dma_start(ROW[:, :], a["rowp"].partition_broadcast(P)).then_inc(cst_in, 16)
            for load, src in enumerate(stream):
                if load >= SLOTS:
                    sp.wait_ge(*freed[load - SLOTS])
                sp.dma_start(RING[:, load % SLOTS, :, :], src).then_inc(filled[load % SLOTS], 16)
            sp.wait_ge(spill_out, 16 * len(spilled))
            sp.wait_ge(arrive, 4)
            back = lambda n0, n1: spill_dram[n0:n1].rearrange("g p n -> p g n")
            sp.dma_start(DFTC[:, :], a["dft_c"]).then_inc(cst_in, 16)
            sp.dma_start(FT[:, :, :], back(0, 4)).then_inc(f_in, 16)
            sp.dma_start(ROPE[:, :, :, :], a["rope"].rearrange("p (t c n) -> p t c n", t=NT, c=2)).then_inc(gq_in, 16)
            sp.dma_start(GQR[:, :, :], back(4, 8)).then_inc(gq_in, 16)
            sp.dma_start(DFTN[:, :, :, :], a["dft_n"].rearrange("p (t c n) -> p t c n", t=NT, c=2)).then_inc(dftn_in, 16)
            sp.dma_start(GKV[:, :, :], back(8, 14)).then_inc(gkv_in, 16)
            sp.wait_ge(arrive, 8)
            for n in range(NBLK):
                if n >= 2:
                    sp.wait_ge(proj_done, blk_done(n - 2))
                if n < 8:
                    dst, src = NRAW[n % 2][:, :, :], w_in[:, :, C_NAQ + n * P:C_NAQ + (n + 1) * P]
                else:
                    dst = NRAW[n % 2][:, :, :].rearrange("p k n -> p (k n)").rearrange("p (a b) -> p a b", a=4)
                    src = w_in[:, 4 * (n - 8):4 * (n - 7), C_NAV:C_NAV + 512]
                sp.dma_start(dst, src).then_inc(raw_in[n % 2], 16)
            sp.wait_ge(arrive, 4 * 4)
            sp.sem_inc(gw_lo, 2)
            wbr = a["w_branch"].rearrange("i (k p) n -> p i k n", p=P)
            badr = a["b_ada"].rearrange("(a n) -> a n", a=1)

            with sp.Fori(0, KT // 2) as q:
                for p in range(4):
                    for k in range(2):
                        n, i, j = 8 * q + 2 * p + k, 2 * (p % 2) + k, p // 2
                        sp.wait_ge(gw_lo, n + 1)
                        sp.dma_start(RAW[:, k, :, :], w_in[:, :, bass.ds(q * (2 * P) + (C_G + i * D + j * P), P)]).then_inc(raw_in[k], 16)
                    for k in range(2):
                        n, i, j = 8 * q + 2 * p + k, 2 * (p % 2) + k, p // 2
                        sp.wait_ge(br_ps, n + 1)
                        sp.wait_ge(ada_ps, n + 1)
                        sp.dma_start(BROW[0:1, k, :], badr[:, bass.ds(n * P + 2 * D, P)]).then_inc(brow_in[k], 16)
                        sp.dma_start(WB[:, k, :, :], wbr[:, i, :, bass.ds(q * (2 * P) + j * P, P)]).then_inc(wb_in[k], 16)
                        sp.wait_ge(ada_tap, 16 * n + 16)
                        sp.dma_start(WADA[:, :, :], w_ada[:, :, bass.ds(n * P + 2 * D, P)]).then_inc(ada_in, 16)
            def load_wo(n):
                c, half = divmod(n, 2)
                sp.dma_start(wo_raw(n), w_out_v[:, 8 * half:8 * half + 8, c * 512:(c + 1) * 512]).then_inc(raw_in[n % 2], 16)

            sp.wait_ge(gw_lo, 2 + KT * NB)
            load_wo(0)
            sp.wait_ge(arrive, 4 * 6)
            for k in range(2):
                sp.wait_ge(y_out[k], 16 * (KT // 2 + 1))
            for k in range(4):
                sp.dma_start(YT[:, 4 * k:4 * k + 4, :], y_dram[4 * k:4 * k + 4].rearrange("k p n -> p k n")).then_inc(y_back[k], 16)
            load_wo(1)
            sp.dma_start(XN[:, :, :], a["x"].rearrange("(t p) d -> p t d", p=P)).then_inc(rows_in, 16)
            for n in range(2, 8):
                sp.wait_ge(wo_read, n - 1)
                load_wo(n)
                if n == 2:
                    for k in range(2):
                        sp.wait_ge(stage_out[k], 16 * 33)
                    row = lambda r: ada_dram[r * D:(r + 1) * D].partition_broadcast(P)
                    sp.dma_start(G1R[:, :], row(0)).then_inc(rows_in, 16)
                    sp.dma_start(SH2[:, :], row(1)).then_inc(rows_in, 16)
                    sp.dma_start(SC2[:, :], row(2)).then_inc(rows_in, 16)
                    sp.dma_start(NF[:, :], a["norm_ffn"].partition_broadcast(P)).then_inc(rows_in, 16)
            sp.wait_ge(out_ps, 16)
            sp.sem_inc(moe_read, SLOTS)
            wg, wu = (a[n].rearrange("e (p k) n -> p e k n", k=KT) for n in ("w_gate", "w_up"))
            wd = a["w_down"].rearrange("e (p f) n -> p e f n", f=FF // P)
            with sp.Fori(0, E // 2) as m:
                for l in range(NL):
                    pos = l % RD
                    dst = ring6[pos].rearrange("p a b -> p (a b)")
                    if l < 16:
                        g = l % 8
                        src = (wg, wu)[l // 8][:, bass.ds(2 * m, 2), 2 * g:2 * g + 2, :]
                        dst = dst.rearrange("p (e k n) -> p e k n", e=2, k=2)
                    else:
                        src = wd[:, bass.ds(2 * m, 2), l - 16, :]
                        dst = dst.rearrange("p (e n) -> p e n", e=2)
                    sp.wait_ge(moe_read, NL * m + l + 1)
                    sp.dma_start(dst, src).then_inc(filled[pos], 16)
            sp.wait_ge(moe_read, RD + NL * (E // 2 - 1) + 16)
            sp.dma_start(FN[:, :], a["final_norm"].partition_broadcast(P)).then_inc(cst_in, 16)
            for t in range(NT):
                sp.wait_ge(o_set, t + 1)
                sp.dma_start(out[t * P:(t + 1) * P, :], XN[:, t, :]).then_inc(o_out, 16)
            sp.wait_ge(o_out, 16 * NT)

        @block.tensor
        def _(pe):
            pe.wait_ge(cst_in, 48)
            for t in range(NTA):
                pe.wait_ge(xn_set, t + 1)
                if t:
                    pe.wait_ge(turned_act, 2 * t)
                    pe.wait_ge(turned_dve, 2 * t)
                for k in range(KT):
                    mm = pe.transpose(PS[:, k // 4, (k % 4) * P:(k % 4 + 1) * P], XT[:, t % 2, k::KT], ident)
                mm.then_inc(turned, 1)
            pe.wait_ge(csilp_set, 1)
            for n in range(ADA1):
                slot_filled(pe, n)
                if n >= 2:
                    pe.wait_ge(ada_evac, n - 1)
                for k in range(KT):
                    j = k % 4
                    mm = pe.matmul(PS[32 * j:32 * j + 32, 4 + n % 2, 0:SW], CSILP[:, k, :], RING[:, n % SLOTS, k, :],
                                   start=k < 4, stop=k >= KT - 4)
                mm.then_inc(ada_read, 1)
            for v in range(2):
                pe.wait_ge(ada_evac, ADA1 // 2 * (v + 1))
                for k in range(KT):
                    c = 2 * k
                    mm = pe.matmul(PS[:, 6 + v, c:c + 2], ADAROW[:, v * D + k:(v + 1) * D:KT], sel[:, 0:2],
                                   start=True, stop=True)
                mm.then_inc(ada_col, 1)

            def project(gs):
                for gr in gs:
                    g = gr["n"]
                    slot_filled(pe, gr["load"])
                    if gr["mode"] == "R":
                        slot_filled(pe, gr["load"] + 1)
                    if g >= 2:
                        pe.wait_ge(evac[g % 2], g // 2)
                    s = gr["load"] % SLOTS
                    for k in range(KT):
                        if g == 0:
                            pe.wait_ge(mod_lat, k + 1)
                        if g == 1:
                            pe.wait_ge(mod_ctx, k + 1)
                        if gr["mode"] == "T":
                            w = RING[:, s, k, gr["col"]:gr["col"] + P]
                            x = HTC[:, k, :] if gr["ctx"] else HT[:, k, :]
                            o = PS[:, g % 2, 0:NCTX] if gr["ctx"] else PS[:, g % 2, :]
                            mm = pe.matmul(o, w, x, start=k == 0, stop=k == KT - 1)
                        else:
                            o = PS[:, g % 2, :].rearrange("p (a b) -> p a b", a=2)
                            mm = pe.matmul(o, token_cols(k, gr["t"])[:, 0, :], RING[:, s:s + 2, k, :],
                                           start=k == 0, stop=k == KT - 1)
                    mm.then_inc(proj_done, 1)

            project(proj_of("xbc", "xbc2"))
            pe.wait_ge(small_in, SMALL_DTW)
            for part, (x, n) in enumerate(((HT, N), (HTC, NCTX))):
                for k in range(KT):
                    j = k % 4
                    mm = pe.matmul(PS[32 * j:32 * j + 32, 2 + part, 0:n], WDT[:, k, :], x[:, k, :],
                                   start=k < 4, stop=k >= KT - 4)
            mm.then_inc(dt_ps, 1)
            project(proj_of("z"))
            pe.wait_ge(dt_t, 2)
            for t in range(NTA):
                mm = pe.matmul(PS[:, 4, 16 * t:16 * t + 16], DTT[:, t * P:(t + 1) * P], sel[:, 0:16], start=True, stop=True)
            mm.then_inc(dt_tok, 1)
            pe.wait_ge(u_set, 14)
            for t in range(NTA):
                if t >= 2:
                    pe.wait_ge(tok_x, t - 1)
                    pe.wait_ge(tok_b, t - 1)
                src, o = (UL, t * P) if t < NT else (UC, (t - NT) * P)
                for b in range(4):
                    pe.transpose(PS[:, 2 + t % 2, b * P:(b + 1) * P], src[:, b, o:o + P], ident)
                for b in range(2):
                    mm = pe.transpose(PS[:, 6 + t % 2, b * P:(b + 1) * P], src[:, 4 + b, o:o + P], ident)
                mm.then_inc(tok_T, 1)
            project(spilled[0:1])
            pe.wait_ge(dt_dve, 7)
            pe.matmul(PS[:, 5, 0:48], triu, da[:, :, 0:8], start=True, stop=True)
            pe.matmul(PS[:, 5, 48:96], tril, da[:, :, 8:16], start=True, stop=True)
            pe.matmul(PS[:, 5, 96:192], ones, da[:, :, :], start=True, stop=True).then_inc(cum_ps, 1)
            project(spilled[1:2])
            steps = [(i, d, t) for i, ft in enumerate(zip((4, 5, 0, 1, 2), (5, 4, 3, 2, 1))) for d, t in enumerate(ft)]
            pe.wait_ge(tok_x, NTA)
            pe.wait_ge(tok_b, NTA)
            for n, (i, d, t) in enumerate(steps):
                pe.wait_ge(xw_set, n + 1)
                if i:
                    pe.wait_ge(st_dve, 2 * n - 4 if i > 1 else n - 1)
                for g in range(2):
                    mm = pe.matmul(PS[:, 2 + d, g * 256:(g + 1) * 256], BTOK[:, t, g * P:(g + 1) * P],
                                   TMP[:, d, g * 256:(g + 1) * 256], start=True, stop=True)
                mm.then_inc(st_ps, 1)
                if n % 2 and n < 8:
                    project(spilled[2 + n // 2:3 + n // 2])
            for t in range(NT):
                pe.wait_ge(datri_set, 2 * t + 2)
                if t:
                    pe.wait_ge(y_dve, 11 * t)
                    pe.wait_ge(yT_set, t)
                else:
                    pe.wait_ge(st_dve, 18)
                for j in range(4):
                    pe.matmul(PS[:, 2 + j, :], ones, DATRI[:, 4 * j:4 * j + 4, :], start=True, stop=True)
                for g in range(2):
                    mm = pe.matmul(PS[:, 7, g * P:(g + 1) * P], UL[:, 4 + g, t * P:(t + 1) * P],
                                   UL[:, 6 + g, t * P:(t + 1) * P], start=True, stop=True)
                mm.then_inc(seg_ps, 1)
                project(spilled[6 + 2 * t:7 + 2 * t])
                pe.wait_ge(seg_dve, 16 * t + 8)
                for d, h in enumerate((HF, HB)):
                    for g in range(2):
                        pe.matmul(PS[:, 2 + d, g * 256:(g + 1) * 256], UL[:, 6 + g, t * P:(t + 1) * P],
                                  h[:, t, g * 256:(g + 1) * 256], start=True, stop=True)
                pe.wait_ge(m_dve, 3 * t + 3)
                for h in range(SH):
                    mm = pe.matmul(PS[:, 6, h * SHD:(h + 1) * SHD], LSEG[:, h, :], XTOK[:, t, h * SHD:(h + 1) * SHD],
                                   start=True, stop=True)
                mm.then_inc(y_ps, 1)
                project(spilled[7 + 2 * t:8 + 2 * t])
                pe.wait_ge(y_dve, 11 * t + 11)
                for b in range(4):
                    mm = pe.transpose(PS[:, 7, b * P:(b + 1) * P], TMP[:, 0, b * P:(b + 1) * P], ident)
                mm.then_inc(yT_ps, 1)
            meet(pe, "pe")

            pe.wait_ge(f_in, 16)
            pe.wait_ge(cst_in, 64)
            for g in range(4):
                for t in range(NT):
                    n = g * NT + t
                    if n >= 2:
                        pe.wait_ge(fc_set, n - 1)
                    pe.matmul(PS[:, 2 + n % 2, 0:256], FT[:, g, t * P:(t + 1) * P], DFTC[:, :],
                              start=True, stop=True).then_inc(fc_ps, 1)
            pe.wait_ge(dftn_in, 16)
            for g in range(4):
                pe.wait_ge(fc_set, NT * (g + 1))
                if g >= 2:
                    pe.wait_ge(fn_set, g - 1)
                for t in range(NT):
                    for c in range(2):
                        mm = pe.matmul(PS[:, 4 + g % 2, :], XCS[:, t, g, c * P:(c + 1) * P], DFTN[:, t, c, :],
                                       start=t + c == 0, stop=t + c == NT)
                mm.then_inc(fn_ps, 1)

            def attend(s):
                units = [(h, t) for h in range(HEADS) for t in range(NT)]

                def values(h):
                    pe.wait_ge(att_pT_dve, s.u + NT * (h + 1))
                    pe.wait_ge(att_pT_act, s.u + NT * (h + 1))
                    if h:
                        pe.wait_ge(att_out, s.h + h)
                    for k in range(NTA):
                        mm = pe.matmul(PS[:, 6, :], v_block(s, k, h), s.pt[:, k, :], start=k == 0, stop=k == NTA - 1)
                    mm.then_inc(att_pv, 1)

                for n in range(len(units) + 2):
                    if n < len(units):
                        h, t = units[n]
                        b = 2 * (n % 2)
                        if n >= 2:
                            pe.wait_ge(att_exp, s.u + n - 1)
                        q = s.q[:, h, t * P:(t + 1) * P]
                        pe.matmul(PS[:, b, :], q, s.k[:, s.kv_of(h), 0:N], start=True, stop=True)
                        pe.matmul(PS[:, b + 1, 0:NCTX], q, s.k[:, s.kv_of(h), N:], start=True,
                                  stop=True).then_inc(att_scores, 1)
                    if n >= 2:
                        m = n - 2
                        h, t = units[m]
                        if t == 0 and h:
                            values(h - 1)
                        pe.wait_ge(att_pn, s.u + m + 1)
                        if m:
                            pe.wait_ge(att_pT_dve, s.u + m)
                            pe.wait_ge(att_pT_act, s.u + m)
                        for k in range(NTA):
                            mm = pe.transpose(PS[:, 4 + k // 4, (k % 4) * P:(k % 4 + 1) * P],
                                              s.p[:, m % 3, k * P:(k + 1) * P], ident)
                        mm.then_inc(att_pT, 1)
                values(HEADS - 1)

            pe.wait_ge(g_dve, 3 + 6 * NT)
            for h in range(HEADS):
                if h:
                    pe.wait_ge(g_Tset, h)
                for t in range(NT):
                    mm = pe.transpose(PS[:, 2, t * P:(t + 1) * P], GQR[:, t, h * HD:(h + 1) * HD], ident)
                mm.then_inc(g_T, 1)
            pe.wait_ge(g_pool, 3 + 6 * NT)
            pe.wait_ge(fn_set, 4)
            for g in range(2):
                pe.wait_ge(g_Tset, HEADS + g)
                for t in range(NTA):
                    mm = pe.transpose(PS[:, 4 + t // 4, (t % 4) * P:(t % 4 + 1) * P], GKV[:, t, g * HD:(g + 1) * HD], ident)
                mm.then_inc(g_T, 1)
            pe.wait_ge(g_Tset, HEADS + 2)
            meet(pe, "pe")
            attend(gqa)
            meet(pe, "pe")
            def products(o, hi, lo, w_hi_, w_lo_, x_moves, start, stop):
                if x_moves:
                    pe.matmul(o, w_hi_, hi, start=start, stop=False)
                    pe.matmul(o, w_hi_, lo, start=False, stop=False)
                    return pe.matmul(o, w_lo_, hi, start=False, stop=stop)
                pe.matmul(o, hi, w_hi_, start=start, stop=False)
                pe.matmul(o, hi, w_lo_, start=False, stop=False)
                return pe.matmul(o, lo, w_hi_, start=False, stop=stop)

            pe.wait_ge(hh_lo, 4)
            for n in range(8):
                b = n % 2
                pe.wait_ge(w_lo, n + 1)
                if n >= 2:
                    pe.wait_ge(evac[0], EV[0] + n - 1)
                for k in range(KT):
                    mm = products(PS[:, b, :], HHI[:, k, :], HLO[:, k, :], WHI[:, b, k, :], WLO[:, b, k, :], True,
                                  k == 0, k == KT - 1)
                mm.then_inc(proj_done, 1)
                if n >= 4:
                    if n >= 6:
                        pe.wait_ge(evac[1], EV[1] + n - 5)
                    for k in range(KT):
                        mm = pe.matmul(PS[:, 2 + b, 0:NCTX], NRAW[b][:, k, :], HTC[:, k, :], start=k == 0, stop=k == KT - 1)
                    mm.then_inc(proj_done, 1)
            pe.wait_ge(evac[1], EV[1] + 4)
            wide = lambda x: x.rearrange("p k n -> p (k n)").rearrange("p (a b) -> p a b", a=4)
            for n in range(8, NBLK):
                b = n % 2
                pe.wait_ge(w_lo, n + 1)
                raw, hi, lo = wide(NRAW[b][:, :, :]), wide(WHI[:, b, :, :]), wide(WLO[:, b, :, :])
                for t in range(NTA):
                    for k in range(4):
                        kk = 4 * (n - 8) + k
                        first, last = kk == 0, kk == KT - 1
                        if t < NT:
                            x = slice(t * P, (t + 1) * P)
                            mm = products(PS[:, 2 + t, :], HHI[:, kk, x], HLO[:, kk, x], hi[:, k, :], lo[:, k, :], False,
                                          first, last)
                        else:
                            mm = pe.matmul(PS[:, 2 + t, :], HTC[:, kk, (t - NT) * P:(t - NT + 1) * P], raw[:, k, :],
                                           start=first, stop=last)
                    if n == NBLK - 1 or t == NTA - 1:
                        mm.then_inc(proj_done, 1)
            meet(pe, "pe")
            attend(na)
            meet(pe, "pe")
            pe.sem_inc(ada_ps, 2)
            pe.sem_inc(br_ps, 2)
            with pe.Fori(0, KT // 2) as q:
                for b in range(8):
                    n, k, i = 8 * q + b, b % 2, b % 4
                    pe.wait_ge(gw_lo, n + 1 + 2)
                    pe.wait_ge(gate_set, n + 1)
                    for c in range(KT):
                        mm = products(PS[:, k, :], HHI[:, c, :], HLO[:, c, :], WHI[:, k, c, :], WLO[:, k, c, :], True,
                                      c == 0, c == KT - 1)
                    mm.then_inc(gate_ps, 1)
                    pe.wait_ge(wb_lo, n + 1)
                    if b < 4:
                        pe.wait_ge(hh_lo, 4 + 1 + i)
                    pe.wait_ge(gated, n + 1)
                    for c in range(NB):
                        mm = products(PS[:, 2 + k, :], OTHI[:, i, c, :], OTLO[:, i, c, :], WBHI[:, k, c, :],
                                      WBLO[:, k, c, :], True, c == 0, c == NB - 1)
                    mm.then_inc(br_ps, 1)
                    pe.wait_ge(ada_tap, 16 * n + 16 + 16)
                    pe.wait_ge(brow_in[k], 64 * q + 16 * (b // 2 + 1))
                    pe.wait_ge(stage_set, n + 1)
                    pe.matmul(PS[:, 4 + k, 0:P], ones, ADACC[:, k, :], start=True, stop=False)
                    pe.matmul(PS[:, 4 + k, 0:P], CST[0:1, K_ONE:K_ONE + P], BROW[0:1, k, :], start=False,
                              stop=True).then_inc(ada_ps, 1)
            meet(pe, "pe")
            for n in range(8):
                c, half = divmod(n, 2)
                pe.wait_ge(w_lo, W_LO + 2 * n + 2)
                for t in range(NT):
                    if half == 0 and c >= 2:
                        pe.wait_ge(out_t, 4 * (c - 2) + t + 1)
                    o = PS[:, 4 * (c % 2) + t, :]
                    for k in range(8):
                        kk = 8 * half + k
                        if n < 2 and t == 0 and k % 4 == 0:
                            pe.wait_ge(hh_lo, ACT_LO + kk // 4 + 1)
                        hi, lo = YHI[:, kk, t * P:(t + 1) * P], YLO[:, kk, t * P:(t + 1) * P]
                        first, last = half == 0 and k == 0, half == 1 and k == 7
                        pe.matmul(o, hi, OHI[:, n % 2, k, :], start=first, stop=False)
                        pe.matmul(o, hi, wo_low(n)[:, k, :], start=False, stop=False)
                        mm = pe.matmul(o, lo, OHI[:, n % 2, k, :], start=False, stop=last)
                    if half == 1:
                        mm.then_inc(out_ps, 1)
                pe.drain().then_inc(wo_read, 1)
            for t in range(NT):
                pe.wait_ge(h_set_dve if t % 2 else h_set, t // 2 + 1)
                if t:
                    pe.wait_ge(turned_act, 2 * NTA + 2 * t)
                    pe.wait_ge(turned_dve, 2 * NTA + 2 * t)
                else:
                    pe.wait_ge(out_t, 16)
                for k in range(KT):
                    mm = pe.transpose(PS[:, k // 4, (k % 4) * P:(k % 4 + 1) * P], H2[:, t, k::KT], ident)
                mm.then_inc(turned, 1)
            pe.wait_ge(turned_act, 2 * NTA + 2 * NT)
            pe.wait_ge(turned_dve, 2 * NTA + 2 * NT)
            pe.wait_ge(small_in, SMALL_WR)
            for k in range(KT):
                j = k % 4
                mm = pe.matmul(PS[32 * j:32 * j + 32, 4, :], WR[:, k, :], H2T[:, k, :], start=k < 4, stop=k >= KT - 4)
            mm.then_inc(r_ps, 1)
            pe.wait_ge(r_act, 1)
            for t in range(NT):
                mm = pe.matmul(PS[:, 5, E * t:E * (t + 1)], T3[:, 0, t * P:(t + 1) * P], sel[:, 0:E], start=True, stop=True)
            mm.then_inc(r_ps, 1)
            pe.drain().then_inc(moe_read, RD - SLOTS)
            pe.wait_ge(r_dve, 4)
            for t in range(NT):
                mm = pe.transpose(PS[0:E, 6, t * P:(t + 1) * P], AFF[:, t, :], ident)
            mm.then_inc(r_ps, 1)
            pe.wait_ge(topk, 21)
            for t in range(NT):
                mm = pe.transpose(PS[:, 7, E * t:E * (t + 1)], AT[:, 4, t * P:(t + 1) * P], ident[0:E, 0:E])
            mm.then_inc(r_ps, 1)
            meet(pe, "pe")

            def gather(m):
                pe.wait_ge(psel_set, m + 1)
                for c in range(4):
                    for t in range(NT):
                        mm = pe.matmul(PS[:, 4 + c, :], PSEL[:, t, :], H2[:, t, c * 512:(c + 1) * 512], start=t == 0, stop=t == NT - 1)
                    mm.then_inc(xs_ps, 1)

            def turn_rows(m):
                pe.wait_ge(xs_act, 2 * m + 2)
                pe.wait_ge(xs_dve, 2 * m + 2)
                for k in range(KT):
                    mm = pe.transpose(PS[:, k // 4, (k % 4) * P:(k % 4 + 1) * P], XS[:, k::KT], ident)
                    if k % 4 == 3:
                        mm.then_inc(xst_ps, 1)

            def expert_pair(m, last):
                pe.wait_ge(xst_act, 2 * m + 2)
                pe.wait_ge(xst_dve, 2 * m + 2)
                pe.wait_ge(ye_set, 4 * m + 4)
                for l in range(16):
                    pos = l % RD
                    pe.wait_ge(filled[pos], 16 * (NL // RD) * m + 16 * (before4[pos] + l // RD + 1))
                    w = ring6[pos].rearrange("p a b -> p (a b)").rearrange("p (e k n) -> p e k n", e=2, k=2)
                    for kk in range(2):
                        k = 2 * (l % 8) + kk
                        for half in range(2):
                            for e in range(2):
                                mm = pe.matmul(PS[64 * e:64 * e + 64, 2 * (l // 8) + half, :], XST[:, k, 64 * e:64 * e + 64],
                                               w[:, e, kk, half * 512:(half + 1) * 512], start=k == 0, stop=k == KT - 1)
                    mm.then_inc(moe_read, 1)
                if not last:
                    pe.wait_ge(acc_set, 16 * m + 16)
                    gather(m + 1)
                pe.wait_ge(hid_set, m + 1)
                if not last:
                    turn_rows(m + 1)
                else:
                    pe.wait_ge(acc_set, 16 * m + 16)
                for f in range(FF // P):
                    mm = pe.transpose(PS[:, 4 + f // 4, (f % 4) * P:(f % 4 + 1) * P], HID[:, f::FF // P], ident)
                    if f % 4 == 3:
                        mm.then_inc(hidT_ps, 1)
                pe.wait_ge(pg_set, m + 1)
                for t in range(NT):
                    mm = pe.transpose(PS[:, 6, t * P:(t + 1) * P], PG[:, t, :], ident)
                mm.then_inc(pgt_ps, 1)
                pe.wait_ge(hidT_act, m + 1)
                pe.wait_ge(hidT_dve, m + 1)
                if not last:
                    pe.wait_ge(xst_act, 2 * m + 4)
                    pe.wait_ge(xst_dve, 2 * m + 4)
                for l in range(16, NL):
                    pos, f = l % RD, l - 16
                    pe.wait_ge(filled[pos], 16 * (NL // RD) * m + 16 * (before4[pos] + l // RD + 1))
                    w = ring6[pos].rearrange("p a b -> p (a b)").rearrange("p (e n) -> p e n", e=2)
                    for c in range(4):
                        for e in range(2):
                            mm = pe.matmul(PS[64 * e:64 * e + 64, c, :], HIDT[:, f, 64 * e:64 * e + 64],
                                           w[:, e, c * 512:(c + 1) * 512], start=f == 0, stop=f == FF // P - 1)
                    mm.then_inc(moe_read, 1)
                pe.wait_ge(pgt_set, m + 1)
                pe.wait_ge(ye_set, 4 * m + 8)
                for g in range(16):
                    t, c = divmod(g, 4)
                    if g >= 4:
                        pe.wait_ge(acc_set, 16 * m + g + 13)
                    pe.matmul(PS[:, 4 + g % 4, :], PGT[:, t * P:(t + 1) * P], XS[:, c * 512:(c + 1) * 512], start=True,
                              stop=True).then_inc(sc_ps, 1)

            gather(0)
            turn_rows(0)
            with pe.Fori(0, E // 2 - 1) as m:
                expert_pair(m, False)
            expert_pair(E // 2 - 1, True)

        @block.scalar
        def _(act):
            act.wait_ge(cst_in, 48)
            act.activation(CSIL[:, :, :], COL[:, Q_C:Q_C + 32].rearrange("p (k v) -> p k v", v=2), ACT.Silu).then_inc(csil_set, 1)
            act.wait_ge(csil_set, 1)
            act.wait_ge(pads_zero, 1)
            act.copy(CSILP[:, :, 0:2], CSIL[:, :, :]).then_inc(csilp_set, 1)
            for t in range(NTA):
                act.wait_ge(x_in[t % 2], 16 * (t // 2 + 1))
                act.activation(JUNK0[:, :], XT[:, t % 2, :], ACT.Square, accum_out=ss0[:, t:t + 1]).then_inc(rms_ss, 1)
                act.wait_ge(rms_ss, t + 1)
                act.activation(rs0[:, t:t + 1], ss0[:, t:t + 1], ACT.Sqrt, bias=eps, scale=1.0 / D).then_inc(rms_sd, 1)
                act.wait_ge(turned, t + 1)
                for q in range(2):
                    act.copy(token_cols(4 * q, t),
                             PS[:, q, :].rearrange("p (a b) -> p a b", a=4)).then_inc(turned_act, 1)
            for n in range(ADA1):
                act.wait_ge(ada_read, n + 1)
                act.copy(ADAROW[:, n * SW:(n + 1) * SW], PS[:, 4 + n % 2, 0:SW]).then_inc(ada_evac, 1)
            act.wait_ge(mod_set, 4)
            for k in range(KT):
                act.activation(HTC[:, k, :], HTC[:, k, :], ACT.Identity, bias=MOD[:, 0, k, 1:2],
                               scale=MODA[:, k, 1:2]).then_inc(mod_ctx, 1)

            act.wait_ge(pads_zero, 2)
            pieces = proj_of("xbc", "xbc2")

            def conv_silu(n):
                gr = pieces[n]
                b = gr["b"] + (4 if gr["name"] == "xbc2" else 0)
                u = UC[:, b, :] if gr["ctx"] else UL[:, b, :]
                act.wait_ge(conv_done, n + 1)
                act.activation(u, u, ACT.Silu).then_inc(u_set, 1)

            for n, gr in enumerate(pieces):
                act.wait_ge(proj_done, gr["n"] + 1)
                if n >= 2:
                    act.wait_ge(conv_done, n - 1)
                w, o = (NCTX, 518) if gr["ctx"] else (N, 2)
                src = PS[:, gr["n"] % 2, 0:w]
                act.copy(XB[:, n % 2, o:o + w], src).then_inc(evac[gr["n"] % 2], 1)
                if n:
                    conv_silu(n - 1)
            conv_silu(len(pieces) - 1)
            act.wait_ge(dt_ps, 1)
            act.copy(DTT[:, 0:N], PS[:, 2, :]).then_inc(dt_t, 1)
            act.copy(DTT[:, N:], PS[:, 3, 0:NCTX]).then_inc(dt_t, 1)
            for gr in proj_of("z"):
                act.wait_ge(proj_done, gr["n"] + 1)
                act.activation(Z[:, gr["t"], :], PS[:, gr["n"] % 2, :], ACT.Silu).then_inc(evac[gr["n"] % 2], 1)
            for t in range(NTA):
                act.wait_ge(tok_T, t + 1)
                act.copy(BTOK[:, t, :], PS[:, 6 + t % 2, 0:256]).then_inc(tok_b, 1)
            def spill(n):
                gr = spilled[n]
                act.wait_ge(proj_done, gr["n"] + 1)
                if n:
                    act.wait_ge(spill_out, 16 * n)
                act.copy(SPILL[:, :], PS[:, gr["n"] % 2, :]).then_inc(evac[gr["n"] % 2], 1)
                act.wait_ge(evac[gr["n"] % 2], gr["n"] // 2 + 1)
                act.dma_start(spill_dram[n], SPILL[:, :]).then_inc(spill_out, 16)

            act.activation(aneg[:, :], ROW[:, R_ALOG:R_ALOG + 16], ACT.Exp).then_inc(dt_act, 1)
            act.wait_ge(dt_v, 1)
            act.activation(m0, dtv, ACT.Abs).then_inc(dt_act, 1)
            act.wait_ge(dt_act, 2)
            act.activation(ex, m0, ACT.Exp, scale=-1.0).then_inc(dt_act, 1)
            act.wait_ge(dt_act, 3)
            act.activation(lnu, ex, ACT.Ln, bias=CST[:, K_ONE:K_ONE + 1]).then_inc(dt_act, 1)
            spill(0)
            act.wait_ge(cum_dve, 1)
            act.activation(ecum, ncum, ACT.Exp, scale=-1.0).then_inc(cum_exp, 1)
            act.wait_ge(cum_dve, 2)
            act.activation(etot, PS[:, 5, 96:192].rearrange("p (t j) -> p t j", j=16), ACT.Exp).then_inc(cum_exp, 1)
            act.activation(tcum, tcum, ACT.Exp).then_inc(cum_exp, 1)
            for n in range(1, 6):
                spill(n)
            for t in range(NT):
                act.wait_ge(seg_dve, 16 * t + 8)
                act.activation(LSEG[:, 0:8, :], LSEG[:, 0:8, :], ACT.Exp).then_inc(seg_exp, 1)
                act.wait_ge(seg_dve, 16 * t + 16)
                act.activation(LSEG[:, 8:16, :], LSEG[:, 8:16, :], ACT.Exp).then_inc(seg_exp, 1)
                spill(6 + 2 * t)
                act.wait_ge(y_dve, 11 * t + 7)
                for g in range(2):
                    act.activation(TMP[:, 2, g * 256:(g + 1) * 256], TMP[:, 0, g * 256:(g + 1) * 256], ACT.Square,
                                   accum_out=ex[:, t, g:g + 1]).then_inc(y_act, 1)
                act.wait_ge(y_act, 3 * t + 2)
                act.activation(m0[:, t, 0:2], ex[:, t, 0:2], ACT.Sqrt, bias=eps, scale=1.0 / 256).then_inc(y_act, 1)
                spill(7 + 2 * t)
                if t == 0:
                    act.wait_ge(proj_done, spilled[7]["n"] + 1)
                for k in range(4 * t, 4 * t + 4) if t < NT - 1 else ():
                    act.copy(HHI[:, k, :], HT[:, k, :]).then_inc(hh_hi, 1)
            meet(act, "act")
            for k in range(4 * NT - 4, KT):
                act.copy(HHI[:, k, :], HT[:, k, :]).then_inc(hh_hi, 1)

            for n in range(1, 16, 2):
                act.wait_ge(fc_ps, n + 1)
                act.wait_ge(fc_set, n)
                act.copy(XCS[:, n % NT, n // NT, :], PS[:, 2 + n % 2, 0:256]).then_inc(fc_set, 1)
            act.wait_ge(g_ms, 2)
            act.activation(SMG[:, 32:60], SMG[:, 0:28], ACT.Sqrt, bias=eps, scale=1.0 / HD).then_inc(g_sd, 1)
            for g in range(4):
                act.wait_ge(fn_ps, g + 1)
                act.copy(OT[:, 3, g, :], PS[:, 4 + g % 2, :]).then_inc(fn_set, 1)
            for g in range(2):
                act.wait_ge(g_T, HEADS + g + 1)
                act.copy(GKT[:, g, :], PS[:, 4:6, :].rearrange("p a b -> p (a b)")[:, 0:NA_ALL]).then_inc(g_Tset, 1)
            meet(act, "act")

            def attend(s):
                def head_out(h):
                    act.wait_ge(att_pv, s.h + h + 1)
                    act.copy(OT[:, s.o, h, :], PS[:, 6, :]).then_inc(att_out, 1)

                for n in range(HEADS * NT + 2):
                    if n < HEADS * NT:
                        act.wait_ge(att_mx, s.u + n + 1)
                        pr = s.p[:, n % 3, :]
                        if s.bias is None:
                            if n >= 3:
                                act.wait_ge(att_pT, s.u + n - 2)
                            src = PS[:, 2 * (n % 2):2 * (n % 2) + 2, :].rearrange("p a b -> p (a b)")[:, 0:NA_ALL]
                            sc = SCALE
                        else:
                            src, sc = pr, 1.0
                        act.activation(pr, src, ACT.Exp, bias=s.st[:, 1, n:n + 1], scale=sc,
                                       accum_out=s.st[:, 2, n:n + 1]).then_inc(att_exp, 1)
                    if n >= 2:
                        m = n - 2
                        h, t = divmod(m, NT)
                        if t == 0 and h:
                            head_out(h - 1)
                        act.wait_ge(att_pT, s.u + m + 1)
                        act.copy(s.pt[:, 4:6, t * P:(t + 1) * P],
                                 PS[:, 5, 0:256].rearrange("p (a b) -> p a b", a=2)).then_inc(att_pT_act, 1)
                head_out(HEADS - 1)

            attend(gqa)
            meet(act, "act")
            for n in range(8):
                act.wait_ge(proj_done, lat_done(n))
                dst = NQT[:, n, :] if n < 4 else NKT[:, n - 4, 0:N]
                act.copy(dst, PS[:, n % 2, :]).then_inc(evac[0], 1)
            for t in range(0, NTA, 2):
                act.wait_ge(proj_done, nav_done(t))
                act.copy(NV[:, t, :], PS[:, 2 + t, :]).then_inc(evac[0], 1)
            meet(act, "act")
            attend(na)
            meet(act, "act")
            act.sem_inc(gate_set, 2)
            act.sem_inc(stage_set, 2)
            for k in range(2):
                act.sem_inc(stage_out[k], 16)
                act.sem_inc(y_out[k], 16)
            for i in range(NB):
                act.copy(OTHI[:, i, :, :], OT[:, i, :, :]).then_inc(hh_hi, 1)
            with act.Fori(0, KT // 2) as q:
                for b in range(8):
                    n, k = 8 * q + b, b % 2
                    act.wait_ge(wb_in[k], 64 * q + 16 * (b // 2 + 1))
                    act.wait_ge(br_ps, n + 1)
                    act.copy(WBHI[:, k, :, :], WB[:, k, :, :]).then_inc(wb_hi, 1)
                    act.wait_ge(gate_ps, n + 1)
                    act.wait_ge(yt_add, n + 1)
                    act.activation(SG[:, k, :], PS[:, k, :], ACT.Sigmoid).then_inc(gate_set, 1)
                    act.wait_ge(ada_ps, n + 1 + 2)
                    act.wait_ge(stage_out[k], 64 * q + 16 * (b // 2 + 1))
                    act.copy(STAGE[0:1, k, :], PS[0:1, 4 + k, 0:P]).then_inc(stage_set, 1)
                    act.wait_ge(stage_set, n + 1 + 2)
                    act.dma_start(ada_dram.rearrange("(a n) -> a n", a=1)[:, bass.ds(n * P, P)],
                                  STAGE[0:1, k, :]).then_inc(stage_out[k], 16)
                    if b % 4 == 3:
                        j = b // 4
                        act.wait_ge(yt_add, n + 1 + 2)
                        act.dma_start(y_dram[bass.ds(2 * q + j, 1), :, :].rearrange("a p n -> p (a n)"),
                                      YS[:, j, :]).then_inc(y_out[j], 16)
            meet(act, "act")
            def squares(c):
                for t in range(NT):
                    act.wait_ge(xn_add, 4 * c + t + 1)
                    act.wait_ge(rms_ss, NORM3 + 4 * c + t)
                    act.activation(JUNK3[:, :], XN[:, t, c * 512:(c + 1) * 512], ACT.Square,
                                   accum_out=SM3[:, 32 + 4 * t + c:33 + 4 * t + c]).then_inc(rms_ss, 1)

            for n in range(8):
                act.wait_ge(raw_in[n % 2], 16 * (NBLK // 2 + 32 + n // 2 + 1))
                if n >= 2:
                    act.wait_ge(wo_read, n - 1)
                for h in range(2):
                    act.copy(OHI[:, n % 2, 4 * h:4 * h + 4, :], wo_raw(n)[:, 4 * h:4 * h + 4, :]).then_inc(w_hi, 1)
                if n < 2:
                    for k in (2 * n, 2 * n + 1):
                        act.wait_ge(y_back[k], 16)
                        act.copy(YHI[:, 4 * k:4 * k + 4, :], YT[:, 4 * k:4 * k + 4, :]).then_inc(hh_hi, 1)
                if n >= 3 and n % 2:
                    squares((n - 3) // 2)
            squares(3)
            act.wait_ge(rms_rs, NORM3 + 1)
            act.activation(SM3[:, 4:8], SM3[:, 0:4], ACT.Sqrt, bias=eps, scale=1.0 / D).then_inc(rms_sd, 1)
            for t in range(NT):
                act.wait_ge(turned, NTA + t + 1)
                for q in range(2):
                    act.copy(H2T[:, 4 * q:4 * q + 4, t * P:(t + 1) * P],
                             PS[:, q, :].rearrange("p (a b) -> p a b", a=4)).then_inc(turned_act, 1)
            act.wait_ge(r_ps, 1)
            act.copy(T3[:, 0, :], PS[:, 4, :]).then_inc(r_act, 1)
            act.wait_ge(r_dve, 2)
            act.activation(SM3[:, 64:128], SM3[:, 64:128], ACT.Exp).then_inc(r_act, 1)
            meet(act, "act")

            def rows(m):
                for c in range(2):
                    act.wait_ge(xs_ps, 4 * m + c + 1)
                    act.copy(XS[:, c * 512:(c + 1) * 512], PS[:, 4 + c, :]).then_inc(xs_act, 1)
                for q in range(2):
                    act.wait_ge(xst_ps, 4 * m + q + 1)
                    act.copy(XST[:, 4 * q:4 * q + 4, :], PS[:, q, :].rearrange("p (a b) -> p a b", a=4)).then_inc(xst_act, 1)

            def expert_pair(m, last):
                act.wait_ge(moe_read, NL * m + RD + 8)
                act.activation(HID[:, :].rearrange("p (a b) -> p a b", a=2), PS[:, 0:2, :], ACT.Silu).then_inc(silu_set, 1)
                if not last:
                    rows(m + 1)
                act.wait_ge(hidT_ps, 2 * m + 1)
                act.copy(HIDT[:, 0:4, :], PS[:, 4, :].rearrange("p (a b) -> p a b", a=4)).then_inc(hidT_act, 1)

            rows(0)
            with act.Fori(0, E // 2 - 1) as m:
                expert_pair(m, False)
            expert_pair(E // 2 - 1, True)
            for t in range(NT):
                act.wait_ge(acc_set, 16 * (E // 2) + 4 * t + 4)
                act.activation(H2[:, t, :], XN[:, t, :], ACT.Square, accum_out=SM5[:, t:t + 1]).then_inc(rms_ss, 1)
                act.wait_ge(rms_ss, SS5 + t + 1)
                act.activation(SM5[:, 4 + t:5 + t], SM5[:, t:t + 1], ACT.Sqrt, bias=eps, scale=1.0 / D).then_inc(rms_sd, 1)

        @block.vector
        def _(dve):
            tt, ts, stt = dve.tensor_tensor, dve.tensor_scalar, dve.scalar_tensor_tensor
            dve.wait_ge(cst_in, 48)
            for t in range(NTA):
                dve.wait_ge(rms_sd, t + 1)
                dve.reciprocal(rs0[:, t:t + 1], rs0[:, t:t + 1]).then_inc(rms_rs, 1)
                dve.wait_ge(rms_rs, t + 1)
                ts(XT[:, t % 2, :], XT[:, t % 2, :], rs0[:, t:t + 1], None, ALU.mult).then_inc(xn_set, 1)
                dve.wait_ge(turned, t + 1)
                for q in range(2, 4):
                    dve.tensor_copy(token_cols(4 * q, t),
                                    PS[:, q, :].rearrange("p (a b) -> p a b", a=4)).then_inc(turned_dve, 1)
            m = Steps(dve, mod_set)
            for v in range(2):
                dve.wait_ge(ada_col, v + 1)
                b = COL[:, Q_BADA + v * KT:Q_BADA + (v + 1) * KT].unsqueeze(2).to_broadcast([P, KT, 2])
                m.done(tt(MOD[:, v, :, :], PS[:, 6 + v, 0:32].rearrange("p (k l) -> p k l", l=2), b, ALU.add))
            m.wait()
            m.done(ts(MODA, MOD[:, 1, :, :], 1.0, None, ALU.add))
            m.wait()
            m.done(tt(MODA, MODA, COL[:, Q_NORM:Q_NORM + KT].unsqueeze(2).to_broadcast([P, KT, 2]), ALU.mult))
            m.wait()
            dve.wait_ge(turned_act, 2 * NTA)
            for k in range(KT):
                ts(HT[:, k, 0:N], HT[:, k, 0:N], MODA[:, k, 0:1], MOD[:, 0, k, 0:1], ALU.mult, ALU.add).then_inc(mod_lat, 1)

            pieces = proj_of("xbc", "xbc2")
            taps = Steps(dve, conv_tap)
            for n, gr in enumerate(pieces):
                b = gr["b"] + (4 if gr["name"] == "xbc2" else 0)
                dve.wait_ge(evac[gr["n"] % 2], gr["n"] // 2 + 1)
                w, o = (NCTX, 516) if gr["ctx"] else (N, 0)
                u = UC[:, b, :] if gr["ctx"] else UL[:, b, :]
                for tap in range(5):
                    wcol = COL[:, Q_CW + 5 * b + tap:Q_CW + 5 * b + tap + 1]
                    src = XB[:, n % 2, o + tap:o + tap + w]
                    if tap == 0:
                        taps.done(ts(u, src, wcol, COL[:, Q_CB + b:Q_CB + b + 1], ALU.mult, ALU.add))
                    else:
                        taps.wait()
                        ins = stt(u, src, wcol, u, ALU.mult, ALU.add)
                        if tap < 4:
                            taps.done(ins)
                        else:
                            ins.then_inc(conv_done, 1)
            for t in range(NTA):
                dve.wait_ge(tok_T, t + 1)
                dve.tensor_copy(XTOK[:, t, :], PS[:, 2 + t % 2, :]).then_inc(tok_x, 1)
            dve.wait_ge(dt_tok, 1)
            bc = lambda row: row.unsqueeze(1).to_broadcast([P, NTA, 16])
            tt(dtv, PS[:, 4, 0:96].rearrange("p (t j) -> p t j", j=16), bc(ROW[:, R_DTB:R_DTB + 16]), ALU.add).then_inc(dt_v, 1)
            q = Steps(dve, dt_dve)
            dve.wait_ge(dt_v, 1)
            q.done(ts(dts, dtv, 0.0, None, ALU.max))
            dve.wait_ge(dt_act, 3)
            q.done(ts(ded, ex, 1.0, -1.0, ALU.add, ALU.add))
            q.wait()
            q.done(tt(ded, ex, ded, ALU.subtract))
            dve.wait_ge(dt_act, 4)
            q.done(tt(dts, dts, lnu, ALU.add))
            q.wait()
            q.done(tt(dts, dts, ded, ALU.add))
            q.wait()
            q.done(tt(da, dts, bc(aneg[:, :]), ALU.mult))
            q.wait()
            q.done(ts(da, da, -1.0, None, ALU.mult))
            dve.wait_ge(cum_ps, 1)
            ts(ncum[:, :, 0:8], PS[:, 5, 0:48].rearrange("p (t j) -> p t j", j=8), -1.0, None, ALU.mult)
            ts(ncum[:, :, 8:16], PS[:, 5, 48:96].rearrange("p (t j) -> p t j", j=8), -1.0, None, ALU.mult).then_inc(cum_dve, 1)
            dve.wait_ge(cum_dve, 1)
            tt(tcum, PS[:, 5, 96:192].rearrange("p (t j) -> p t j", j=16), ncum, ALU.add).then_inc(cum_dve, 1)
            dve.wait_ge(cum_exp, 3)
            tt(wx, tcum, dts, ALU.mult).then_inc(wx_set, 1)
            store = {0: (3, 0, 1, 2, 3), 1: (0, 3, 2, 1, 0)}
            steps = [(i, d, t) for i, ft in enumerate(zip((4, 5, 0, 1, 2), (5, 4, 3, 2, 1))) for d, t in enumerate(ft)]
            st = Steps(dve, st_dve)
            v3 = lambda ap: ap.rearrange("p (h c) -> p h c", c=SHD)
            for n, (i, d, t) in enumerate(steps):
                hbuf = (HF, HB)[d]
                new = hbuf[:, store[d][i], :]
                dve.wait_ge(st_ps, n + 1)
                if i == 0:
                    st.done(dve.tensor_copy(new, PS[:, 2 + d, :]))
                else:
                    old = hbuf[:, store[d][i - 1], :]
                    st.wait()
                    st.done(tt(v3(new), v3(old), etot[:, t, 8 * d:8 * d + 8].unsqueeze(2).to_broadcast([P, SH, SHD]), ALU.mult))
                    st.wait()
                    st.done(tt(new, new, PS[:, 2 + d, :], ALU.add))
            assert st.n == 18
            sg, mm_, yy = Steps(dve, seg_dve), Steps(dve, m_dve), Steps(dve, y_dve)
            for t in range(NT):
                dve.wait_ge(seg_ps, t + 1)
                if t:
                    dve.wait_ge(y_ps, t)
                for j in range(16):
                    mask = CST[:, K_MF:K_MF + P] if j < 8 else CST[:, K_MB:K_MB + P]
                    sg.done(stt(LSEG[:, j, :], PS[:, 2 + j // 4, (j % 4) * P:(j % 4 + 1) * P], ncum[:, t, j:j + 1], mask,
                                ALU.add, ALU.add))
                dve.wait_ge(seg_exp, 2 * t + 2)
                bj = lambda x, d: x[:, t, 8 * d:8 * d + 8].unsqueeze(2)
                mm_.done(tt(LSEG[:, 8:16, :], LSEG[:, 8:16, :], bj(dts, 1).to_broadcast([P, SH, P]), ALU.mult))
                mm_.wait()
                dve.wait_ge(lf_set, t + 1)
                mm_.done(tt(LSEG[:, 0:8, :], LSEG[:, 0:8, :], LSEG[:, 8:16, :], ALU.add))
                mm_.wait()
                mm_.done(tt(LSEG[:, 0:8, :].rearrange("p (g e) l -> p g e l", g=2),
                            LSEG[:, 0:8, :].rearrange("p (g e) l -> p g e l", g=2),
                            PS[:, 7, 0:256].rearrange("p (g l) -> p g l", g=2).unsqueeze(2).to_broadcast([P, 2, 4, P]), ALU.mult))
                dve.wait_ge(y_ps, t + 1)
                if t:
                    dve.wait_ge(yT_ps, t)
                T0, T1 = TMP[:, 0, :], TMP[:, 1, :]
                yy.done(tt(v3(T0), v3(PS[:, 2, :]), bj(ecum, 0).to_broadcast([P, SH, SHD]), ALU.mult))
                yy.done(tt(v3(T1), v3(PS[:, 3, :]), bj(ecum, 1).to_broadcast([P, SH, SHD]), ALU.mult))
                yy.wait()
                yy.done(tt(T0, T0, T1, ALU.add))
                yy.wait()
                yy.done(tt(T0, T0, PS[:, 6, :], ALU.add))
                yy.done(tt(v3(T1), v3(XTOK[:, t, :]), ROW[:, R_DSK:R_DSK + SH].unsqueeze(2).to_broadcast([P, SH, SHD]), ALU.mult))
                yy.wait()
                yy.done(tt(T0, T0, T1, ALU.add))
                yy.wait()
                yy.done(tt(T0, T0, Z[:, t, :], ALU.mult))
                dve.wait_ge(y_act, 3 * t + 3)
                yy.done(dve.reciprocal(m0[:, t, 2:4], m0[:, t, 0:2]))
                yy.wait()
                for g in range(2):
                    yy.done(ts(TMP[:, 0, g * 256:(g + 1) * 256], TMP[:, 0, g * 256:(g + 1) * 256], m0[:, t, 2 + g:3 + g], None, ALU.mult))
                yy.wait()
                yy.done(tt(T0, T0, ROW[:, R_SSDN:R_SSDN + 512], ALU.mult))
                assert yy.n == 11 * (t + 1)
                dve.wait_ge(yT_ps, t + 1)
                dve.tensor_copy(OT[:, 1, :, t * P:(t + 1) * P], PS[:, 7, :].rearrange("p (a b) -> p a b", a=4)).then_inc(yT_set, 1)
            meet(dve, "dve")

            for n in range(0, 16, 2):
                dve.wait_ge(fc_ps, n + 1)
                if n:
                    dve.wait_ge(fc_set, n)
                dve.tensor_copy(XCS[:, n % NT, n // NT, :], PS[:, 2, 0:256]).then_inc(fc_set, 1)

            dve.wait_ge(gq_in, 32)
            v = Steps(dve, g_dve)
            q16 = lambda ap: ap.rearrange("p t (h c) -> p (t h) c", c=HD)
            v.done(tt(SQ[:, :, :], GQR[:, :, :], GQR[:, :, :], ALU.mult))
            v.wait()
            dve.tensor_reduce(SMG[:, 0:16], q16(SQ[:, :, :]), AX.X, ALU.add).then_inc(g_ms, 1)
            dve.wait_ge(g_sqk, 1)
            dve.tensor_reduce(SMG[:, 16:28], q16(SQK[:, :, :]), AX.X, ALU.add).then_inc(g_ms, 1)
            dve.wait_ge(g_sd, 1)
            dve.reciprocal(SMG[:, 32:60], SMG[:, 32:60]).then_inc(g_rs, 1)
            dve.wait_ge(g_rs, 1)
            v.done(tt(q16(GQR[:, :, :]), q16(GQR[:, :, :]), SMG[:, 32:48].unsqueeze(2).to_broadcast([P, 16, HD]), ALU.mult))
            v.wait()
            v.done(tt(q16(GQR[:, :, :]), q16(GQR[:, :, :]), ROW[:, R_QG:R_QG + HD].unsqueeze(1).to_broadcast([P, 16, HD]), ALU.mult))
            v.wait()
            rotate(v, tt, GQR, RTQ, ROPE, HEADS)
            for h in range(HEADS):
                dve.wait_ge(g_T, h + 1)
                dve.tensor_copy(GQT[:, h, :], PS[:, 2, :]).then_inc(g_Tset, 1)
            meet(dve, "dve")

            def attend(s):
                units = HEADS * NT
                stat = Steps(dve, att_stat)
                stat.n = 2 * s.u
                for n in range(units + 2):
                    if n < units:
                        h, t = divmod(n, NT)
                        dve.wait_ge(att_scores, s.u + n + 1)
                        src = PS[:, 2 * (n % 2):2 * (n % 2) + 2, :].rearrange("p a b -> p (a b)")
                        if s.bias is not None:
                            if n >= 3:
                                dve.wait_ge(att_pT, s.u + n - 2)
                            if t == 0:
                                dve.wait_ge(bias_set, h + 1)
                            pr = s.p[:, n % 3, :]
                            u0 = 7 - 2 * t
                            stt(pr[:, 0:N], src[:, 0:N], SCALE, NBIAS[:, h % 2, u0:u0 + 8, :].rearrange("p a b -> p (a b)"),
                                ALU.mult, ALU.add)
                            ts(pr[:, N:], src[:, N:NA_ALL], SCALE, None, ALU.mult).then_inc(att_raw, 1)
                            dve.wait_ge(att_raw, n + 1)
                            src, sc = pr, 1.0
                        else:
                            src, sc = src[:, 0:NA_ALL], SCALE
                        st0, st1 = s.st[:, 0, n:n + 1], s.st[:, 1, n:n + 1]
                        stat.done(dve.tensor_reduce(st0, src, AX.X, ALU.max))
                        stat.wait()
                        ts(st1, st0, -sc, None, ALU.mult).then_inc(att_mx, 1)
                    if 1 <= n <= units:
                        m = n - 1
                        dve.wait_ge(att_exp, s.u + m + 1)
                        st3 = s.st[:, 3, m:m + 1]
                        stat.done(dve.reciprocal(st3, s.st[:, 2, m:m + 1]))
                        stat.wait()
                        ts(s.p[:, m % 3, :], s.p[:, m % 3, :], st3, None, ALU.mult).then_inc(att_pn, 1)
                    if n >= 2:
                        m = n - 2
                        h, t = divmod(m, NT)
                        dve.wait_ge(att_pT, s.u + m + 1)
                        if t == 0 and h:
                            dve.wait_ge(att_pv, s.h + h)
                        dve.tensor_copy(s.pt[:, 0:4, t * P:(t + 1) * P],
                                        PS[:, 4, :].rearrange("p (a b) -> p a b", a=4)).then_inc(att_pT_dve, 1)

            attend(gqa)
            meet(dve, "dve")
            for n in range(4, 8):
                dve.wait_ge(proj_done, ctx_done(n))
                dve.tensor_copy(NKT[:, n - 4, N:], PS[:, 2 + n % 2, 0:NCTX]).then_inc(evac[1], 1)
            for t in range(1, NTA, 2):
                dve.wait_ge(proj_done, nav_done(t))
                dve.tensor_copy(NV[:, t, :], PS[:, 2 + t, :]).then_inc(evac[1], 1)
            meet(dve, "dve")
            attend(na)
            meet(dve, "dve")
            dve.sem_inc(ada_tap, 16)
            dve.sem_inc(gated, 2)
            dve.sem_inc(yt_add, 2)
            for i in range(NB):
                dve.wait_ge(hh_hi, KT + i + 1)
                tt(OTLO[:, i, :, :], OT[:, i, :, :], OTHI[:, i, :, :].bitcast(F32), ALU.subtract).then_inc(hh_lo, 1)
            with dve.Fori(0, KT // 2) as q:
                for b in range(8):
                    n, k = 8 * q + b, b % 2
                    dve.wait_ge(wb_hi, n + 1)
                    tt(WBLO[:, k, :, :], WB[:, k, :, :], WBHI[:, k, :, :].bitcast(F32), ALU.subtract).then_inc(wb_lo, 1)
                    dve.wait_ge(ada_in, 16 * n + 16)
                    dve.wait_ge(ada_ps, n + 1)
                    for c in range(KT):
                        w, col = WADA[:, c, :], CSIL[:, c, 0:1]
                        if c == 0:
                            ts(ADACC[:, k, :], w, col, None, ALU.mult).then_inc(ada_tap, 1)
                        else:
                            dve.wait_ge(ada_tap, 16 * n + 16 + c)
                            stt(ADACC[:, k, :], w, col, ADACC[:, k, :], ALU.mult, ALU.add).then_inc(ada_tap, 1)
                    dve.wait_ge(gate_set, n + 1 + 2)
                    dve.wait_ge(br_ps, n + 1 + 2)
                    y = YS[:, b // 4, :]
                    tt(SG[:, k, :], SG[:, k, :], PS[:, 2 + k, :], ALU.mult).then_inc(gated, 1)
                    dve.wait_ge(gated, n + 1 + 2)
                    if b % 4 == 0:
                        dve.wait_ge(y_out[b // 4], 16 * q + 16)
                        dve.tensor_copy(y, SG[:, k, :]).then_inc(yt_add, 1)
                    else:
                        dve.wait_ge(yt_add, n + 2)
                        tt(y, y, SG[:, k, :], ALU.add).then_inc(yt_add, 1)
            meet(dve, "dve")
            def add_projection(c):
                for t in range(NT):
                    g = 4 * c + t
                    dve.wait_ge(out_ps, g + 1)
                    tt(T3[:, g % 2, :], PS[:, 4 * (c % 2) + t, :], G1R[:, c * 512:(c + 1) * 512], ALU.mult).then_inc(out_t, 1)
                    dve.wait_ge(out_t, g + 1)
                    x = XN[:, t, c * 512:(c + 1) * 512]
                    tt(x, x, T3[:, g % 2, :], ALU.add).then_inc(xn_add, 1)

            for n in range(8):
                for h in range(2):
                    dve.wait_ge(w_hi, W_HI + 2 * n + h + 1)
                    tt(wo_low(n)[:, 4 * h:4 * h + 4, :], wo_raw(n)[:, 4 * h:4 * h + 4, :],
                       OHI[:, n % 2, 4 * h:4 * h + 4, :].bitcast(F32), ALU.subtract).then_inc(w_lo, 1)
                for k in (2 * n, 2 * n + 1) if n < 2 else ():
                    dve.wait_ge(hh_hi, ACT_HI + k + 1)
                    tt(YLO[:, 4 * k:4 * k + 4, :], YT[:, 4 * k:4 * k + 4, :], YHI[:, 4 * k:4 * k + 4, :].bitcast(F32),
                       ALU.subtract).then_inc(hh_lo, 1)
                if n == 3:
                    dve.wait_ge(rows_in, 80)
                    stt(SC2[:, :], SC2[:, :], 1.0, NF[:, :], ALU.add, ALU.mult).then_inc(sc2_set, 1)
                if n >= 3 and n % 2:
                    add_projection((n - 3) // 2)
            add_projection(3)
            dve.wait_ge(sc2_set, 1)
            dve.wait_ge(rms_ss, NORM3 + 4 * NT)
            dve.tensor_reduce(SM3[:, 0:4], SM3[:, 32:48].rearrange("p (t c) -> p t c", c=4), AX.X, ALU.add).then_inc(rms_rs, 1)
            dve.wait_ge(rms_sd, NORM3 + 1)
            dve.reciprocal(SM3[:, 8:12], SM3[:, 4:8]).then_inc(rms_rs, 1)
            dve.wait_ge(rms_rs, NORM3 + 2)
            def normed(t):
                stt(H2[:, t, :], XN[:, t, :], SM3[:, 8 + t:9 + t], SC2[:, :], ALU.mult, ALU.mult).then_inc(h_mul, 1)

            def shifted(t):
                dve.wait_ge(h_mul, t + 1)
                tt(H2[:, t, :], H2[:, t, :], SH2[:, :], ALU.add).then_inc(h_set_dve, 1)

            def turned_out(t):
                dve.wait_ge(turned, NTA + t + 1)
                for q in range(2, 4):
                    dve.tensor_copy(H2T[:, 4 * q:4 * q + 4, t * P:(t + 1) * P],
                                    PS[:, q, :].rearrange("p (a b) -> p a b", a=4)).then_inc(turned_dve, 1)

            assert NT == 4
            normed(0)
            normed(1)
            shifted(1)
            normed(2)
            turned_out(0)
            normed(3)
            turned_out(1)
            shifted(3)
            turned_out(2)
            turned_out(3)
            LG = SM3[:, 64:128].rearrange("p (t e) -> p t e", e=E)
            bE = lambda o: SM3[:, o:o + 4].unsqueeze(2).to_broadcast([P, NT, E])
            r = Steps(dve, r_dve)
            dve.wait_ge(r_ps, 2)
            r.done(dve.tensor_reduce(SM3[:, 16:20], PS[:, 5, 0:64].rearrange("p (t e) -> p t e", e=E), AX.X, ALU.max))
            r.wait()
            r.done(tt(LG, PS[:, 5, 0:64].rearrange("p (t e) -> p t e", e=E), bE(16), ALU.subtract))
            dve.wait_ge(r_act, 2)
            dve.tensor_reduce(SM3[:, 20:24], LG, AX.X, ALU.add).then_inc(pos_set, 1)
            dve.wait_ge(pos_set, 1)
            r.done(dve.reciprocal(SM3[:, 24:28], SM3[:, 20:24]))
            r.wait()
            r.done(tt(AFF[:, :, :], LG, bE(24), ALU.mult))
            k = Steps(dve, topk)
            dve.wait_ge(r_ps, 3)
            k.done(dve.tensor_copy(AT[:, 0, :], PS[0:E, 6, :]))
            k.done(dve.memset(AT[:, 2, :], 1.0))
            for i in range(CAP // 8):
                k.wait()
                k.done(dve.max(M8[:, i, :], AT[:, i % 2, :]))
                k.wait()
                k.done(dve.match_replace(AT[:, (i + 1) % 2, :], M8[:, i, :], AT[:, i % 2, :], -1.0))
            k.wait()
            k.done(ts(AT[:, 1, :], AT[:, (CAP // 8) % 2, :], 0.0, None, ALU.is_lt))
            k.wait()
            k.done(dve.tensor_tensor_scan(AT[:, 3, :], AT[:, 2, :], AT[:, 1, :], 0.0, ALU.mult, ALU.add))
            k.wait()
            dve.tensor_tensor(AT[:, 3, :], AT[:, 3, :], AT[:, 1, :], ALU.mult).then_inc(pos_set, 1)
            dve.wait_ge(pos_set, 2)
            k.done(ts(AT[:, 4, :], AT[:, 3, :], -1.0, None, ALU.add))
            assert k.n == 21
            dve.wait_ge(r_ps, 4)
            dve.tensor_copy(POS[:, :, :], PS[:, 7, 0:64].rearrange("p (t e) -> p t e", e=E)).then_inc(pos_set, 1)
            meet(dve, "dve")

            p4 = lambda x: x[:, :, :].rearrange("p t (e s) -> p t e s", e=2)

            def choice(m):
                iota = CST[:, K_IOTA:K_IOTA + 64].unsqueeze(1).unsqueeze(1).to_broadcast([P, NT, 2, 64])
                tt(p4(PSEL), POS[:, :, bass.ds(2 * m, 2)].unsqueeze(3).to_broadcast([P, NT, 2, 64]), iota,
                   ALU.is_equal).then_inc(psel_set, 1)

            def weighted_choice(m):
                dve.wait_ge(psel_set, m + 1)
                tt(p4(PG), p4(PSEL), AFF[:, :, bass.ds(2 * m, 2)].unsqueeze(3).to_broadcast([P, NT, 2, 64]),
                   ALU.mult).then_inc(pg_set, 1)

            def rows(m):
                for c in range(2, 4):
                    dve.wait_ge(xs_ps, 4 * m + c + 1)
                    dve.tensor_copy(XS[:, c * 512:(c + 1) * 512], PS[:, 4 + c, :]).then_inc(xs_dve, 1)
                for q in range(2, 4):
                    dve.wait_ge(xst_ps, 4 * m + q + 1)
                    dve.tensor_copy(XST[:, 4 * q:4 * q + 4, :], PS[:, q, :].rearrange("p (a b) -> p a b", a=4)).then_inc(xst_dve, 1)

            def expert_pair(m, last):
                if not last:
                    choice(m + 1)
                dve.wait_ge(moe_read, NL * m + RD + 16)
                dve.wait_ge(silu_set, m + 1)
                h = HID[:, :].rearrange("p (a b) -> p a b", a=2)
                tt(h, h, PS[:, 2:4, :], ALU.mult).then_inc(hid_set, 1)
                if not last:
                    rows(m + 1)
                dve.wait_ge(hidT_ps, 2 * m + 2)
                dve.tensor_copy(HIDT[:, 4:8, :], PS[:, 5, :].rearrange("p (a b) -> p a b", a=4)).then_inc(hidT_dve, 1)
                dve.wait_ge(pgt_ps, m + 1)
                dve.tensor_copy(PGT[:, :], PS[:, 6, :]).then_inc(pgt_set, 1)
                if not last:
                    weighted_choice(m + 1)
                dve.wait_ge(moe_read, NL * m + RD + NL)
                for c in range(4):
                    tt(XS[:, c * 512:(c + 1) * 512], PS[:, c, :], G2R[:, c * 512:(c + 1) * 512], ALU.mult).then_inc(ye_set, 1)
                for g in range(16):
                    t, c = divmod(g, 4)
                    dve.wait_ge(sc_ps, 16 * m + g + 1)
                    x = XN[:, t, c * 512:(c + 1) * 512]
                    tt(x, x, PS[:, 4 + g % 4, :], ALU.add).then_inc(acc_set, 1)

            dve.sem_inc(ye_set, 4)
            dve.sem_inc(acc_set, 16)
            choice(0)
            weighted_choice(0)
            dve.wait_ge(small_in, SMALL_G2)
            rows(0)
            with dve.Fori(0, E // 2 - 1) as m:
                expert_pair(m, False)
            expert_pair(E // 2 - 1, True)
            dve.wait_ge(cst_in, 80)
            for t in range(NT):
                dve.wait_ge(rms_sd, SD5 + t + 1)
                dve.reciprocal(SM5[:, 8 + t:9 + t], SM5[:, 4 + t:5 + t]).then_inc(rms_rs, 1)
                dve.wait_ge(rms_rs, RS5 + t + 1)
                stt(XN[:, t, :], XN[:, t, :], SM5[:, 8 + t:9 + t], FN[:, :], ALU.mult, ALU.mult).then_inc(o_set, 1)

        @block.gpsimd
        def _(pool):
            tt = pool.tensor_tensor
            pool.memset(CSILP[:, :, :], 0.0).then_inc(pads_zero, 1)
            for t in range(NTA):
                if t >= 2:
                    pool.wait_ge(turned, t - 1)
                src = a["x"][t * P:(t + 1) * P, :] if t < NT else a["ctx"][(t - NT) * P:(t - NT + 1) * P, :]
                pool.dma_start(XT[:, t % 2, :], src).then_inc(x_in[t % 2], 16)
            pool.memset(WDT[:, :, :], 0.0).then_inc(dtw_zero, 1)
            pool.memset(XB[:, :, :], 0.0).then_inc(pads_zero, 1)
            pool.wait_ge(dtw_zero, 1)
            pool.dma_start(WDT[:, :, 0:16], w_in[:, :, C_DT:C_DT + 16]).then_inc(small_in, 16)
            pool.wait_ge(wx_set, 1)
            pool.wait_ge(tok_x, NTA)
            v3 = lambda ap: ap.rearrange("p (h c) -> p h c", c=SHD)
            n = 0
            for i, ft in enumerate(zip((4, 5, 0, 1, 2), (5, 4, 3, 2, 1))):
                for d, t in enumerate(ft):
                    if i:
                        pool.wait_ge(st_ps, n - 1)
                    tt(v3(TMP[:, d, :]), v3(XTOK[:, t, :]), wx[:, t, 8 * d:8 * d + 8].unsqueeze(2).to_broadcast([P, SH, SHD]),
                       ALU.mult).then_inc(xw_set, 1)
                    n += 1
            for t in range(NT):
                if t:
                    pool.wait_ge(seg_ps, t)
                for d, tri in enumerate((triu, tril)):
                    tt(DATRI[:, 8 * d:8 * d + 8, :], tri.unsqueeze(1).to_broadcast([P, SH, P]),
                       da[:, t, 8 * d:8 * d + 8].unsqueeze(2).to_broadcast([P, SH, P]), ALU.mult).then_inc(datri_set, 1)
                pool.wait_ge(seg_exp, 2 * t + 1)
                tt(LSEG[:, 0:8, :], LSEG[:, 0:8, :], dts[:, t, 0:8].unsqueeze(2).to_broadcast([P, SH, P]),
                   ALU.mult).then_inc(lf_set, 1)
            meet(pool, "pool")
            pool.wait_ge(gkv_in, 16)
            v = Steps(pool, g_pool)
            kraw = GKV[:, :, 0:256]
            tt(SQK[:, :, :], kraw, kraw, ALU.mult).then_inc(g_sqk, 1)
            pool.wait_ge(g_rs, 1)
            k3 = kraw.rearrange("p t (h c) -> p t h c", c=HD)
            rk = SMG[:, 48:60].rearrange("p (t h) -> p t h", h=2).unsqueeze(3).to_broadcast([P, NTA, 2, HD])
            v.done(tt(k3, k3, rk, ALU.mult))
            v.wait()
            for h in range(2):
                kh = GKV[:, :, h * HD:(h + 1) * HD]
                v.done(tt(kh, kh, ROW[:, R_KG:R_KG + HD].unsqueeze(1).to_broadcast([P, NTA, HD]), ALU.mult))
            v.wait()
            pool.wait_ge(gq_in, 32)
            rotate(v, tt, GKV, RTK, ROPE, 2)
            meet(pool, "pool")

            def high(w, raw, k, count):
                pool.wait_ge(raw_in[k], 16 * count)
                tt(w, raw, ones.unsqueeze(1).to_broadcast([P, KT, P]), ALU.mult).then_inc(w_hi, 1)

            def split(n):
                k = n % 2
                if n >= 2:
                    pool.wait_ge(proj_done, blk_done(n - 2))
                high(WHI[:, k, :, :], NRAW[k][:, :, :], k, n // 2 + 1)
                pool.wait_ge(w_hi, n + 1)
                tt(WLO[:, k, :, :], NRAW[k][:, :, :], WHI[:, k, :, :].bitcast(F32), ALU.subtract).then_inc(w_lo, 1)

            for c in range(4):
                pool.wait_ge(hh_hi, 4 * c + 4)
                tt(HLO[:, 4 * c:4 * c + 4, :], HT[:, 4 * c:4 * c + 4, :], HHI[:, 4 * c:4 * c + 4, :].bitcast(F32),
                   ALU.subtract).then_inc(hh_lo, 1)
            split(0)
            split(1)
            meet(pool, "pool")
            def load_bias(h):
                for rr in range(2):
                    pool.dma_start(NBIAS[rr * GRID_W:(rr + 1) * GRID_W, h % 2, :, :],
                                   a["rpb_win"][:, h, 1 - rr:16 - rr, :]).then_inc(bias_in, 16)

            load_bias(0)
            load_bias(1)
            for n in range(2, 6):
                split(n)
            pool.wait_ge(bias_in, 64)
            for h in range(HEADS):
                if h >= 2:
                    pool.wait_ge(att_raw, NT * (h - 1))
                    load_bias(h)
                    pool.wait_ge(bias_in, 32 * (h + 1))
                tt(NBIAS[:, h % 2, :, :], NBIAS[:, h % 2, :, :],
                   CST[:, K_NAM:K_NAM + GRID_W].unsqueeze(1).to_broadcast([P, 15, GRID_W]), ALU.add).then_inc(bias_set, 1)
                if h == 1:
                    for n in range(6, NBLK):
                        split(n)
                    meet(pool, "pool")
            for k in range(2):
                high(WHI[:, k, :, :], RAW[:, k, :, :], k, NBLK // 2 + 1)
            meet(pool, "pool")
            def low(k, count):
                pool.wait_ge(w_hi, count)
                tt(WLO[:, k, :, :], RAW[:, k, :, :], WHI[:, k, :, :].bitcast(F32), ALU.subtract).then_inc(gw_lo, 1)

            for k in range(2):
                low(k, NBLK + 1 + k)
            with pool.Fori(1, 32) as q:
                for k in range(2):
                    n = 2 * q + k
                    pool.wait_ge(br_ps, n + 1)
                    high(WHI[:, k, :, :], RAW[:, k, :, :], k, q + 1 + NBLK // 2)
                    low(k, n + 1 + NBLK)
            meet(pool, "pool")
            pool.memset(WR[:, :, :], 0.0).then_inc(wr_zero, 1)
            pool.wait_ge(wr_zero, 1)
            pool.dma_start(WR[:, :, 0:E], a["w_router"].rearrange("(p k) e -> p k e", k=KT)).then_inc(small_in, 16)
            for t in range(0, NT, 2):
                pool.wait_ge(h_mul, t + 1)
                tt(H2[:, t, :], H2[:, t, :], SH2[:, :], ALU.add).then_inc(h_set, 1)
            pool.wait_ge(r_ps, 2)
            pool.dma_start(G2R[:, :], ada_dram[3 * D:4 * D].partition_broadcast(P)).then_inc(small_in, 16)
            meet(pool, "pool")


def rotate(steps, tt, x, tmp, rope, heads):
    w = heads * 64
    for t in range(NT):
        v = x[:, t, 0:heads * HD].rearrange("p (m r d) -> p m r d", r=2, d=32)
        re, im = v[:, :, 0, :], v[:, :, 1, :]
        re = re.rearrange("p (h a) d -> p h a d", a=2)
        im = im.rearrange("p (h a) d -> p h a d", a=2)
        tab = lambda i: rope[:, t, i, :].rearrange("p (a d) -> p a d", a=2).unsqueeze(1).to_broadcast([P, heads, 2, 32])
        b = lambda i: tmp[:, i, 0:w].rearrange("p (h a d) -> p h a d", h=heads, a=2)
        if t:
            steps.wait()
        steps.done(tt(b(0), re, tab(0), ALU.mult))
        steps.done(tt(b(1), im, tab(1), ALU.mult))
        steps.done(tt(b(2), re, tab(1), ALU.mult))
        steps.done(tt(b(3), im, tab(0), ALU.mult))
        steps.wait()
        steps.done(tt(re, b(0), b(1), ALU.subtract))
        steps.done(tt(im, b(2), b(3), ALU.add))


def constants():
    i = np.arange(P)
    cst = np.zeros((P, K_W), np.float32)
    cst[:, K_ID:K_ID + P] = np.eye(P)
    cst[:, K_ONE:K_ONE + P] = 1
    up = i[:, None] <= i[None, :]
    cst[:, K_TU:K_TU + P] = up
    cst[:, K_TL:K_TL + P] = up.T
    cst[:, K_MF:K_MF + P] = np.where(up, 0, NEG)
    cst[:, K_MB:K_MB + P] = np.where(up.T, 0, NEG)
    c, kc = (i % GRID_W)[:, None], np.arange(GRID_W)[None, :]
    start = np.clip(c - NA_C // 2, 0, GRID_W - NA_C)
    cst[:, K_NAM:K_NAM + GRID_W] = np.where((kc >= start) & (kc < start + NA_C), 0, NEG)
    cst[:, K_IOTA:K_IOTA + 64] = np.arange(64)
    cst[:, K_SEL:K_SEL + 32] = (i % 32)[:, None] == np.arange(32)[None, :]
    cst[:, K_EPS] = EPS
    k = np.outer(np.arange(P), np.arange(P)) * (2 * np.pi / P)
    dft_c = np.concatenate([np.cos(k), np.sin(k)], 1).astype(np.float32)
    k = (np.outer(np.arange(N), np.arange(N)) % N) * (2 * np.pi / N)
    cs = np.stack([np.cos(k), -np.sin(k)], 1) / np.sqrt(N * P)
    dft_n = cs.reshape(NT, P, 2 * N).transpose(1, 0, 2).reshape(P, -1).astype(np.float32)
    t = np.arange(N)
    pos = np.stack([t // GRID_W, t % GRID_W], -1).astype(np.float32)
    inv = (np.float32(10000.0) ** (-np.arange(32, dtype=np.float32) / 32)).astype(np.float32)
    ang = (pos[:, :, None] * inv).reshape(N, 64)
    rope = np.stack([np.cos(ang), np.sin(ang)], 1).astype(np.float32)
    rope = rope.reshape(NT, P, 128).transpose(1, 0, 2).reshape(P, -1)
    return dict(cst=cst, dft_c=dft_c, dft_n=np.ascontiguousarray(dft_n), rope=np.ascontiguousarray(rope))


def layout(i):
    g = {k: np.asarray(v) for k, v in i.items()}
    r = lambda v: v.reshape(P, KT)
    c2 = np.stack([r(g["c"][0]), r(g["c_ctx"])], -1).reshape(P, 32)
    cw = g["ssd_conv_w"][0].T.reshape(8, P, 5).transpose(1, 0, 2).reshape(P, 40)
    cb = g["ssd_conv_b"][0].reshape(8, P).T
    bada = g["b_ada"][0]
    colp = np.concatenate([r(g["norm_mix"][0]), cw, cb, c2, r(bada[:D]), r(bada[D:2 * D])], 1)
    rowp = np.concatenate([g["ssd_a_log"][0].ravel(), g["ssd_dt_bias"][0].ravel(), g["ssd_d"][0], g["ssd_norm"][0],
                           g["gqa_q_norm"][0], g["gqa_k_norm"][0]])
    rpb = np.zeros((HEADS, 17, 127), np.float32)
    rpb[:, 1:16, 48:79] = g["na_rpb"][0]
    rpb_win = np.stack([rpb[:, :, 63 - c:127 - c] for c in range(GRID_W)])
    return dict(
        x=g["x"][0], ctx=g["ctx"][0], w_ada=g["w_ada"][0], w_in=g["w_in"][0], colp=colp, rowp=rowp, rpb_win=rpb_win,
        b_ada=bada, w_branch=g["w_branch"][0], w_out=g["w_out"][0], w_router=g["w_router"][0],
        w_gate=g["moe_w_gate"][0], w_up=g["moe_w_up"][0], w_down=g["moe_w_down"][0],
        norm_ffn=g["norm_ffn"][0], final_norm=g["final_norm"])


def kernel(**inputs):
    import concourse.bacc as bacc
    from concourse.bass_utils import run_bass_kernel_spmd

    nc = bacc.Bacc("TRN2", target_bir_lowering=False, num_devices=1)
    arrays = {f"in_{k}": np.ascontiguousarray(v) for k, v in {**layout(inputs), **constants()}.items()}
    aps = {k[3:]: nc.dram_tensor(k, v.shape, F32, kind="ExternalInput").ap() for k, v in arrays.items()}
    out = nc.dram_tensor("out", [N, D], F32, kind="ExternalOutput").ap()
    build_layer(nc, aps, out)
    r = run_bass_kernel_spmd(nc, [arrays], core_ids=[0])
    return r.results[0]["out"].reshape(1, N, D)
```
